# Optimizing a Trainium2 kernel written in Bass

```python
import jax, jax.numpy as jnp
from jax import lax
import numpy as np

D_MODEL = 1024
BATCH = 1
SEQ = 256
DEPTH = 1
DEC_BATCH = 8
DEC_SEQ = 1
PAST_LEN = 2048
PAGE_SIZE = 128

MIX_WIDTH = D_MODEL
LRU_WIDTH = MIX_WIDTH // 2
CF_WIDTH = MIX_WIDTH - LRU_WIDTH
LRU_HEADS = 8
LRU_HEAD_DIM = LRU_WIDTH // LRU_HEADS
LRU_CONV = 4
LRU_C = 8.0
CF_CONV = 31
IN_WIDTH = 2 * LRU_WIDTH + 2 * CF_WIDTH
N_MEM = 256
XA_HEADS = 4
XA_HEAD_DIM = D_MODEL // XA_HEADS
N_EXPERTS = 32
TOP_K = 4
D_EXPERT = D_MODEL
SWIGLU_LIMIT = 7.0
SWIGLU_ALPHA = 1.702
MOE_BLOCK = 128
EPS = 1e-6

kernel_name = "hymba_rglru_conformer_moe_xattn_step"

def rms_norm(x, g):
    xf = x.astype(jnp.float32)
    y = xf * lax.rsqrt(jnp.mean(xf * xf, axis=-1, keepdims=True) + EPS)
    return (y * g.astype(jnp.float32)).astype(x.dtype)

def layer_norm(x, g, b):
    xf = x.astype(jnp.float32)
    mu = jnp.mean(xf, axis=-1, keepdims=True)
    xc = xf - mu
    y = xc * lax.rsqrt(jnp.mean(xc * xc, axis=-1, keepdims=True) + EPS)
    return (y * g.astype(jnp.float32) + b.astype(jnp.float32)).astype(x.dtype)

def causal_dwconv(buf, x, w, b):
    width = w.shape[0]
    xp = jnp.concatenate([buf.astype(x.dtype), x], axis=1)
    y = lax.conv_general_dilated(
        xp, w[:, None, :].astype(x.dtype), window_strides=(1,), padding='VALID',
        dimension_numbers=('NWC', 'WIO', 'NWC'), feature_group_count=x.shape[-1])
    return y + b.astype(x.dtype), xp[:, xp.shape[1] - (width - 1):, :]

def rg_lru(x, h0, w_a, b_a, w_x, b_x, lam):
    B, T, _ = x.shape
    xf = x.astype(jnp.float32)
    xh = xf.reshape(B, T, LRU_HEADS, LRU_HEAD_DIM)
    r = jax.nn.sigmoid(jnp.einsum('bthi,hij->bthj', xh, w_a.astype(jnp.float32)).reshape(B, T, LRU_WIDTH) + b_a.astype(jnp.float32))
    i = jax.nn.sigmoid(jnp.einsum('bthi,hij->bthj', xh, w_x.astype(jnp.float32)).reshape(B, T, LRU_WIDTH) + b_x.astype(jnp.float32))
    log_a = -LRU_C * r * jax.nn.softplus(-lam.astype(jnp.float32))
    a = jnp.exp(log_a)
    u = jnp.sqrt(-jnp.expm1(2.0 * log_a)) * (i * xf)

    def step(h, au):
        a_t, u_t = au
        h = a_t * h + u_t
        return h, h

    h_last, hs = lax.scan(step, h0.astype(jnp.float32), (jnp.swapaxes(a, 0, 1), jnp.swapaxes(u, 0, 1)))
    return jnp.swapaxes(hs, 0, 1).astype(x.dtype), h_last

def head_group_mixer(xn, lru_h, lru_buf, cf_buf, mix_w):
    (w_in, w_lru_conv, b_lru_conv, w_lru_a, b_lru_a, w_lru_x, b_lru_x, lru_lambda,
     w_cf_conv, b_cf_conv, g_cf_ln, b_cf_ln, w_out) = mix_w
    z = xn @ w_in
    zx, zg, za, zb = jnp.split(z, [LRU_WIDTH, 2 * LRU_WIDTH, 2 * LRU_WIDTH + CF_WIDTH], axis=-1)
    xc, lru_buf_new = causal_dwconv(lru_buf, zx, w_lru_conv, b_lru_conv)
    hs, lru_h_new = rg_lru(xc, lru_h, w_lru_a, b_lru_a, w_lru_x, b_lru_x, lru_lambda)
    y_lru = hs * jax.nn.gelu(zg)
    glu = za * jax.nn.sigmoid(zb)
    gc, cf_buf_new = causal_dwconv(cf_buf, glu, w_cf_conv, b_cf_conv)
    y_cf = jax.nn.silu(layer_norm(gc, g_cf_ln, b_cf_ln))
    y = jnp.concatenate([y_lru, y_cf], axis=-1) @ w_out
    return y, lru_h_new, lru_buf_new, cf_buf_new

def memory_kv(mem, g_mem, w_k, w_v):
    B = mem.shape[0]
    mn = rms_norm(mem, g_mem)
    k = (mn @ w_k).reshape(B, N_MEM, XA_HEADS, XA_HEAD_DIM)
    v = (mn @ w_v).reshape(B, N_MEM, XA_HEADS, XA_HEAD_DIM)
    return k, v

def cross_attention(xn, k, v, w_q, w_o):
    B, T, _ = xn.shape
    q = (xn @ w_q).reshape(B, T, XA_HEADS, XA_HEAD_DIM)
    s = jnp.einsum('bthd,bmhd->bhtm', q, k.astype(q.dtype)).astype(jnp.float32) * (XA_HEAD_DIM ** -0.5)
    p = jax.nn.softmax(s, axis=-1).astype(v.dtype)
    o = jnp.einsum('bhtm,bmhd->bthd', p, v).reshape(B, T, D_MODEL).astype(xn.dtype)
    return o @ w_o

def routed_experts(xn, moe_w):
    w_router, b_router, w_e1, b_e1, w_e2, b_e2 = moe_w
    B, T, D = xn.shape
    N = B * T
    xf = xn.reshape(N, D)
    logits = (xf @ w_router).astype(jnp.float32) + b_router.astype(jnp.float32)
    top_v, top_e = lax.top_k(logits, TOP_K)
    gates = jax.nn.softmax(top_v, axis=-1)
    A = N * TOP_K
    e_flat = top_e.reshape(A)
    order = jnp.argsort(e_flat)
    e_sorted = e_flat[order]
    counts = jnp.bincount(e_flat, length=N_EXPERTS)
    padded = (counts + MOE_BLOCK - 1) // MOE_BLOCK * MOE_BLOCK
    start = jnp.cumsum(counts) - counts
    pstart = jnp.cumsum(padded) - padded
    dest = pstart[e_sorted] + (jnp.arange(A) - start[e_sorted])
    n_blocks = -(-A // MOE_BLOCK) + N_EXPERTS
    P = n_blocks * MOE_BLOCK
    tok = jnp.full((P,), N, jnp.int32).at[dest].set((order // TOP_K).astype(jnp.int32))
    gate_rows = jnp.zeros((P,), jnp.float32).at[dest].set(gates.reshape(A)[order])
    blk_e = jnp.clip(jnp.searchsorted(jnp.cumsum(padded), jnp.arange(n_blocks) * MOE_BLOCK, side='right'),
                     0, N_EXPERTS - 1).astype(jnp.int32)
    x_pad = jnp.concatenate([xf, jnp.zeros((1, D), xf.dtype)], axis=0)

    def run_block(args):
        e, idx = args
        xb = x_pad[idx]
        gu = xb @ w_e1[e] + b_e1[e]
        g, u = gu[:, :D_EXPERT], gu[:, D_EXPERT:]
        g = jnp.minimum(g, SWIGLU_LIMIT)
        u = jnp.clip(u, -SWIGLU_LIMIT, SWIGLU_LIMIT)
        h = (u + 1.0) * (g * jax.nn.sigmoid(SWIGLU_ALPHA * g))
        return h @ w_e2[e] + b_e2[e]

    rows = lax.map(run_block, (blk_e, tok.reshape(n_blocks, MOE_BLOCK)))
    rows = rows.reshape(P, D).astype(jnp.float32) * gate_rows[:, None]
    out = jax.ops.segment_sum(rows, tok, num_segments=N + 1)[:N]
    return out.astype(xn.dtype).reshape(B, T, D)

def decoder_layer(x, lru_h, lru_buf, cf_buf, mem_k, mem_v, g_mix, g_xa, g_moe, mix_w, xa_w, moe_w):
    y, lru_h_new, lru_buf_new, cf_buf_new = head_group_mixer(rms_norm(x, g_mix), lru_h, lru_buf, cf_buf, mix_w)
    x = x + y
    x = x + cross_attention(rms_norm(x, g_xa), mem_k, mem_v, xa_w[0], xa_w[1])
    x = x + routed_experts(rms_norm(x, g_moe), moe_w)
    return x, lru_h_new, lru_buf_new, cf_buf_new

def setup_inputs(seed: int = 0) -> dict:
    key = jax.random.key(seed)
    keys = jax.random.split(key, 40)
    counter = [0]
    f32 = jnp.float32

    def nxt():
        k = keys[counter[0]]
        counter[0] += 1
        return k

    def nrm(shape, scale):
        return jax.random.normal(nxt(), shape, f32) * scale

    def gain(shape):
        return 1.0 + nrm(shape, 0.02)

    L = DEPTH
    x_prompt = nrm((BATCH, SEQ, D_MODEL), 1.0)
    x_sample = nrm((DEC_BATCH, DEC_SEQ, D_MODEL), 1.0)
    state_lru_h = nrm((L, DEC_BATCH, LRU_WIDTH), 0.5)
    cache_lru_conv = nrm((L, DEC_BATCH, LRU_CONV - 1, LRU_WIDTH), 1.0)
    cache_cf_conv = nrm((L, DEC_BATCH, CF_CONV - 1, CF_WIDTH), 0.5)
    cache_mem_k = nrm((L, DEC_BATCH, N_MEM, XA_HEADS, XA_HEAD_DIM), 1.0)
    cache_mem_v = nrm((L, DEC_BATCH, N_MEM, XA_HEADS, XA_HEAD_DIM), 1.0)
    mem_prompt = nrm((BATCH, N_MEM, D_MODEL), 1.0)

    g_mix = gain((L, D_MODEL))
    w_in = nrm((L, D_MODEL, IN_WIDTH), D_MODEL ** -0.5)
    w_lru_conv = nrm((L, LRU_CONV, LRU_WIDTH), LRU_CONV ** -0.5)
    b_lru_conv = nrm((L, LRU_WIDTH), 0.02)
    w_lru_a = nrm((L, LRU_HEADS, LRU_HEAD_DIM, LRU_HEAD_DIM), LRU_HEAD_DIM ** -0.5)
    b_lru_a = nrm((L, LRU_WIDTH), 0.02)
    w_lru_x = nrm((L, LRU_HEADS, LRU_HEAD_DIM, LRU_HEAD_DIM), LRU_HEAD_DIM ** -0.5)
    b_lru_x = nrm((L, LRU_WIDTH), 0.02)
    a0 = jax.random.uniform(nxt(), (L, LRU_WIDTH), f32, 0.9, 0.999)
    s0 = a0 ** (1.0 / LRU_C)
    lru_lambda = jnp.log(s0) - jnp.log1p(-s0)
    w_cf_conv = nrm((L, CF_CONV, CF_WIDTH), CF_CONV ** -0.5)
    b_cf_conv = nrm((L, CF_WIDTH), 0.02)
    g_cf_ln = gain((L, CF_WIDTH))
    b_cf_ln = nrm((L, CF_WIDTH), 0.02)
    w_out = nrm((L, MIX_WIDTH, D_MODEL), MIX_WIDTH ** -0.5)

    g_xa = gain((L, D_MODEL))
    g_mem = gain((L, D_MODEL))
    w_q = nrm((L, D_MODEL, D_MODEL), D_MODEL ** -0.5)
    w_k = nrm((L, D_MODEL, D_MODEL), D_MODEL ** -0.5)
    w_v = nrm((L, D_MODEL, D_MODEL), D_MODEL ** -0.5)
    w_o = nrm((L, D_MODEL, D_MODEL), D_MODEL ** -0.5)

    g_moe = gain((L, D_MODEL))
    w_router = nrm((L, D_MODEL, N_EXPERTS), D_MODEL ** -0.5)
    b_router = nrm((L, N_EXPERTS), 0.01)
    w_e1 = nrm((L, N_EXPERTS, D_MODEL, 2 * D_EXPERT), D_MODEL ** -0.5)
    b_e1 = nrm((L, N_EXPERTS, 2 * D_EXPERT), 0.01)
    w_e2 = nrm((L, N_EXPERTS, D_EXPERT, D_MODEL), D_EXPERT ** -0.5)
    b_e2 = nrm((L, N_EXPERTS, D_MODEL), 0.01)
    g_final = gain((D_MODEL,))

    return {
        "x_prompt": x_prompt, "x_sample": x_sample,
        "state_lru_h": state_lru_h, "cache_lru_conv": cache_lru_conv, "cache_cf_conv": cache_cf_conv,
        "cache_mem_k": cache_mem_k, "cache_mem_v": cache_mem_v,
        "mem_prompt": mem_prompt,
        "g_mix": g_mix, "w_in": w_in, "w_lru_conv": w_lru_conv, "b_lru_conv": b_lru_conv,
        "w_lru_a": w_lru_a, "b_lru_a": b_lru_a, "w_lru_x": w_lru_x, "b_lru_x": b_lru_x,
        "lru_lambda": lru_lambda, "w_cf_conv": w_cf_conv, "b_cf_conv": b_cf_conv,
        "g_cf_ln": g_cf_ln, "b_cf_ln": b_cf_ln, "w_out": w_out,
        "g_xa": g_xa, "g_mem": g_mem, "w_q": w_q, "w_k": w_k, "w_v": w_v, "w_o": w_o,
        "g_moe": g_moe, "w_router": w_router, "b_router": b_router,
        "w_e1": w_e1, "b_e1": b_e1, "w_e2": w_e2, "b_e2": b_e2,
        "g_final": g_final,
    }

def reference(x_prompt, x_sample, state_lru_h, cache_lru_conv, cache_cf_conv, cache_mem_k, cache_mem_v,
              mem_prompt, g_mix, w_in, w_lru_conv, b_lru_conv, w_lru_a, b_lru_a, w_lru_x, b_lru_x,
              lru_lambda, w_cf_conv, b_cf_conv, g_cf_ln, b_cf_ln, w_out, g_xa, g_mem, w_q, w_k, w_v, w_o,
              g_moe, w_router, b_router, w_e1, b_e1, w_e2, b_e2, g_final):
    xp, xs = x_prompt, x_sample
    hp_l, lcp_l, ccp_l, mkp_l, mvp_l = [], [], [], [], []
    hs_l, lcs_l, ccs_l = [], [], []
    for l in range(DEPTH):
        mix_w = (w_in[l], w_lru_conv[l], b_lru_conv[l], w_lru_a[l], b_lru_a[l], w_lru_x[l], b_lru_x[l],
                 lru_lambda[l], w_cf_conv[l], b_cf_conv[l], g_cf_ln[l], b_cf_ln[l], w_out[l])
        xa_w = (w_q[l], w_o[l])
        moe_w = (w_router[l], b_router[l], w_e1[l], b_e1[l], w_e2[l], b_e2[l])
        mk, mv = memory_kv(mem_prompt, g_mem[l], w_k[l], w_v[l])
        h0 = jnp.zeros((xp.shape[0], LRU_WIDTH), jnp.float32)
        lb0 = jnp.zeros((xp.shape[0], LRU_CONV - 1, LRU_WIDTH), xp.dtype)
        cb0 = jnp.zeros((xp.shape[0], CF_CONV - 1, CF_WIDTH), xp.dtype)
        xp, hp, lcp, ccp = decoder_layer(xp, h0, lb0, cb0, mk, mv, g_mix[l], g_xa[l], g_moe[l], mix_w, xa_w, moe_w)
        xs, hs, lcs, ccs = decoder_layer(xs, state_lru_h[l], cache_lru_conv[l], cache_cf_conv[l],
                                         cache_mem_k[l], cache_mem_v[l], g_mix[l], g_xa[l], g_moe[l],
                                         mix_w, xa_w, moe_w)
        hp_l.append(hp); lcp_l.append(lcp); ccp_l.append(ccp); mkp_l.append(mk); mvp_l.append(mv)
        hs_l.append(hs); lcs_l.append(lcs); ccs_l.append(ccs)
    y_prompt = rms_norm(xp, g_final)
    y_sample = rms_norm(xs, g_final)
    return (y_prompt, y_sample, jnp.stack(hp_l), jnp.stack(lcp_l), jnp.stack(ccp_l), jnp.stack(mkp_l),
            jnp.stack(mvp_l), jnp.stack(hs_l), jnp.stack(lcs_l), jnp.stack(ccs_l))


_drawn_inputs = setup_inputs


def setup_inputs(seed=0):
    import zlib

    import numpy as np

    out = dict(_drawn_inputs(seed))
    spreads = {}
    factors = {'b_lru_a': 6.907,
     'b_lru_x': 5.722,
     'g_xa': 6.988,
     'g_mem': 2.897,
     'b_e1': 8.0,
     'b_e2': 34.664,
     'g_final': 25.206,
     'g_moe': 2.826,
     'b_router': 6.543}
    for name, (base, spread) in spreads.items():
        noise = np.random.default_rng([zlib.crc32(name.encode()), seed]).standard_normal(out[name].shape)
        drawn = base * np.exp(spread * noise) if base else spread * noise
        out[name] = __import__('jax').numpy.asarray(drawn.astype(out[name].dtype))
    for name, factor in factors.items():
        out[name] = (out[name] * factor).astype(out[name].dtype)
    return out
```

```python
import numpy as np
from contextlib import ExitStack

import concourse.bass as bass
import concourse.mybir as mybir

F32 = mybir.dt.float32
I32 = mybir.dt.int32
U32 = mybir.dt.uint32
ALU = mybir.AluOpType
ACT = mybir.ActivationFunctionType
AX = mybir.AxisListType

P = 128
D = 1024
KD = D // P
SEQ = 256
NB = 8
TOK = SEQ + NB
TT = [(0, P), (P, P), (2 * P, NB)]
LRU = 512
LC = LRU // P
HEAD = 64
CW = 31
LW = 4
NMEM = 256
H = 4
HD = D // H
NE = 32
CAP = 64
PASSES = -(-TOK // CAP)
NCOL = PASSES * NE
EPS = 1e-6
LIMIT = 7.0
ALPHA = 1.702
GELU_C = 0.7978845608028654
GELU_A = 0.044715
BIG = 4096.0

SLOT = 2048
RING = 12
W_SLOTS = 8
HEADROOM = 4

FRONT = [("in", 8), ("k", 4), ("v", 4), ("out", 4), ("q", 4), ("kc", 8), ("vc", 8), ("o", 4)]
START = {}
_n = HEADROOM
for _kind, _count in FRONT:
    START[_kind] = _n
    _n += _count
MOE0 = _n
assert MOE0 % RING == 0
KC_SLOTS = 8

IN_ORDER = [4, 5, 6, 7, 0, 1, 2, 3]

C_WCF = 0
C_B = CW * LC
C_WL, C_BLC, C_BA, C_BX, C_LAM, C_BCF, C_GLN, C_BLN = (C_B + 4 * i for i in (0, 4, 5, 6, 7, 8, 9, 10))
C_GMIX, C_GXA, C_GMEM, C_GMOE = (C_B + 44 + 8 * i for i in range(4))
B_ROWS = 76
C_H0 = C_B + B_ROWS
NPAR = C_H0 + LC * NB


def freed_after(n):
    if n < START["kc"]:
        return n + 1
    return n + 1 - KC_SLOTS


def fills_before(n):
    return n // RING + 1 - (1 if n % RING < HEADROOM else 0)


def build(nc, a, outs):
    ctx = ExitStack()
    with ctx:
        def sb(name, shape, dt=F32):
            return ctx.enter_context(nc.sbuf_tensor(name, shape, dt))

        def sem(name):
            return ctx.enter_context(nc.semaphore(name))

        ring = sb("ring", [P, RING, SLOT])
        MIXW = 4 * (30 + TOK) + 4 * (3 + TOK) + 9 * LC * TOK
        mix = sb("mix", [P, MIXW])
        xT = sb("xT", [P, KD, TOK])
        xn = sb("xn", [P, KD, TOK])
        sq = sb("sq", [P, KD, TOK])
        tok = sb("tok", [P, 3, D])
        vtok = sb("vtok", [P, 2, D])
        kT = sb("kT", [P, KD, NMEM])
        wgate = sb("wgate", [P, 2, LC, P])
        par = sb("par", [P, NPAR])
        ident = sb("ident", [P, P])
        ones = sb("ones", [P, P])
        before = sb("before", [P, P])
        wr = sb("wr", [P, KD, NE])
        brow = sb("brow", [1, NE])
        iota_s = sb("iota_s", [P, 2, CAP])
        iota_e = sb("iota_e", [P, NE])
        indc = sb("indc", [120, 4])
        indl = sb("indl", [24, NB])
        eps = sb("eps", [P, 1])
        small = sb("small", [P, 64])

        pos = [0]

        def part(width, shape=None, **kw):
            v = mix[:, pos[0]:pos[0] + width]
            pos[0] += width
            return v.rearrange(shape, **kw) if shape else v

        gpad = part(4 * (30 + TOK), "p (c t) -> p c t", c=LC)
        xpad = part(4 * (3 + TOK), "p (c t) -> p c t", c=LC)
        zg, za, th, gc, xc, tr, ti, av, uv = (part(LC * TOK, "p (c t) -> p c t", c=LC) for _ in range(9))
        hs = th
        assert pos[0] == MIXW
        stage_a = av.rearrange("p c t -> p (c t)")[:, 0:P]
        stage_b = tr.rearrange("p c t -> p (c t)")[:, 0:P]
        stage_h = uv.rearrange("p c t -> p (c t)")[0:NB, 0:LRU]
        rows_out = sq[:, 4:8, :].rearrange("p c t -> p (c t)")
        pos[0] = 0
        qT = part(KD * TOK, "p (c t) -> p c t", c=KD)
        oT = part(KD * TOK, "p (c t) -> p c t", c=KD)
        pm = part(H * 2 * NMEM, "p (h t m) -> p h t m", h=H, t=2)
        pT = part(H * 2 * SEQ, "p (h m t) -> p h m t", h=H, m=2)
        qs = part(D)
        sT = part(2 * NB * H, "p (m c) -> p m c", m=2)
        psS = part(2 * P)
        psT = part(2 * NB * H, "p (m c) -> p m c", m=2)
        pos[0] = 0
        xnt = part(3 * D, "p (t d) -> p t d", t=3)
        xeT = part(KD * CAP, "p (k s) -> p k s", k=KD)
        sel = part(3 * CAP, "p (t s) -> p t s", t=3)
        selg = part(3 * P, "p (t s) -> p t s", t=3)
        gT = part(3 * P)
        g1, u1, tg, hh, hT, ysb = (part(512) for _ in range(6))
        hTv = hT.rearrange("p (j s) -> p j s", j=4)
        b1row = part(2 * D)
        be2 = part(D)
        gfin = part(D)
        assert pos[0] <= MIXW
        sqf = sq[:, :, :].rearrange("p c t -> p (c t)")
        rkp = sqf[:, 0:3 * NCOL].rearrange("p (t c) -> p t c", t=3)
        gcol = sqf[:, 3 * NCOL:3 * NCOL + 3 * NE].rearrange("p (t c) -> p t c", t=3)
        mask = sqf[:, 576:576 + 96].rearrange("p (t c) -> p t c", t=3)
        lg = sqf[:, 672:768].rearrange("p (t c) -> p t c", t=3)
        flag = sqf[:, 768:896]
        scan = sqf[:, 896:1024]
        tb = sqf[:, 1024:1152]
        iota_b = sqf[:, 1152:1280]
        gcp = sqf[:, 1280:1280 + 3 * NCOL].rearrange("p (t c) -> p t c", t=3)
        tabrow = sqf[0:1, 1780:1908]
        rk = sqf[:, 1920:2016].rearrange("p (t c) -> p t c", t=3)
        gateT = xT[:, 0, :][0:NE, :]
        tabi = sb("tabi", [1, 2, P], I32)
        nblk = sb("nblk", [1, 1], I32)

        mn = sqf[:, 0:KD * NMEM].rearrange("p (k m) -> p k m", k=KD)
        ktok = tok[:, 0:2, :]
        x0 = ring[:, 0:2, :].rearrange("p s c -> p (s c)")[:, 0:3 * D].rearrange("p (t d) -> p t d", t=3)
        wlrep = ring[0:24, 1, D:D + LRU]
        lcache = ring[0:24, 1, D + LRU:D + 2 * LRU]
        mem = ring[:, 2, :].rearrange("p (t d) -> p t d", t=2)
        ccache = ring[0:120, 3, 0:2 * LRU].rearrange("p (t c) -> p t c", t=2)
        wcrep = ring[0:120, 3, 2 * LRU:3 * LRU]

        small_at = [0]

        def tiny(n):
            v = small[:, small_at[0]:small_at[0] + n]
            small_at[0] += n
            return v

        rm = tiny(2)
        mss = tiny(2)
        spn, spp, sp_e, sp_z, sp_q, sp_t = (tiny(4) for _ in range(6))
        hba, hbx = tiny(4), tiny(4)
        mxn, rs, fss, frs = tiny(8), tiny(8), tiny(3), tiny(3)

        extra = sb("extra", [P, 8 + 8 + 8 + 8 + 8])
        m8 = extra[:, 0:8]
        ge = extra[:, 8:16]
        idf = extra[:, 16:24]
        smx, ssum = extra[:, 24:25], extra[:, 25:26]
        tbc = extra[:, 27:28]
        gsum = extra[:, 28:29]
        nv0 = extra[:, 29:30]
        nm8 = sb("idx8", [P, 3, 8], U32)
        rstd = sb("rstd", [P, TOK])

        ps = [ctx.enter_context(nc.psum_tensor(f"ps{i}", [P, 512], F32)) for i in range(8)]

        filled = [sem(f"filled{i}") for i in range(RING)]
        names = """x_loaded par_loaded h0_loaded mem_loaded cc_loaded lc_loaded gate_loaded wr_loaded
        br_loaded consts zeroed ident_ready freed kc_freed
        x_turned x_copied x_squared sum_done sd_ready rstd_ready xn_ready par_turned par_ready
        mem_squared mem_sd mem_rec mem_scaled mem_turned mem_ready prods
        in_done in_kept glu_ready cf_tap cf_smp l_tap l_smp sp_chain sp_exp sp_ready
        kv_kept kt_turned kt_ready k_stored v_stored
        gate_done gate_tanh a_ready t_ready beta_chain u_ready scan_ready gelu_sq gelu_in gelu_th gelu_g ylru_ready
        rows_turned rows_kept rows_stored caches_shifted
        mu_done gc_cent gc_sq var_done ln_chain yn_ready y_th ycf_ready
        out_done res_added q_done q_kept score_done mx_ready p_exp p_scaled pt_turned pt_kept pv_done pv_kept
        qs_turned qs_kept qb_done dots_done s_turned smax_ready s_exp s_scaled sp_turned sp_kept spv_kept
        o_done tm_turned tokr_kept xnt_kept logit_done route_chain v0_ready ge_ready mask_ready rank_done
        gt0_turned gt0_kept be2_loaded b2_done tab_turned tab_ready table_ready
        tail_zeroed sel_ready selg_ready gathered xe_ready gt_turned gt_ready g_clamped u_clamped t_done tu_done h_ready
        h_turned hT_ready y_ready comb_done acc_done b1_filled b1_used gfin_loaded
        fin_sq fin_sd fin_rec fin_ready y_stored""".split()
        S = {n: sem(n) for n in names}

        def slot(n):
            return ring[:, n % RING, :]

        def wait_tile(eng, kind, done, o):
            if o % 2:
                eng.wait_ge(S["freed"], freed_after(START[kind] + o // 2))
            else:
                eng.wait_ge(S[done], o // 2 + 1)

        def wslot(n):
            return slot(n).rearrange("p (k c) -> p k c", k=KD)

        block = ctx.enter_context(nc.Block())

        @block.sync
        def _(sp):
            sp.dma_start(x0[:, 0:2, :], a["x_prompt"][0].rearrange("(t p) d -> p t d", p=P)).then_inc(S["x_loaded"], 16)
            sp.dma_start(x0[0:NB, 2, :], a["x_sample"].rearrange("b t d -> (b t) d")).then_inc(S["x_loaded"], 16)
            sp.dma_start(mem, a["mem_prompt"][0].rearrange("(t p) d -> p t d", p=P)).then_inc(S["mem_loaded"], 16)

            def source(kind, i):
                if kind == "kc" or kind == "vc":
                    c = a["cache_mem_k" if kind == "kc" else "cache_mem_v"]
                    return c[0, i].rearrange("(t p) h d -> p t (h d)", p=P)
                w = a["w_" + kind][0]
                c = IN_ORDER[i] if kind == "in" else i
                return w[:, 256 * c:256 * c + 256].rearrange("(k p) c -> p k c", p=P)

            for kind, count in FRONT:
                for i in range(count):
                    n = START[kind] + i
                    if n >= RING:
                        m = n - RING
                        if START["kc"] <= m < START["vc"]:
                            sp.wait_ge(S["kc_freed"], m - START["kc"] + 1)
                        else:
                            sp.wait_ge(S["freed"], freed_after(m))
                    dst = slot(n).rearrange("p (t c) -> p t c", t=2) if kind in ("kc", "vc") else wslot(n)
                    sp.dma_start(dst, source(kind, i)).then_inc(filled[n % RING], 16)

            def expert(e, b):
                for s in range(RING):
                    sp.wait_ge(S["freed"], RING * b + (freed_after(MOE0 + s - RING)))
                    if s < W_SLOTS:
                        src = a["w_e1"][0][bass.ds(e, 1), s * P:(s + 1) * P, :].rearrange("o p c -> p (o c)")
                        dst = ring[:, s, :]
                    else:
                        j = s - W_SLOTS
                        src = a["w_e2"][0][bass.ds(e, 1), j * 2 * P:(j + 1) * 2 * P, :].rearrange(
                            "o (t p) c -> p (o t) c", p=P)
                        dst = ring[:, s, :].rearrange("p (t c) -> p t c", t=2)
                    sp.dma_start(dst, src).then_inc(filled[s], 16)

            def bias(e):
                sp.dma_start(b1row[0:1, :], a["b_e1"][0][bass.ds(e, 1), :]).then_inc(S["b1_filled"], 16)

            expert(0, 0)
            sp.wait_ge(S["freed"], freed_after(MOE0 - 1))
            bias(0)
            sp.dma_start(be2[0:NE, :], a["b_e2"][0]).then_inc(S["be2_loaded"], 16)
            sp.dma_start(gfin, a["g_final"].partition_broadcast(P)).then_inc(S["gfin_loaded"], 16)
            with sp.Fori(1, NE) as e:
                sp.wait_ge(S["b1_used"], e)
                bias(e)
                expert(e, e)
            sp.wait_ge(S["table_ready"], 1)
            n = sp.value_load(nblk[0:1, 0:1], min_val=0, max_val=P)
            with sp.If(n > 0):
                with sp.Fori(0, n) as j:
                    e = sp.value_load(tabi[0:1, 0, bass.ds(j, 1)], min_val=0, max_val=NE - 1)
                    sp.wait_ge(S["b1_used"], j + NE)
                    bias(e)
                    expert(e, j + NE)
            sp.wait_ge(S["fin_ready"], 3)
            sp.dma_start(outs["y_prompt"][0].rearrange("(t p) d -> p t d", p=P), tok[:, 0:2, :]).then_inc(S["y_stored"], 16)
            sp.dma_start(outs["y_sample"].rearrange("b t d -> (b t) d"), tok[0:NB, 2, :]).then_inc(S["y_stored"], 16)
            sp.wait_ge(S["y_stored"], 32)
            sp.wait_ge(S["k_stored"], 16)
            sp.wait_ge(S["v_stored"], 16)
            sp.wait_ge(S["rows_stored"], 16 * 6)
            sp.wait_ge(S["caches_shifted"], 32)

        @block.gpsimd
        def _(pool):
            pool.memset(wgate[:, :, :, :], 0.0).then_inc(S["zeroed"], 1)
            pool.memset(gpad[:, :, 0:30], 0.0).then_inc(S["zeroed"], 1)
            pool.memset(xpad[:, :, 0:3], 0.0).then_inc(S["zeroed"], 1)
            pool.memset(ident[:, :], 0.0).then_inc(S["ident_ready"], 1)
            pool.memset(ones[:, :], 1.0).then_inc(S["consts"], 1)
            pool.memset(before[:, :], 1.0).then_inc(S["consts"], 1)
            pool.memset(indc[:, :], 1.0).then_inc(S["consts"], 1)
            pool.memset(indl[:, :], 1.0).then_inc(S["consts"], 1)
            pool.memset(eps[:, :], EPS).then_inc(S["consts"], 1)
            pool.iota(iota_s[:, :, :], pattern=[[0, 2], [1, CAP]], base=0, channel_multiplier=0,
                      allow_small_or_imprecise_dtypes=True).then_inc(S["consts"], 1)
            pool.iota(iota_e[:, :], pattern=[[1, NE]], base=0, channel_multiplier=0,
                      allow_small_or_imprecise_dtypes=True).then_inc(S["consts"], 1)
            pool.wait_ge(S["ident_ready"], 1)
            pool.affine_select(out=ident[:, :], in_=ident[:, :], compare_op=ALU.not_equal, fill=1.0, base=0,
                               pattern=[[-1, P]], channel_multiplier=1).then_inc(S["ident_ready"], 1)
            pool.wait_ge(S["consts"], 7)
            pool.affine_select(out=before[:, :], in_=before[:, :], compare_op=ALU.is_gt, fill=0.0, base=0,
                               pattern=[[1, P]], channel_multiplier=-1).then_inc(S["consts"], 1)
            for n, (ind, taps, width) in enumerate(((indc, CW - 1, 4), (indl, LW - 1, NB))):
                pool.affine_select(out=ind[:, :], in_=ind[:, :], compare_op=ALU.is_ge, fill=0.0, base=0,
                                   pattern=[[-taps, width]], channel_multiplier=1).then_inc(S["consts"], 1)
                pool.wait_ge(S["consts"], 9 + 2 * n)
                pool.affine_select(out=ind[:, :], in_=ind[:, :], compare_op=ALU.is_gt, fill=0.0, base=taps,
                                   pattern=[[taps, width]], channel_multiplier=-1).then_inc(S["consts"], 1)

            pool.wait_ge(S["xnt_kept"], 6)
            pool.memset(gT[:, TOK:3 * P], 0.0).then_inc(S["tail_zeroed"], 1)

        CONSTS = 12
        n_par = 16 * 13

        @block.scalar
        def _(act):
            act.dma_start(stage_a[0:CW * LC, :], a["w_cf_conv"][0].rearrange("w (t c) -> (w t) c", c=P)).then_inc(S["par_loaded"], 16)
            r = 0
            for name, rows in (("w_lru_conv", 16), ("b_lru_conv", 4), ("b_lru_a", 4), ("b_lru_x", 4), ("lru_lambda", 4),
                               ("b_cf_conv", 4), ("g_cf_ln", 4), ("b_cf_ln", 4), ("g_mix", 8), ("g_xa", 8),
                               ("g_mem", 8), ("g_moe", 8)):
                src = a[name]
                src = src[0].rearrange("w (t c) -> (w t) c", c=P) if rows == 16 else src.rearrange("o (t c) -> (o t) c", c=P)
                act.dma_start(stage_b[r:r + rows, :], src).then_inc(S["par_loaded"], 16)
                r += rows
            assert r == B_ROWS
            act.dma_start(stage_h, a["state_lru_h"][0]).then_inc(S["h0_loaded"], 16)
            act.dma_start(ccache, a["cache_cf_conv"][0].rearrange("(t b) w c -> (b w) t c", t=2)
                          if False else a["cache_cf_conv"][0].rearrange("b w c -> (b w) c").rearrange("(t r) c -> r t c", t=2)).then_inc(S["cc_loaded"], 16)
            for b in range(4):
                act.dma_start(wcrep[30 * b:30 * b + 30, :], a["w_cf_conv"][0, 0:30, :]).then_inc(S["cc_loaded"], 16)
            act.dma_start(lcache, a["cache_lru_conv"][0].rearrange("b w c -> (b w) c")).then_inc(S["lc_loaded"], 16)
            for b in range(NB):
                act.dma_start(wlrep[3 * b:3 * b + 3, :], a["w_lru_conv"][0, 0:3, :]).then_inc(S["lc_loaded"], 16)
            act.dma_start(wr[:, :, :], a["w_router"][0].rearrange("(k p) e -> p k e", p=P)).then_inc(S["wr_loaded"], 16)
            act.dma_start(brow[0:1, :], a["b_router"]).then_inc(S["br_loaded"], 16)
            act.wait_ge(S["zeroed"], 1)
            for g, name in enumerate(("w_lru_a", "w_lru_x")):
                w = a[name][0].rearrange("(c two) i j -> two i c j", two=2)
                for half in range(2):
                    r = slice(HEAD * half, HEAD * half + HEAD)
                    act.dma_start(wgate[r, g, :, r], w[half]).then_inc(S["gate_loaded"], 16)
            act.dma_start(outs["cache_lru"][0, :, 0:LW - 2, :], a["cache_lru_conv"][0, :, 1:LW - 1, :]).then_inc(S["caches_shifted"], 16)
            act.dma_start(outs["cache_cf"][0, :, 0:CW - 2, :], a["cache_cf_conv"][0, :, 1:CW - 1, :]).then_inc(S["caches_shifted"], 16)

            for k in range(KD):
                act.wait_ge(S["x_copied"], k + 1)
                act.activation(sq[:, k, :], xT[:, k, :], ACT.Square).then_inc(S["x_squared"], 1)
            act.wait_ge(S["mem_loaded"], 16)
            for t in range(2):
                act.activation(xc.rearrange("p c t -> p (c t)")[:, 0:D], mem[:, t, :], ACT.Square,
                               accum_out=mss[:, t:t + 1]).then_inc(S["mem_squared"], 1)
                act.wait_ge(S["mem_squared"], t + 1)

            def root(n):
                act.wait_ge(S["sum_done"], n + 1)
                act.activation(rstd[:, :], ps[5][:, 0:TOK], ACT.Sqrt, bias=eps[:, 0:1], scale=1.0 / D).then_inc(S["sd_ready"], 1)

            act.wait_ge(S["consts"], CONSTS)
            root(0)
            act.activation(rm, mss, ACT.Sqrt, bias=eps[:, 0:1], scale=1.0 / D).then_inc(S["mem_sd"], 1)
            act.wait_ge(S["par_ready"], 1)
            for j in range(4):
                act.wait_ge(S["mem_turned"], j + 1)
                for i in range(2):
                    k = 2 * j + i
                    act.activation(mn[:, k, :], ps[6 + j % 2][:, NMEM * i:NMEM * i + NMEM], ACT.Copy,
                                   scale=par[:, C_GMEM + k:C_GMEM + k + 1]).then_inc(S["mem_ready"], 1)
            act.wait_ge(S["par_ready"], 2)
            act.activation(sp_e, spn, ACT.Exp).then_inc(S["sp_exp"], 1)
            act.wait_ge(S["zeroed"], 3)
            for o in range(16):
                wait_tile(act, "in", "in_done", o)
                src, c = ps[o % 4][:, 0:TOK], o % 4
                if o < 4:
                    act.activation(za[:, c, :], src, ACT.Copy, scale=0.5).then_inc(S["in_kept"], 1)
                elif o < 8:
                    act.activation(th[:, c, :], src, ACT.Tanh, scale=0.5).then_inc(S["in_kept"], 1)
                elif o < 12:
                    act.activation(xpad[:, c, 3:3 + TOK], src, ACT.Copy).then_inc(S["in_kept"], 1)
                else:
                    act.activation(zg[:, c, :], src, ACT.Copy).then_inc(S["in_kept"], 1)

            def keep_kv(j, dst):
                act.wait_ge(S["freed"], freed_after(START["k"] + j))
                c = 256 * (j % 4)
                act.activation(dst[:, :, c:c + 256], ps[6 + j % 2][:, :].rearrange("p (t c) -> p t c", t=2),
                               ACT.Copy).then_inc(S["kv_kept"], 1)

            for j in range(4):
                keep_kv(j, ktok)
            act.wait_ge(S["kv_kept"], 4)
            act.dma_start(outs["mem_k"][0, 0].rearrange("(t p) h d -> p t (h d)", p=P), ktok).then_inc(S["k_stored"], 16)
            act.wait_ge(S["in_kept"], 16)
            act.activation(uv, zg, ACT.Square).then_inc(S["gelu_sq"], 1)
            act.wait_ge(S["gelu_in"], 2)
            act.activation(uv, uv, ACT.Tanh, scale=GELU_C).then_inc(S["gelu_th"], 1)
            for j in range(4):
                act.wait_ge(S["kt_turned"], j + 1)
                act.activation(kT[:, 2 * j:2 * j + 2, :], ps[6 + j % 2][:, :].rearrange("p (t c) -> p t c", t=2),
                               ACT.Copy).then_inc(S["kt_ready"], 1)
            act.wait_ge(S["sp_ready"], 1)
            for g, (dst, hb) in enumerate(((tr, hba), (ti, hbx))):
                for c in range(LC):
                    act.wait_ge(S["gate_done"], 4 * g + c + 1)
                    act.activation(dst[:, c, :], ps[c][:, 0:TOK], ACT.Tanh, bias=hb[:, c:c + 1],
                                   scale=0.5).then_inc(S["gate_tanh"], 1)
            act.wait_ge(S["gate_tanh"], 4)
            for c in range(LC):
                act.activation(av[:, c, :], tr[:, c, :], ACT.Exp, bias=spn[:, c:c + 1],
                               scale=spn[:, c:c + 1]).then_inc(S["a_ready"], 1)
            act.wait_ge(S["a_ready"], 4)
            for c in range(LC):
                act.activation(tr[:, c, :], tr[:, c, :], ACT.Tanh, bias=spp[:, c:c + 1],
                               scale=spp[:, c:c + 1]).then_inc(S["t_ready"], 1)
            act.wait_ge(S["beta_chain"], 3)
            act.activation(tr, tr, ACT.Sqrt).then_inc(S["t_ready"], 1)
            for j in range(4):
                keep_kv(4 + j, vtok)
            act.wait_ge(S["kv_kept"], 8)
            act.dma_start(outs["mem_v"][0, 0].rearrange("(t p) h d -> p t (h d)", p=P), vtok[:, :, :]).then_inc(S["v_stored"], 16)
            act.wait_ge(S["gc_cent"], 1)
            act.activation(gc, za, ACT.Square).then_inc(S["gc_sq"], 1)
            act.wait_ge(S["var_done"], 1)
            act.activation(rstd[:, :], ps[5][:, 0:TOK], ACT.Sqrt, bias=eps[:, 0:1], scale=1.0 / LRU).then_inc(S["ln_chain"], 1)
            act.wait_ge(S["yn_ready"], 1)
            act.activation(gc, za, ACT.Tanh, scale=0.5).then_inc(S["y_th"], 1)
            act.wait_ge(S["rows_kept"], 3)
            z3, g3, h3 = rows_out[0:11, 0:512], rows_out[0:38, 512:1024], tok[0:9, 2, 0:512]
            for dst, src in ((outs["lru_conv_prompt"][0, 0], z3[0:3, :]), (outs["cache_lru"][0, :, LW - 2, :], z3[3:11, :]),
                             (outs["cf_conv_prompt"][0, 0], g3[0:30, :]), (outs["cache_cf"][0, :, CW - 2, :], g3[30:38, :]),
                             (outs["lru_h_prompt"][0], h3[0:1, :]), (outs["lru_h_sample"][0], h3[1:9, :])):
                act.dma_start(dst, src).then_inc(S["rows_stored"], 16)
            act.wait_ge(S["rows_stored"], 16 * 6)
            for k in range(KD):
                act.wait_ge(S["res_added"], k + 1)
                act.activation(sq[:, k, :], xT[:, k, :], ACT.Square).then_inc(S["x_squared"], 1)
            root(1)
            for o in range(KD):
                wait_tile(act, "q", "q_done", o)
                act.activation(qT[:, o, :], ps[o % 4][:, 0:TOK], ACT.Copy, scale=HD ** -0.5).then_inc(S["q_kept"], 1)
            for i in range(2):
                act.wait_ge(S["qs_turned"], i + 1)
                act.activation(qs[0:NB, 512 * i:512 * i + 512], ps[6 + i][0:NB, :], ACT.Copy).then_inc(S["qs_kept"], 1)
            for h in range(H):
                act.wait_ge(S["mx_ready"], h + 1)
                for t in range(2):
                    act.activation(pm[:, h, t, :], ps[h][:, NMEM * t:NMEM * t + NMEM], ACT.Exp,
                                   bias=mxn[:, 2 * h + t:2 * h + t + 1],
                                   accum_out=rs[:, 2 * h + t:2 * h + t + 1]).then_inc(S["p_exp"], 1)
            for h in range(H):
                act.wait_ge(S["pt_turned"], h + 1)
                act.activation(pT[:, h, :, :], ps[6 + h % 2][:, :].rearrange("p (m t) -> p m t", m=2), ACT.Copy).then_inc(S["pt_kept"], 1)
            for h in range(H):
                act.wait_ge(S["pv_done"], h + 1)
                act.activation(oT[:, 2 * h:2 * h + 2, 0:SEQ], ps[h][:, :].rearrange("p (m t) -> p m t", m=2), ACT.Copy).then_inc(S["pv_kept"], 1)
            act.wait_ge(S["smax_ready"], 1)
            act.activation(psS[0:32, :], ps[6][0:32, 0:256], ACT.Exp, bias=smx[0:32, :], accum_out=ssum[0:32, :]).then_inc(S["s_exp"], 1)
            act.wait_ge(S["sp_turned"], 1)
            act.activation(psT, ps[7][:, 0:64].rearrange("p (m c) -> p m c", m=2), ACT.Copy).then_inc(S["sp_kept"], 1)
            act.wait_ge(S["freed"], freed_after(START["o"] - 1))
            act.activation(oT[:, :, SEQ:TOK], ps[4][:, 0:64].rearrange("p (c b) -> p c b", b=NB), ACT.Copy).then_inc(S["spv_kept"], 1)
            for k in range(KD):
                act.wait_ge(S["res_added"], KD + k + 1)
                act.activation(sq[:, k, :], xT[:, k, :], ACT.Square).then_inc(S["x_squared"], 1)
            root(2)
            for t, (t0, rows) in enumerate(TT):
                for i in range(2):
                    j = 6 + 2 * t + i
                    act.wait_ge(S["tm_turned"], j + 1)
                    act.activation(xnt[0:rows, t, 512 * i:512 * i + 512], ps[j % 4][0:rows, :], ACT.Copy).then_inc(S["xnt_kept"], 1)
            for t, (t0, rows) in enumerate(TT):
                act.wait_ge(S["v0_ready"], t + 1)
                act.activation(ge[0:rows, 0:4], m8[0:rows, 0:4], ACT.Exp, bias=nv0[0:rows, :],
                               accum_out=gsum[0:rows, :]).then_inc(S["ge_ready"], 1)
            act.wait_ge(S["gt0_turned"], 1)
            act.activation(gateT, ps[4][0:NE, 0:TOK], ACT.Copy).then_inc(S["gt0_kept"], 1)
            act.wait_ge(S["tab_turned"], 1)
            act.activation(tabrow, ps[5][0:1, 0:P], ACT.Copy).then_inc(S["tab_ready"], 1)

            def keep_gathered(n):
                act.wait_ge(S["gathered"], n + 1)
                act.activation(xeT, ps[4][:, :].rearrange("p (k s) -> p k s", k=KD), ACT.Copy).then_inc(S["xe_ready"], 1)

            def keep_gates(b):
                act.wait_ge(S["gt_turned"], b + 1)
                act.activation(gT[:, 0:TOK], ps[5][:, 0:TOK], ACT.Copy).then_inc(S["gt_ready"], 1)

            def half_swish(b):
                act.wait_ge(S["g_clamped"], b + 1)
                act.activation(tg, g1, ACT.Tanh, scale=ALPHA / 2).then_inc(S["t_done"], 1)

            def keep_h(b):
                act.wait_ge(S["h_turned"], b + 1)
                act.activation(hT, ps[2][:, :], ACT.Copy, scale=0.5).then_inc(S["hT_ready"], 1)

            def keep_y(b):
                act.wait_ge(S["freed"], RING * b + (freed_after(MOE0 - 1) + RING))
                act.activation(ysb, ps[3][:, :], ACT.Copy).then_inc(S["y_ready"], 1)

            keep_gathered(0)
            with act.Fori(0, NE) as b:
                half_swish(b)
                keep_gathered(b + 1)
                keep_gates(b)
                keep_h(b)
                keep_y(b)
            act.wait_ge(S["table_ready"], 1)
            n = act.value_load(nblk[0:1, 0:1], min_val=0, max_val=P)
            with act.If(n > 0):
                with act.Fori(0, n) as j:
                    keep_gathered(j + (NE + 1))
                    half_swish(j + NE)
                    keep_gates(j + NE)
                    keep_h(j + NE)
                    keep_y(j + NE)
            act.wait_ge(S["fin_sq"], 3)
            act.activation(frs, fss, ACT.Sqrt, bias=eps[:, 0:1], scale=1.0 / D).then_inc(S["fin_sd"], 1)

        @block.vector
        def _(dve):
            for k in range(KD):
                dve.wait_ge(S["x_turned"], k + 1)
                dve.tensor_copy(xT[:, k, :], ps[k % 4][:, 0:TOK]).then_inc(S["x_copied"], 1)
            dve.wait_ge(S["par_turned"], 1)
            dve.tensor_copy(par[:, :], ps[4][:, 0:NPAR]).then_inc(S["par_ready"], 1)
            dve.wait_ge(S["par_ready"], 1)
            lam = par[:, C_LAM:C_LAM + 4]
            dve.tensor_scalar(sp_t, lam, -1.0, None, ALU.mult).then_inc(S["sp_chain"], 1)
            dve.tensor_scalar(hba, par[:, C_BA:C_BA + 4], 0.5, None, ALU.mult).then_inc(S["sp_chain"], 1)
            dve.tensor_scalar(hbx, par[:, C_BX:C_BX + 4], 0.5, None, ALU.mult).then_inc(S["sp_chain"], 1)
            dve.wait_ge(S["sp_chain"], 3)
            dve.tensor_tensor(spn, lam, sp_t, ALU.min).then_inc(S["par_ready"], 1)

            def norm(n, gain):
                dve.wait_ge(S["sd_ready"], n + 1)
                dve.reciprocal(rstd[:, :], rstd[:, :]).then_inc(S["rstd_ready"], 1)
                dve.wait_ge(S["rstd_ready"], n + 1)
                for k in range(KD):
                    dve.scalar_tensor_tensor(out=xn[:, k, :], in0=xT[:, k, :], scalar=par[:, gain + k:gain + k + 1],
                                             in1=rstd[:, :], op0=ALU.mult, op1=ALU.mult).then_inc(S["xn_ready"], 1)

            dve.wait_ge(S["x_copied"], KD)
            norm(0, C_GMIX)
            dve.wait_ge(S["mem_sd"], 1)
            dve.reciprocal(rm, rm).then_inc(S["mem_rec"], 1)
            dve.wait_ge(S["mem_rec"], 1)
            for t in range(2):
                dve.tensor_scalar(mem[:, t, :], mem[:, t, :], rm[:, t:t + 1], None, ALU.mult).then_inc(S["mem_scaled"], 1)
            dve.wait_ge(S["cc_loaded"], 16 * 5)
            dve.wait_ge(S["lc_loaded"], 16 * 9)
            for t in range(2):
                dve.tensor_tensor(ccache[:, t, :], ccache[:, t, :], wcrep, ALU.mult).then_inc(S["prods"], 1)
            dve.tensor_tensor(lcache, lcache, wlrep, ALU.mult).then_inc(S["prods"], 1)
            n_sp = [3]

            def sp_step(ins):
                n_sp[0] += 1
                ins.then_inc(S["sp_chain"], 1)
                dve.wait_ge(S["sp_chain"], n_sp[0])

            dve.wait_ge(S["sp_exp"], 1)
            sp_step(dve.tensor_scalar(sp_q, sp_e, 2.0, None, ALU.add))
            sp_step(dve.reciprocal(sp_q, sp_q))
            sp_step(dve.tensor_tensor(sp_z, sp_e, sp_q, ALU.mult))
            sp_step(dve.tensor_tensor(sp_e, sp_z, sp_z, ALU.mult))
            sp_step(dve.tensor_scalar(sp_q, sp_e, 1.0 / 15, None, ALU.mult))
            for odd in (13, 11, 9, 7, 5, 3):
                sp_step(dve.scalar_tensor_tensor(out=sp_q, in0=sp_q, scalar=1.0 / odd, in1=sp_e, op0=ALU.add, op1=ALU.mult))
            sp_step(dve.scalar_tensor_tensor(out=sp_q, in0=sp_q, scalar=1.0, in1=sp_z, op0=ALU.add, op1=ALU.mult))
            sp_step(dve.tensor_scalar(sp_t, sp_t, 0.0, None, ALU.max))
            sp_step(dve.scalar_tensor_tensor(out=sp_q, in0=sp_q, scalar=2.0, in1=sp_t, op0=ALU.mult, op1=ALU.add))
            dve.tensor_scalar(spn, sp_q, -4.0, None, ALU.mult).then_inc(S["sp_chain"], 1)
            dve.wait_ge(S["sp_chain"], n_sp[0] + 1)
            dve.tensor_scalar(spp, sp_q, 4.0, None, ALU.mult).then_inc(S["sp_ready"], 1)

            dve.wait_ge(S["zeroed"], 3)
            for c in range(LC):
                dve.wait_ge(S["in_kept"], 5 + c)
                dve.scalar_tensor_tensor(out=gpad[:, c, 30:30 + TOK], in0=th[:, c, :], scalar=1.0, in1=za[:, c, :],
                                         op0=ALU.add, op1=ALU.mult).then_inc(S["glu_ready"], 1)
            dve.wait_ge(S["glu_ready"], 4)
            for c in range(LC):
                dve.tensor_scalar(gc[:, c, 0:SEQ], gpad[:, c, 0:SEQ], par[:, C_WCF + c:C_WCF + c + 1],
                                  par[:, C_BCF + c:C_BCF + c + 1], ALU.mult, ALU.add).then_inc(S["cf_tap"], 1)
            with dve.Fori(1, CW) as w:
                for c in range(LC):
                    dve.wait_ge(S["cf_tap"], 4 * w + (c - 3))
                    dve.scalar_tensor_tensor(out=gc[:, c, 0:SEQ], in0=gpad[:, c, bass.ds(w, SEQ)],
                                             scalar=par[:, bass.ds(4 * w + (C_WCF + c), 1)], in1=gc[:, c, 0:SEQ],
                                             op0=ALU.mult, op1=ALU.add).then_inc(S["cf_tap"], 1)
            dve.wait_ge(S["in_kept"], 12)
            for w in range(LW):
                for c in range(LC):
                    src, tap = xpad[:, c, w:w + SEQ], par[:, C_WL + 4 * w + c:C_WL + 4 * w + c + 1]
                    if w == 0:
                        dve.tensor_scalar(xc[:, c, 0:SEQ], src, tap, par[:, C_BLC + c:C_BLC + c + 1],
                                          ALU.mult, ALU.add).then_inc(S["l_tap"], 1)
                        continue
                    dve.wait_ge(S["l_tap"], 4 * w + c - 3)
                    dve.scalar_tensor_tensor(out=xc[:, c, 0:SEQ], in0=src, scalar=tap, in1=xc[:, c, 0:SEQ],
                                             op0=ALU.mult, op1=ALU.add).then_inc(S["l_tap"], 1)
            for c in range(LC):
                dve.tensor_scalar(xc[:, c, SEQ:TOK], xpad[:, c, 3 + SEQ:3 + TOK], par[:, C_WL + 12 + c:C_WL + 13 + c],
                                  par[:, C_BLC + c:C_BLC + c + 1], ALU.mult, ALU.add).then_inc(S["l_smp"], 1)
                dve.tensor_scalar(gc[:, c, SEQ:TOK], gpad[:, c, 30 + SEQ:30 + TOK],
                                  par[:, C_WCF + 120 + c:C_WCF + 121 + c],
                                  par[:, C_BCF + c:C_BCF + c + 1], ALU.mult, ALU.add).then_inc(S["l_smp"], 1)
            dve.wait_ge(S["l_smp"], 8)
            dve.wait_ge(S["freed"], HEADROOM)
            dve.tensor_tensor(xc[:, :, SEQ:TOK], xc[:, :, SEQ:TOK],
                              ps[4][:, 32:64].rearrange("p (c b) -> p c b", b=NB), ALU.add).then_inc(S["l_smp"], 1)
            dve.tensor_tensor(gc[:, :, SEQ:TOK], gc[:, :, SEQ:TOK],
                              ps[4][:, 0:32].rearrange("p (c b) -> p c b", b=NB), ALU.add).then_inc(S["cf_smp"], 1)
            dve.wait_ge(S["gelu_sq"], 1)
            dve.tensor_scalar(uv, uv, GELU_A, 1.0, ALU.mult, ALU.add).then_inc(S["gelu_in"], 1)
            dve.wait_ge(S["gelu_in"], 1)
            dve.tensor_tensor(uv, uv, zg, ALU.mult).then_inc(S["gelu_in"], 1)
            dve.wait_ge(S["gelu_th"], 1)
            dve.scalar_tensor_tensor(out=zg, in0=uv, scalar=1.0, in1=zg, op0=ALU.add, op1=ALU.mult).then_inc(S["gelu_g"], 1)
            dve.wait_ge(S["mu_done"], 1)
            dve.scalar_tensor_tensor(out=za, in0=ps[5][:, 0:TOK].unsqueeze(1).to_broadcast([P, LC, TOK]),
                                     scalar=-1.0 / LRU, in1=gc, op0=ALU.mult, op1=ALU.add).then_inc(S["gc_cent"], 1)
            dve.wait_ge(S["gate_tanh"], 8)
            dve.wait_ge(S["gelu_g"], 1)
            dve.scalar_tensor_tensor(out=ti, in0=ti, scalar=1.0, in1=xc, op0=ALU.add, op1=ALU.mult).then_inc(S["beta_chain"], 1)
            dve.wait_ge(S["t_ready"], 4)
            dve.tensor_scalar(uv, tr, 1.0, 0.5, ALU.add, ALU.mult).then_inc(S["beta_chain"], 1)
            dve.wait_ge(S["beta_chain"], 2)
            dve.reciprocal(uv, uv).then_inc(S["u_ready"], 1)
            dve.wait_ge(S["u_ready"], 1)
            dve.tensor_tensor(tr, tr, uv, ALU.mult).then_inc(S["beta_chain"], 1)
            dve.wait_ge(S["t_ready"], 5)
            dve.scalar_tensor_tensor(out=uv, in0=tr, scalar=0.5, in1=ti, op0=ALU.mult, op1=ALU.mult).then_inc(S["u_ready"], 1)
            dve.wait_ge(S["u_ready"], 2)
            dve.wait_ge(S["a_ready"], 4)
            for c in range(LC):
                dve.tensor_tensor_scan(hs[:, c, 0:SEQ], av[:, c, 0:SEQ], uv[:, c, 0:SEQ], 0.0,
                                       ALU.mult, ALU.add).then_inc(S["scan_ready"], 1)
            dve.tensor_tensor(hs[:, :, SEQ:TOK], av[:, :, SEQ:TOK],
                              par[:, C_H0:C_H0 + 32].rearrange("p (c b) -> p c b", b=NB), ALU.mult).then_inc(S["scan_ready"], 1)
            dve.wait_ge(S["scan_ready"], 5)
            dve.tensor_tensor(hs[:, :, SEQ:TOK], hs[:, :, SEQ:TOK], uv[:, :, SEQ:TOK], ALU.add).then_inc(S["scan_ready"], 1)
            dve.wait_ge(S["scan_ready"], 6)
            dve.scalar_tensor_tensor(out=zg, in0=zg, scalar=0.5, in1=hs, op0=ALU.mult, op1=ALU.mult).then_inc(S["ylru_ready"], 1)
            dve.wait_ge(S["ln_chain"], 1)
            dve.reciprocal(rstd[:, :], rstd[:, :]).then_inc(S["ln_chain"], 1)
            dve.wait_ge(S["ln_chain"], 2)
            dve.tensor_tensor(za, za, rstd[:, :].unsqueeze(1).to_broadcast([P, LC, TOK]), ALU.mult).then_inc(S["ln_chain"], 1)
            dve.wait_ge(S["ln_chain"], 3)
            for c in range(LC):
                last = dve.tensor_scalar(za[:, c, :], za[:, c, :], par[:, C_GLN + c:C_GLN + c + 1],
                                         par[:, C_BLN + c:C_BLN + c + 1], ALU.mult, ALU.add)
            last.then_inc(S["yn_ready"], 1)
            dve.wait_ge(S["y_th"], 1)
            dve.tensor_scalar(gc, gc, 1.0, 0.5, ALU.add, ALU.mult).then_inc(S["ln_chain"], 1)
            dve.wait_ge(S["ln_chain"], 4)
            dve.tensor_tensor(gc, gc, za, ALU.mult).then_inc(S["ycf_ready"], 1)
            dve.wait_ge(S["rows_turned"], 1)
            dve.tensor_copy(rows_out[0:11, 0:512], ps[6][0:11, :]).then_inc(S["rows_kept"], 1)
            dve.wait_ge(S["rows_turned"], 2)
            dve.tensor_copy(rows_out[0:38, 512:1024], ps[7][0:38, :]).then_inc(S["rows_kept"], 1)
            dve.wait_ge(S["rows_turned"], 3)
            dve.tensor_copy(tok[0:9, 2, 0:512], ps[4][0:9, :]).then_inc(S["rows_kept"], 1)

            def residual(kind, done, base):
                for o in range(KD):
                    wait_tile(dve, kind, done, o)
                    dve.tensor_tensor(xT[:, o, :], xT[:, o, :], ps[o % 4][:, 0:TOK], ALU.add).then_inc(S["res_added"], 1)
                dve.wait_ge(S["res_added"], base + KD)

            residual("out", "out_done", 0)
            norm(1, C_GXA)
            for h in range(H):
                dve.wait_ge(S["score_done"], h + 1)
                dve.tensor_reduce(mxn[:, 2 * h:2 * h + 2], ps[h][:, :].rearrange("p (t m) -> p t m", t=2), AX.X,
                                  ALU.max, negate=True).then_inc(S["mx_ready"], 1)
            n_rec = 0
            for h in range(H):
                dve.wait_ge(S["p_exp"], 2 * h + 2)
                dve.reciprocal(rs[:, 2 * h:2 * h + 2], rs[:, 2 * h:2 * h + 2]).then_inc(S["mx_ready"], 1)
                dve.wait_ge(S["mx_ready"], H + h + 1)
                for t in range(2):
                    last = dve.tensor_scalar(pm[:, h, t, :], pm[:, h, t, :], rs[:, 2 * h + t:2 * h + t + 1], None, ALU.mult)
                last.then_inc(S["p_scaled"], 1)
            for b in range(NB):
                n = START["kc"] + b
                dve.wait_ge(filled[n % RING], 16 * fills_before(n))
                dve.wait_ge(S["qb_done"], b + 1)
                key = slot(n).rearrange("p (t h d) -> p t h d", t=2, h=H)
                for t in range(2):
                    for h in range(H):
                        q = ps[4 + h // 2][:, HD * (h % 2):HD * (h % 2) + HD]
                        last = dve.tensor_tensor_reduce(key[:, t, h, :], key[:, t, h, :], q, 1.0, 0.0, ALU.mult, ALU.add,
                                                        sT[:, t, 4 * b + h:4 * b + h + 1])
                last.then_inc(S["kc_freed"], 1)
            dve.wait_ge(S["s_turned"], 1)
            dve.tensor_reduce(smx[0:32, :], ps[6][0:32, 0:256], AX.X, ALU.max, negate=True).then_inc(S["smax_ready"], 1)
            dve.wait_ge(S["s_exp"], 1)
            dve.reciprocal(ssum[0:32, :], ssum[0:32, :]).then_inc(S["s_scaled"], 1)
            dve.wait_ge(S["s_scaled"], 1)
            dve.tensor_scalar(psS[0:32, :], psS[0:32, :], ssum[0:32, :], None, ALU.mult).then_inc(S["s_scaled"], 1)
            residual("o", "o_done", KD)
            norm(2, C_GMOE)
            dve.wait_ge(S["k_stored"], 16)
            dve.wait_ge(S["rows_stored"], 16 * 6)
            for t, (t0, rows) in enumerate(TT):
                for i in range(2):
                    j = 2 * t + i
                    dve.wait_ge(S["tm_turned"], j + 1)
                    dve.tensor_copy(tok[0:rows, t, 512 * i:512 * i + 512], ps[j % 4][0:rows, :]).then_inc(S["tokr_kept"], 1)
            n_rt = [0]

            def step(ins):
                n_rt[0] += 1
                ins.then_inc(S["route_chain"], 1)
                dve.wait_ge(S["route_chain"], n_rt[0])

            dve.wait_ge(S["logit_done"], 1)
            for t, (t0, rows) in enumerate(TT):
                r = slice(0, rows)
                step(dve.tensor_copy(lg[r, t, :], ps[4][r, NE * t:NE * t + NE]))
                step(dve.max(m8[r, :], lg[r, t, :]))
                dve.tensor_scalar(nv0[r, :], m8[r, 0:1], -1.0, None, ALU.mult).then_inc(S["v0_ready"], 1)
                step(dve.max_index(nm8[r, t, :], m8[r, :], lg[r, t, :]))
                step(dve.tensor_copy(idf[r, :], nm8[r, t, :]))
                step(dve.tensor_scalar(mask[r, t, :], iota_e[r, :], idf[r, 0:1], None, ALU.is_equal))
                for k in range(1, 4):
                    step(dve.scalar_tensor_tensor(out=mask[r, t, :], in0=iota_e[r, :], scalar=idf[r, k:k + 1],
                                                  in1=mask[r, t, :], op0=ALU.is_equal, op1=ALU.add))
                dve.wait_ge(S["ge_ready"], t + 1)
                step(dve.reciprocal(gsum[r, :], gsum[r, :]))
                step(dve.tensor_scalar(ge[r, 0:4], ge[r, 0:4], gsum[r, :], None, ALU.mult))
                step(dve.tensor_scalar(gcol[r, t, :], iota_e[r, :], idf[r, 0:1], ge[r, 0:1], ALU.is_equal, ALU.mult))
                for k in range(1, 4):
                    step(dve.tensor_scalar(lg[r, t, :], iota_e[r, :], idf[r, k:k + 1], ge[r, k:k + 1], ALU.is_equal, ALU.mult))
                    step(dve.tensor_tensor(gcol[r, t, :], gcol[r, t, :], lg[r, t, :], ALU.add))
                dve.tensor_scalar(rk[r, t, :], mask[r, t, :], -BIG, BIG, ALU.mult, ALU.add).then_inc(S["mask_ready"], 1)
            dve.wait_ge(S["mask_ready"], 3)
            dve.wait_ge(S["rank_done"], 1)
            for t, (t0, rows) in enumerate(TT):
                r = slice(0, rows)
                step(dve.tensor_tensor(rkp[r, t, 0:NE], rk[r, t, :], ps[5][r, NE * t:NE * t + NE], ALU.add))
                step(dve.tensor_copy(gcp[r, t, :].rearrange("p (q e) -> p q e", e=NE),
                                     gcol[r, t, :].unsqueeze(1).to_broadcast([rows, PASSES, NE])))
                for q in range(1, PASSES):
                    step(dve.tensor_scalar(rkp[r, t, NE * q:NE * q + NE], rkp[r, t, 0:NE], -float(CAP * q), None, ALU.add))
            count = ps[5][:, 96:128]
            for q in range(1, PASSES):
                step(dve.tensor_scalar(flag[:, NE * (q - 1):NE * q], count, float(CAP * q), None, ALU.is_gt))
            step(dve.tensor_tensor_scan(scan, flag, flag, 0.0, ALU.add, ALU.max)
                 if False else dve.tensor_tensor_scan(scan, ones[:, :], flag, 0.0, ALU.mult, ALU.add))
            step(dve.tensor_copy(nblk[0:1, 0:1], scan[0:1, P - 1:P]))
            step(dve.tensor_scalar(tb, before[:, :], 1.0, None, ALU.mult))
            step(dve.tensor_reduce(tbc, tb, AX.X, ALU.add))
            step(dve.tensor_scalar(tbc, tbc, -1.0, float(P), ALU.mult, ALU.add))
            step(dve.tensor_scalar(tb, scan, tbc, None, ALU.is_equal))
            step(dve.tensor_tensor(tb, tb, flag, ALU.mult))
            step(dve.tensor_tensor_scan(iota_b, ones[:, :], ones[:, :], -1.0, ALU.mult, ALU.add))
            step(dve.tensor_tensor(tb, tb, iota_b, ALU.mult))
            dve.tensor_reduce(tbc, tb, AX.X, ALU.add).then_inc(S["tab_ready"], 1)
            dve.wait_ge(S["tab_ready"], 2)
            step(dve.tensor_copy(tabi[0:1, 1, :], tabrow))
            step(dve.tensor_scalar(tabi[0:1, 0, :], tabi[0:1, 1, :], NE - 1, None, ALU.bitwise_and))
            step(dve.tensor_scalar(tabrow, tabrow, float(NE), None, ALU.add))
            dve.tensor_copy(tabi[0:1, 1, :], tabrow).then_inc(S["table_ready"], 1)

            def add_rounds(first):
                for t, (t0, rows) in enumerate(TT):
                    dve.wait_ge(S["comb_done"], first + (t + 1))
                    for i in range(2):
                        dst = tok[0:rows, t, 512 * i:512 * i + 512]
                        last = dve.tensor_tensor(dst, dst, ps[6 + i][0:rows, :], ALU.add)
                    last.then_inc(S["acc_done"], 1)

            def one_hot(n, col):
                dve.wait_ge(S["gathered"], n)
                for t, (t0, rows) in enumerate(TT):
                    last = dve.tensor_scalar(sel[0:rows, t, :], iota_s[0:rows, 0, :], rkp[0:rows, t, bass.ds(col, 1)],
                                             None, ALU.is_equal)
                last.then_inc(S["sel_ready"], 1)

            def gated(col):
                for t, (t0, rows) in enumerate(TT):
                    last = dve.tensor_scalar(selg[0:rows, t, :], iota_s[0:rows, :, :].rearrange("p a s -> p (a s)"),
                                             rkp[0:rows, t, bass.ds(col, 1)], gcp[0:rows, t, bass.ds(col, 1)],
                                             ALU.is_equal, ALU.mult)
                last.then_inc(S["selg_ready"], 1)

            def swiglu(b):
                dve.wait_ge(S["freed"], RING * b + (freed_after(MOE0 - 1) + W_SLOTS))
                dve.tensor_scalar(g1, ps[0][:, :], LIMIT, None, ALU.min).then_inc(S["g_clamped"], 1)
                dve.tensor_scalar(u1, ps[1][:, :], -LIMIT, LIMIT, ALU.max, ALU.min).then_inc(S["u_clamped"], 1)
                dve.wait_ge(S["t_done"], b + 1)
                dve.scalar_tensor_tensor(out=tg, in0=tg, scalar=1.0, in1=g1, op0=ALU.add, op1=ALU.mult).then_inc(S["tu_done"], 1)
                dve.wait_ge(S["tu_done"], b + 1)
                dve.wait_ge(S["u_clamped"], b + 1)
                dve.scalar_tensor_tensor(out=hh, in0=u1, scalar=1.0, in1=tg, op0=ALU.add, op1=ALU.mult).then_inc(S["h_ready"], 1)

            dve.memset(fss, 0.0).then_inc(S["fin_rec"], 1)
            dve.wait_ge(S["route_chain"], n_rt[0])
            for t, (t0, rows) in enumerate(TT):
                last = dve.tensor_scalar(sel[0:rows, t, :], iota_s[0:rows, 0, :], rkp[0:rows, t, 0:1], None, ALU.is_equal)
            last.then_inc(S["sel_ready"], 1)
            dve.wait_ge(S["tokr_kept"], 6)
            with dve.Fori(0, NE) as b:
                add_rounds(3 * b)
                one_hot(b + 1, b + 1)
                gated(b)
                swiglu(b)
            add_rounds(3 * NE)
            n = dve.value_load(nblk[0:1, 0:1], min_val=0, max_val=P)
            with dve.If(n > 0):
                with dve.Fori(0, n) as j:
                    col = dve.value_load(tabi[0:1, 1, bass.ds(j, 1)], min_val=NE, max_val=NCOL - 1)
                    one_hot(j + (NE + 1), col)
                    gated(col)
                    swiglu(j + NE)
                    add_rounds(3 * j + 3 * (NE + 1))
            dve.wait_ge(S["acc_done"], 3 * n + 3 * (NE + 1))
            dve.wait_ge(S["fin_rec"], 1)
            for t, (t0, rows) in enumerate(TT):
                r = slice(0, rows)
                dve.tensor_tensor_reduce(xnt[r, t, :], tok[r, t, :], tok[r, t, :], 1.0, 0.0, ALU.mult, ALU.add,
                                         fss[r, t:t + 1]).then_inc(S["fin_sq"], 1)
            dve.wait_ge(S["fin_sd"], 1)
            dve.reciprocal(frs, frs).then_inc(S["fin_rec"], 1)
            dve.wait_ge(S["fin_rec"], 2)
            dve.wait_ge(S["gfin_loaded"], 16)
            for t, (t0, rows) in enumerate(TT):
                r = slice(0, rows)
                dve.scalar_tensor_tensor(out=tok[r, t, :], in0=tok[r, t, :], scalar=frs[r, t:t + 1], in1=gfin[r, :],
                                         op0=ALU.mult, op1=ALU.mult).then_inc(S["fin_ready"], 1)

        @block.tensor
        def _(pe):
            pe.wait_ge(S["ident_ready"], 2)
            pe.wait_ge(S["x_loaded"], 32)
            for k in range(KD):
                if k >= 4:
                    pe.wait_ge(S["x_copied"], k - 3)
                for t, (t0, rows) in enumerate(TT):
                    m = pe.transpose(ps[k % 4][:, t0:t0 + rows], x0[0:rows, t, k * P:(k + 1) * P], ident[0:rows, 0:rows])
                m.then_inc(S["x_turned"], 1)
            pe.wait_ge(S["par_loaded"], n_par)
            pe.wait_ge(S["h0_loaded"], 16)
            pe.transpose(ps[4][:, 0:C_B], stage_a[0:C_B, :], ident[0:C_B, 0:C_B])
            pe.transpose(ps[4][:, C_B:C_H0], stage_b[0:B_ROWS, :], ident[0:B_ROWS, 0:B_ROWS])
            for c in range(LC):
                m = pe.transpose(ps[4][:, C_H0 + NB * c:C_H0 + NB * c + NB], stage_h[:, c * P:(c + 1) * P], ident[0:NB, 0:NB])
            m.then_inc(S["par_turned"], 1)
            pe.wait_ge(S["consts"], CONSTS)

            def norm_sum(n):
                for k in range(KD):
                    pe.wait_ge(S["x_squared"], KD * n + k + 1)
                    m = pe.matmul(ps[5][:, 0:TOK], ones[:, :], sq[:, k, :], start=(k == 0), stop=(k == KD - 1))
                m.then_inc(S["sum_done"], 1)

            norm_sum(0)
            for j in range(4):
                if j == 0:
                    pe.wait_ge(S["mem_scaled"], 2)
                if j >= 2:
                    pe.wait_ge(S["mem_ready"], 2 * (j - 1))
                for i in range(2):
                    for t in range(2):
                        m = pe.transpose(ps[6 + j % 2][:, NMEM * i + P * t:NMEM * i + P * t + P],
                                         mem[:, t, (2 * j + i) * P:(2 * j + i + 1) * P], ident[:, :])
                m.then_inc(S["mem_turned"], 1)
            pe.wait_ge(S["prods"], 3)
            pe.wait_ge(S["par_ready"], 1)
            for c in range(LC):
                for t in range(2):
                    pe.matmul(ps[4][:, NB * c + 4 * t:NB * c + 4 * t + 4], ccache[:, t, c * P:(c + 1) * P], indc[:, :],
                              start=True, stop=True)
                m = pe.matmul(ps[4][:, 32 + NB * c:40 + NB * c], lcache[:, c * P:(c + 1) * P], indl[:, :],
                              start=True, stop=True)
            m.then_inc(S["freed"], HEADROOM)

            def project(kind, done, src, bank_free, first_wait):
                count = dict(FRONT)[kind]
                for i in range(count):
                    n = START[kind] + i
                    pe.wait_ge(filled[n % RING], 16 * fills_before(n))
                    for half in range(2):
                        o = 2 * i + half
                        bank_free(o)
                        for k in range(KD):
                            if i == 0 and half == 0:
                                first_wait(k)
                            m = pe.matmul(ps[o % 4][:, 0:TOK], wslot(n)[:, k, half * P:(half + 1) * P], src(k),
                                          start=(k == 0), stop=(k == KD - 1))
                        m.then_inc(S["freed" if half else done], 1)

            def in_free(o):
                if o >= 4:
                    pe.wait_ge(S["in_kept"], o - 3)

            project("in", "in_done", lambda k: xn[:, k, :], in_free, lambda k: pe.wait_ge(S["xn_ready"], k + 1))

            def kv(kind, j0):
                for i in range(4):
                    n, j = START[kind] + i, j0 + i
                    pe.wait_ge(filled[n % RING], 16 * fills_before(n))
                    if j >= 2:
                        pe.wait_ge(S["kv_kept"], j - 1)
                    if j == 4:
                        pe.wait_ge(S["kt_ready"], 3)
                    if j == 5:
                        pe.wait_ge(S["kt_ready"], 4)
                    for t in range(2):
                        for k in range(KD):
                            m = pe.matmul(ps[6 + j % 2][:, 256 * t:256 * t + 256], mn[:, k, P * t:P * t + P],
                                          wslot(n)[:, k, :], start=(k == 0), stop=(k == KD - 1))
                    m.then_inc(S["freed"], 1)

            pe.wait_ge(S["mem_ready"], KD)
            kv("k", 0)
            pe.wait_ge(S["kv_kept"], 4)
            for j in range(4):
                if j >= 2:
                    pe.wait_ge(S["kt_ready"], j - 1)
                for i in range(2):
                    for t in range(2):
                        m = pe.transpose(ps[6 + j % 2][:, NMEM * i + P * t:NMEM * i + P * t + P],
                                         ktok[:, t, (2 * j + i) * P:(2 * j + i + 1) * P], ident[:, :])
                m.then_inc(S["kt_turned"], 1)
            pe.wait_ge(S["gate_loaded"], 64)
            pe.wait_ge(S["l_tap"], 16)
            pe.wait_ge(S["l_smp"], 9)
            pe.wait_ge(S["in_kept"], 16)
            for g in range(2):
                for c in range(LC):
                    if g:
                        pe.wait_ge(S["gate_tanh"], c + 1)
                    pe.matmul(ps[c][:, 0:TOK], wgate[:, g, c, :], xc[:, c, :], start=True, stop=True).then_inc(S["gate_done"], 1)
            pe.wait_ge(S["cf_smp"], 1)
            pe.wait_ge(S["cf_tap"], 4 * CW)
            for c in range(LC):
                m = pe.matmul(ps[5][:, 0:TOK], ones[:, :], gc[:, c, :], start=(c == 0), stop=(c == LC - 1))
            m.then_inc(S["mu_done"], 1)
            kv("v", 4)
            pe.wait_ge(S["gc_sq"], 1)
            for c in range(LC):
                m = pe.matmul(ps[5][:, 0:TOK], ones[:, :], gc[:, c, :], start=(c == 0), stop=(c == LC - 1))
            m.then_inc(S["var_done"], 1)
            pe.wait_ge(S["kv_kept"], 8)
            for c in range(LC):
                m = pe.transpose(ps[6][0:11, c * P:(c + 1) * P], xpad[:, c, 3 + SEQ - 3:3 + TOK], ident[:, :])
            m.then_inc(S["rows_turned"], 1)
            for c in range(LC):
                m = pe.transpose(ps[7][0:38, c * P:(c + 1) * P], gpad[:, c, 30 + SEQ - 30:30 + TOK], ident[:, :])
            m.then_inc(S["rows_turned"], 1)
            pe.wait_ge(S["scan_ready"], 6)
            for c in range(LC):
                m = pe.transpose(ps[4][0:9, c * P:(c + 1) * P], hs[:, c, SEQ - 1:TOK], ident[:, :])
            m.then_inc(S["rows_turned"], 1)

            def out_free(o):
                if o >= 4:
                    pe.wait_ge(S["res_added"], o - 3)

            pe.wait_ge(S["ylru_ready"], 1)
            pe.wait_ge(S["gate_tanh"], 8)

            def out_wait(k):
                if k == 4:
                    pe.wait_ge(S["ycf_ready"], 1)

            project("out", "out_done", lambda k: zg[:, k, :] if k < 4 else gc[:, k - 4, :], out_free, out_wait)
            norm_sum(1)

            def q_free(o):
                if o < 4:
                    pe.wait_ge(S["res_added"], o + 5)
                else:
                    pe.wait_ge(S["q_kept"], o - 3)

            project("q", "q_done", lambda k: xn[:, k, :], q_free, lambda k: pe.wait_ge(S["xn_ready"], KD + k + 1))
            pe.wait_ge(S["q_kept"], KD)
            pe.wait_ge(S["rows_kept"], 3)
            for i in range(2):
                for c in range(4):
                    m = pe.transpose(ps[6 + i][0:NB, c * P:(c + 1) * P], qT[:, 4 * i + c, SEQ:TOK], ident[:, :])
                m.then_inc(S["qs_turned"], 1)
            for h in range(H):
                for t in range(2):
                    for i in range(2):
                        m = pe.matmul(ps[h][:, NMEM * t:NMEM * t + NMEM], qT[:, 2 * h + i, P * t:P * t + P],
                                      kT[:, 2 * h + i, :], start=(i == 0), stop=(i == 1))
                m.then_inc(S["score_done"], 1)
            pe.wait_ge(S["qs_kept"], 2)

            def spread(b):
                for i in range(2):
                    m = pe.matmul(ps[4 + i][:, :], ident[0:NB, b:b + 1].to_broadcast([NB, P]),
                                  qs[0:NB, 512 * i:512 * i + 512], start=True, stop=True)
                m.then_inc(S["qb_done"], 1)

            pe.wait_ge(S["rstd_ready"], 2)
            spread(0)
            for h in range(H):
                pe.wait_ge(S["p_scaled"], h + 1)
                if h >= 2:
                    pe.wait_ge(S["pt_kept"], h - 1)
                for mt in range(2):
                    for t in range(2):
                        m = pe.transpose(ps[6 + h % 2][:, SEQ * mt + P * t:SEQ * mt + P * t + P],
                                         pm[:, h, t, P * mt:P * mt + P], ident[:, :])
                m.then_inc(S["pt_turned"], 1)
            for b in range(1, NB):
                pe.wait_ge(S["kc_freed"], b)
                spread(b)
                if b % 2 == 0 or b == NB - 1:
                    h = (b - 1) // 2
                    pe.wait_ge(S["pt_kept"], h + 1)
                    for i in range(2):
                        for mt in range(2):
                            m = pe.matmul(ps[h][:, SEQ * i:SEQ * i + SEQ], vtok[:, mt, HD * h + P * i:HD * h + P * i + P],
                                          pT[:, h, mt, :], start=(mt == 0), stop=(mt == 1))
                    m.then_inc(S["pv_done"], 1)
            pe.wait_ge(S["kc_freed"], NB)
            for t in range(2):
                m = pe.transpose(ps[6][0:32, P * t:P * t + P], sT[:, t, :], ident[:, :])
            m.then_inc(S["s_turned"], 1)
            pe.wait_ge(S["s_scaled"], 2)
            for t in range(2):
                m = pe.transpose(ps[7][:, 32 * t:32 * t + 32], psS[0:32, P * t:P * t + P], ident[0:32, 0:32])
            m.then_inc(S["sp_turned"], 1)
            pe.wait_ge(S["sp_kept"], 1)
            for b in range(NB):
                n = START["vc"] + b
                pe.wait_ge(filled[n % RING], 16 * fills_before(n))
                val = slot(n).rearrange("p (t c) -> p t c", t=2)
                for c in range(KD):
                    for t in range(2):
                        m = pe.matmul(ps[4][:, NB * c + b:NB * c + b + 1], val[:, t, P * c:P * c + P],
                                      psT[:, t, 4 * b + c // 2:4 * b + c // 2 + 1], start=(t == 0), stop=(t == 1))
                m.then_inc(S["freed"], 1)
            pe.wait_ge(S["spv_kept"], 1)
            pe.wait_ge(S["pv_kept"], H)

            def o_free(o):
                if o >= 4:
                    pe.wait_ge(S["res_added"], KD + o - 3)

            project("o", "o_done", lambda k: oT[:, k, :], o_free, lambda k: None)
            norm_sum(2)
            for j in range(12):
                t, i = (j % 6) // 2, j % 2
                t0, rows = TT[t]
                if j == 0:
                    pe.wait_ge(S["res_added"], 2 * KD)
                if j >= 4:
                    pe.wait_ge(S["tokr_kept"], min(j - 3, 6))
                if j >= 10:
                    pe.wait_ge(S["xnt_kept"], j - 9)
                src = xT if j < 6 else xn
                for c in range(4):
                    if j == 6 + i:
                        pe.wait_ge(S["xn_ready"], 2 * KD + 4 * i + c + 1)
                    m = pe.transpose(ps[j % 4][0:rows, c * P:(c + 1) * P], src[:, 4 * i + c, t0:t0 + rows], ident[:, :])
                m.then_inc(S["tm_turned"], 1)
            pe.wait_ge(S["wr_loaded"], 16)
            pe.wait_ge(S["br_loaded"], 16)
            for t, (t0, rows) in enumerate(TT):
                dst = ps[4][0:rows, NE * t:NE * t + NE]
                pe.matmul(dst, ones[0:1, 0:rows], brow[0:1, :], start=True, stop=False)
                for k in range(KD):
                    m = pe.matmul(dst, xn[:, k, t0:t0 + rows], wr[:, k, :], start=False, stop=(k == KD - 1))
            m.then_inc(S["logit_done"], 1)
            pe.wait_ge(S["mask_ready"], 3)
            for t, (t0, rows) in enumerate(TT):
                for i in range(t + 1):
                    n_k = TT[i][1]
                    lhs = before if i == t else ones
                    m = pe.matmul(ps[5][0:rows, NE * t:NE * t + NE], lhs[0:n_k, 0:rows], mask[0:n_k, i, :],
                                  start=(i == 0), stop=(i == t))
            for i, (t0, n_k) in enumerate(TT):
                m = pe.matmul(ps[5][:, 96:128], ones[0:n_k, :], mask[0:n_k, i, :], start=(i == 0), stop=(i == 2))
            m.then_inc(S["rank_done"], 1)
            for t, (t0, rows) in enumerate(TT):
                m = pe.transpose(ps[4][0:NE, t0:t0 + rows], gcol[0:rows, t, :], ident[0:rows, 0:rows])
            m.then_inc(S["gt0_turned"], 1)

            def combine(t, lhs, rhs, free, rows):
                t0 = TT[t][0]
                pe.wait_ge(S["acc_done"], free)
                for i in range(2):
                    m = pe.matmul(ps[6 + i][0:rows, :], lhs(i, t0, rows), rhs(i), start=True, stop=True)
                m.then_inc(S["comb_done"], 1)

            pe.wait_ge(S["gt0_kept"], 1)
            pe.wait_ge(S["be2_loaded"], 16)
            for t, (t0, rows) in enumerate(TT):
                if t:
                    combine(t, lambda i, t0, rows: gateT[:, t0:t0 + rows], lambda i: be2[0:NE, 512 * i:512 * i + 512], t, rows)
                else:
                    for i in range(2):
                        m = pe.matmul(ps[6 + i][0:rows, :], gateT[:, t0:t0 + rows], be2[0:NE, 512 * i:512 * i + 512],
                                      start=True, stop=True)
                    m.then_inc(S["comb_done"], 1)
                if t == 0:
                    pe.wait_ge(S["tab_ready"], 1)
                    pe.transpose(ps[5][0:1, 0:P], tbc, ident[:, :]).then_inc(S["tab_turned"], 1)

            def rounds(b, t):
                combine(t, lambda i, t0, rows: gT[CAP * i:CAP * i + CAP, t0:t0 + rows],
                        lambda i: ysb[CAP * i:CAP * i + CAP, :], 3 * b + (3 + t), P)

            def gather(n):
                pe.wait_ge(S["sel_ready"], n + 1)
                for k in range(KD):
                    for t, (t0, rows) in enumerate(TT):
                        m = pe.matmul(ps[4][:, CAP * k:CAP * k + CAP], xnt[0:rows, t, k * P:(k + 1) * P],
                                      sel[0:rows, t, :], start=(t == 0), stop=(t == 2))
                m.then_inc(S["gathered"], 1)

            def turn_gates(b):
                pe.wait_ge(S["selg_ready"], b + 1)
                for t, (t0, rows) in enumerate(TT):
                    m = pe.transpose(ps[5][:, t0:t0 + rows], selg[0:rows, t, :], ident[0:rows, 0:rows])
                m.then_inc(S["gt_turned"], 1)

            def up(b, n, between):
                pe.wait_ge(S["xe_ready"], n + 1)
                pe.wait_ge(S["b1_filled"], 16 * b + 16)
                for gu in range(2):
                    for i in range(2):
                        m = pe.matmul(ps[gu][CAP * i:CAP * i + CAP, :], ones[0:1, 0:CAP],
                                      b1row[0:1, D * gu + 512 * i:D * gu + 512 * i + 512], start=True, stop=False)
                m.then_inc(S["b1_used"], 1)
                for k in range(W_SLOTS):
                    pe.wait_ge(filled[k], 16 * b + 16 * fills_before(MOE0 + k))
                    for gu in range(2):
                        for i in range(2):
                            m = pe.matmul(ps[gu][CAP * i:CAP * i + CAP, :], xeT[:, k, :],
                                          ring[:, k, D * gu + 512 * i:D * gu + 512 * i + 512],
                                          start=False, stop=(k == W_SLOTS - 1))
                    m.then_inc(S["freed"], 1)
                    between(k)

            def down(b):
                pe.wait_ge(S["h_ready"], b + 1)
                for j in range(4):
                    m = pe.transpose(ps[2][:, j * P:(j + 1) * P], hh[:, j * P:(j + 1) * P], ident[:, :])
                m.then_inc(S["h_turned"], 1)
                pe.wait_ge(S["hT_ready"], b + 1)
                for k in range(KD):
                    s = W_SLOTS + k // 2
                    if k % 2 == 0:
                        pe.wait_ge(filled[s], 16 * b + 16 * fills_before(MOE0 + s))
                    for i in range(2):
                        m = pe.matmul(ps[3][CAP * i:CAP * i + CAP, :], hTv[:, k % 4, CAP * (k // 4):CAP * (k // 4) + CAP],
                                      ring[:, s, D * (k % 2) + 512 * i:D * (k % 2) + 512 * i + 512],
                                      start=(k == 0), stop=(k == KD - 1))
                    if k % 2:
                        m.then_inc(S["freed"], 1)

            def block_b(b, first):
                def between(k):
                    if not first and k in (1, 3, 5):
                        if k == 1:
                            pe.wait_ge(S["y_ready"], b)
                            pe.wait_ge(S["gt_ready"], b)
                        rounds(b - 1, (k - 1) // 2)

                up(b, b, between)
                gather(b + 1)
                turn_gates(b)
                down(b)

            pe.wait_ge(S["xnt_kept"], 6)
            pe.wait_ge(S["tab_ready"], 2)
            pe.wait_ge(S["tail_zeroed"], 1)
            gather(0)
            block_b(0, True)
            with pe.Fori(1, NE) as b:
                block_b(b, False)
            pe.wait_ge(S["y_ready"], NE)
            pe.wait_ge(S["gt_ready"], NE)
            for t in range(3):
                rounds(NE - 1, t)
            pe.wait_ge(S["table_ready"], 1)
            n = pe.value_load(nblk[0:1, 0:1], min_val=0, max_val=P)
            with pe.If(n > 0):
                with pe.Fori(0, n) as j:
                    pe.wait_ge(S["xe_ready"], j + (NE + 1))
                    gather(j + (NE + 1))
                    up(j + NE, j + (NE + 1), lambda k: None)
                    turn_gates(j + NE)
                    down(j + NE)
                    pe.wait_ge(S["y_ready"], j + (NE + 1))
                    pe.wait_ge(S["gt_ready"], j + (NE + 1))
                    for t in range(3):
                        rounds(j + NE, t)


INPUTS = ["x_prompt", "x_sample", "state_lru_h", "cache_lru_conv", "cache_cf_conv", "cache_mem_k", "cache_mem_v",
          "mem_prompt", "g_mix", "w_in", "w_lru_conv", "b_lru_conv", "w_lru_a", "b_lru_a", "w_lru_x", "b_lru_x",
          "lru_lambda", "w_cf_conv", "b_cf_conv", "g_cf_ln", "b_cf_ln", "w_out", "g_xa", "g_mem", "w_q", "w_k", "w_v",
          "w_o", "g_moe", "w_router", "b_router", "w_e1", "b_e1", "w_e2", "b_e2", "g_final"]
OUTPUTS = [("y_prompt", (1, SEQ, D)), ("y_sample", (NB, 1, D)), ("lru_h_prompt", (1, 1, LRU)),
           ("lru_conv_prompt", (1, 1, LW - 1, LRU)), ("cf_conv_prompt", (1, 1, CW - 1, LRU)),
           ("mem_k", (1, 1, NMEM, H, HD)), ("mem_v", (1, 1, NMEM, H, HD)), ("lru_h_sample", (1, NB, LRU)),
           ("cache_lru", (1, NB, LW - 1, LRU)), ("cache_cf", (1, NB, CW - 1, LRU))]


def kernel(**inputs):
    import concourse.bacc as bacc
    from concourse.bass_utils import run_bass_kernel_spmd

    nc = bacc.Bacc("TRN2", target_bir_lowering=False, num_devices=1)
    arrays, a, outs = {}, {}, {}
    for name in INPUTS:
        x = np.ascontiguousarray(inputs[name])
        arrays["in_" + name] = x
        a[name] = nc.dram_tensor("in_" + name, x.shape, mybir.dt.from_np(x.dtype), kind="ExternalInput").ap()
    for name, shape in OUTPUTS:
        outs[name] = nc.dram_tensor("out_" + name, shape, F32, kind="ExternalOutput").ap()
    build(nc, a, outs)
    r = run_bass_kernel_spmd(nc, [arrays], core_ids=[0])
    return tuple(r.results[0]["out_" + name] for name, _ in OUTPUTS)
```

```python
import numpy as np
from contextlib import ExitStack

import concourse.bass as bass
import concourse.mybir as mybir

F32 = mybir.dt.float32
I32 = mybir.dt.int32
U32 = mybir.dt.uint32
ALU = mybir.AluOpType
ACT = mybir.ActivationFunctionType
AX = mybir.AxisListType

P = 128
D = 1024
KD = D // P
SEQ = 256
NB = 8
TOK = SEQ + NB
TT = [(0, P), (P, P), (2 * P, NB)]
LRU = 512
LC = LRU // P
HEAD = 64
CW = 31
LW = 4
NMEM = 256
H = 4
HD = D // H
NE = 32
CAP = 64
PASSES = -(-TOK // CAP)
NCOL = PASSES * NE
EPS = 1e-6
LIMIT = 7.0
ALPHA = 1.702
GELU_C = 0.7978845608028654
GELU_A = 0.044715
BIG = 4096.0

SLOT = 2048
RING = 12
W_SLOTS = 8
HEADROOM = 4
PAIRS = NE // 2

FRONT = [("in", 8), ("k", 4), ("out", 4), ("q", 4), ("v", 4), ("kc", 8), ("vc", 8), ("o", 4)]
START = {}
_n = HEADROOM
for _kind, _count in FRONT:
    START[_kind] = _n
    _n += _count
MOE0 = _n
assert MOE0 % RING == 0
KC_SLOTS = 8

IN_ORDER = [4, 5, 6, 7, 0, 1, 2, 3]

C_WCF = 0
C_B = CW * LC
C_WL, C_BLC, C_BA, C_BX, C_LAM, C_BCF, C_GLN, C_BLN = (C_B + 4 * i for i in (0, 4, 5, 6, 7, 8, 9, 10))
C_GMIX, C_GXA, C_GMEM, C_GMOE = (C_B + 44 + 8 * i for i in range(4))
B_ROWS = 76
C_H0 = C_B + B_ROWS
NPAR = C_H0 + LC * NB


def freed_after(n):
    if n < HEADROOM:
        return 2 * HEADROOM
    if n < 2 * HEADROOM:
        return n - HEADROOM + 1
    if n < START["kc"]:
        return n + 1
    return n + 1 - KC_SLOTS


def fills_before(n):
    return n // RING + 1 - (1 if n % RING < HEADROOM else 0)


def build(nc, a, outs):
    ctx = ExitStack()
    with ctx:
        def sb(name, shape, dt=F32):
            return ctx.enter_context(nc.sbuf_tensor(name, shape, dt))

        def sem(name):
            return ctx.enter_context(nc.semaphore(name))

        ring = sb("ring", [P, RING, SLOT])
        MIXW = 4 * (30 + TOK) + 4 * (3 + TOK) + 9 * LC * TOK
        mix = sb("mix", [P, MIXW])
        xT = sb("xT", [P, KD, TOK])
        xn = sb("xn", [P, KD, TOK])
        sq = sb("sq", [P, KD, TOK])
        tok = sb("tok", [P, 3, D])
        mn = sb("mn", [P, KD, NMEM])
        kT = sb("kT", [P, KD, NMEM])
        wgate = sb("wgate", [P, 2, LC, P])
        par = sb("par", [P, NPAR])
        ident = sb("ident", [P, P])
        ones = sb("ones", [P, P])
        before = sb("before", [P, P])
        wr = sb("wr", [P, KD, NE])
        brow = sb("brow", [1, NE])
        iota_s = sb("iota_s", [P, 2, CAP])
        iota_e = sb("iota_e", [P, NE])
        indc = sb("indc", [120, 4])
        indl = sb("indl", [24, NB])
        eps = sb("eps", [P, 1])
        small = sb("small", [P, 64])

        pos = [0]

        def part(width, shape=None, **kw):
            v = mix[:, pos[0]:pos[0] + width]
            pos[0] += width
            return v.rearrange(shape, **kw) if shape else v

        gpad = part(4 * (30 + TOK), "p (c t) -> p c t", c=LC)
        xpad = part(4 * (3 + TOK), "p (c t) -> p c t", c=LC)
        zg, za, th, gc, xc, tr, ti, av, uv = (part(LC * TOK, "p (c t) -> p c t", c=LC) for _ in range(9))
        hs = th
        assert pos[0] == MIXW
        stage_a = av.rearrange("p c t -> p (c t)")[:, 0:P]
        stage_b = tr.rearrange("p c t -> p (c t)")[:, 0:P]
        stage_h = uv.rearrange("p c t -> p (c t)")[0:NB, 0:LRU]
        rows_out = sq[:, 4:8, :].rearrange("p c t -> p (c t)")
        pos[0] = 0
        qT = part(KD * TOK, "p (c t) -> p c t", c=KD)
        oT = part(KD * TOK, "p (c t) -> p c t", c=KD)
        pm_at = pos[0]
        pm = part(H * 2 * NMEM, "p (h t m) -> p h t m", h=H, t=2)
        osb = mix[:, pm_at:pm_at + 2 * D].rearrange("p (g c) -> p g c", g=2)
        pT = part(H * 2 * SEQ, "p (h m t) -> p h m t", h=H, m=2)
        qrow = part(2 * D)
        sT = part(2 * NB * H, "p (m c) -> p m c", m=2)
        psS = part(2 * P)
        psT = part(2 * NB * H, "p (m c) -> p m c", m=2)
        pos[0] = 0
        xnt = part(3 * D, "p (t d) -> p t d", t=3)
        xeT = part(KD * 2 * CAP, "p (k s) -> p k s", k=KD)
        sel = part(3 * P, "p (t s) -> p t s", t=3)
        selg = part(3 * P, "p (t s) -> p t s", t=3)
        gT = part(3 * P)
        g1, u1, tg, hh, hT = (part(512) for _ in range(5))
        hTv = hT.rearrange("p (j s) -> p j s", j=4)
        ysb = part(D)
        b1row = part(2 * D)
        assert pos[0] <= MIXW
        sqf = sq[:, :, :].rearrange("p c t -> p (c t)")
        xnf = xn[:, :, :].rearrange("p c t -> p (c t)")
        be2, gfin = xnf[:, 0:D], xnf[:, D:2 * D]
        qb = xnf[:, 0:2 * D].rearrange("p (i c) -> p i c", i=2)
        qs = tok[:, 2, :]
        at = [0]

        def table(*shape):
            n = int(np.prod(shape))
            v = sqf[:, at[0]:at[0] + n]
            at[0] += n
            return v if len(shape) == 1 else v.rearrange("p (a c) -> p a c", a=shape[0])

        rkp, gcp = table(3, NCOL), table(3, NCOL)
        gcol, mask, lg, rk = (table(3, NE) for _ in range(4))
        iota_b = table(P)
        eq_at = at[0]
        eq = table(3 * 4 * NE).rearrange("p (t k e) -> p t k e", t=3, k=4)
        flag, scan, tb = (sqf[:, eq_at + P * i:eq_at + P * i + P] for i in range(3))
        tabrow = table(P)[0:1, :]
        count = table(NE)
        assert at[0] <= KD * TOK
        gateT = xT[:, 0, :][0:NE, :]
        tabi = sb("tabi", [1, 2, P], I32)
        nblk = sb("nblk", [1, 1], I32)

        kvtok = tok[:, 0:2, :]
        x0 = ring[:, 0:2, :].rearrange("p s c -> p (s c)")[:, 0:3 * D].rearrange("p (t d) -> p t d", t=3)
        wlrep = ring[0:24, 1, D:D + LRU]
        lcache = ring[0:24, 1, D + LRU:D + 2 * LRU]
        mem = ring[:, 2, :].rearrange("p (t d) -> p t d", t=2)
        ccache = ring[0:120, 3, 0:2 * LRU].rearrange("p (t c) -> p t c", t=2)
        wcrep = ring[0:120, 3, 2 * LRU:3 * LRU]

        small_at = [0]

        def tiny(n):
            v = small[:, small_at[0]:small_at[0] + n]
            small_at[0] += n
            return v

        rm = tiny(2)
        mss = tiny(2)
        spn, spp, sp_e, sp_z, sp_q, sp_t = (tiny(4) for _ in range(6))
        hba, hbx = tiny(4), tiny(4)
        mxn, rs, fss, frs = tiny(8), tiny(8), tiny(3), tiny(3)

        pick = sb("pick", [P, 2, H, 4])
        extra = sb("extra", [P, 96])
        m8 = extra[:, 0:24].rearrange("p (t k) -> p t k", t=3)
        ge = extra[:, 24:36].rearrange("p (t k) -> p t k", t=3)
        idf = extra[:, 36:60].rearrange("p (t k) -> p t k", t=3)
        smx, ssum = extra[:, 60:61], extra[:, 61:62]
        tbc = extra[:, 62:63]
        gsum, nv0, grec = extra[:, 63:66], extra[:, 66:69], extra[:, 69:72]
        nm8 = sb("idx8", [P, 3, 8], U32)
        rstd = sb("rstd", [P, TOK])

        ps = [ctx.enter_context(nc.psum_tensor(f"ps{i}", [P, 512], F32)) for i in range(8)]

        filled = [sem(f"filled{i}") for i in range(RING)]
        names = """x_loaded par_loaded h0_loaded mem_loaded cc_loaded lc_loaded gate_loaded wr_loaded
        br_loaded consts zeroed ident_ready pick_ready freed kc_freed
        x_turned x_copied x_squared sum_done sd_ready rstd_ready xn_ready par_turned par_ready
        mem_squared mem_sd mem_rec mem_scaled mem_turned mem_ready prods
        in_done in_kept glu_ready cf_tap cf_smp l_tap l_smp sp_chain sp_exp sp_ready
        kv_kept kt_turned kt_ready k_stored v_stored
        gate_done gate_tanh a_ready t_ready beta_chain u_ready scan_ready gelu_sq gelu_in gelu_th gelu_g ylru_ready
        rows_turned rows_kept rows_stored caches_shifted
        mu_done gc_cent gc_sq var_done ln_chain yn_ready y_th ycf_ready
        out_done res_added q_done q_kept score_done mx_ready p_exp p_scaled pt_turned pt_kept pv_done pv_kept
        qs_turned qs_kept qrow_loaded qb_ready s_turned smax_ready s_exp s_scaled sp_turned sp_kept spv_done osb_kept picked spv_kept
        o_done tm_turned tokr_kept xnt_kept logit_done lg_zeroed lg_ready idx_ready eq_ready gate_chain rank_chain block_chain nblk_ready v0_ready ge_ready mask_ready rank_done
        gt0_turned gt0_kept be2_loaded b2_done tab_turned tab_ready table_ready
        tail_zeroed sel_ready selg_ready gathered xe_ready gt_turned gt_ready g_clamped u_clamped t_done tu_done h_ready
        h_turned hT_ready y_ready comb_done acc_done b1_filled b1_used gfin_loaded
        fin_sq fin_sd fin_rec fin_ready y_stored""".split()
        S = {n: sem(n) for n in names}

        def slot(n):
            return ring[:, n % RING, :]

        def wait_tile(eng, kind, done, o):
            if o % 2:
                eng.wait_ge(S["freed"], freed_after(START[kind] + o // 2))
            else:
                eng.wait_ge(S[done], o // 2 + 1)

        def wslot(n):
            return slot(n).rearrange("p (k c) -> p k c", k=KD)

        CONSTS = 12
        n_par = 16 * 13
        block = ctx.enter_context(nc.Block())

        @block.sync
        def _(sp):
            sp.dma_start(x0[:, 0:2, :], a["x_prompt"][0].rearrange("(t p) d -> p t d", p=P)).then_inc(S["x_loaded"], 16)
            sp.dma_start(x0[0:NB, 2, :], a["x_sample"].rearrange("b t d -> (b t) d")).then_inc(S["x_loaded"], 16)
            sp.dma_start(mem, a["mem_prompt"][0].rearrange("(t p) d -> p t d", p=P)).then_inc(S["mem_loaded"], 16)

            def source(kind, i):
                if kind == "kc" or kind == "vc":
                    c = a["cache_mem_k" if kind == "kc" else "cache_mem_v"]
                    return c[0, i].rearrange("(t p) h d -> p t (h d)", p=P)
                w = a["w_" + kind][0]
                c = IN_ORDER[i] if kind == "in" else i
                return w[:, 256 * c:256 * c + 256].rearrange("(k p) c -> p k c", p=P)

            for kind, count in FRONT:
                for i in range(count):
                    n = START[kind] + i
                    if n >= RING:
                        m = n - RING
                        if START["kc"] <= m < START["vc"]:
                            sp.wait_ge(S["kc_freed"], m - START["kc"] + 1)
                        else:
                            sp.wait_ge(S["freed"], freed_after(m))
                    dst = slot(n).rearrange("p (t c) -> p t c", t=2) if kind in ("kc", "vc") else wslot(n)
                    sp.dma_start(dst, source(kind, i)).then_inc(filled[n % RING], 16)

            def expert(e, b):
                for s in range(RING):
                    sp.wait_ge(S["freed"], RING * b + (freed_after(MOE0 + s - RING)))
                    if s < W_SLOTS:
                        src = a["w_e1"][0][bass.ds(e, 1), s * P:(s + 1) * P, :].rearrange("o p c -> p (o c)")
                        dst = ring[:, s, :]
                    else:
                        j = s - W_SLOTS
                        src = a["w_e2"][0][bass.ds(e, 1), j * 2 * P:(j + 1) * 2 * P, :].rearrange(
                            "o (t p) c -> p (o t) c", p=P)
                        dst = ring[:, s, :].rearrange("p (t c) -> p t c", t=2)
                    sp.dma_start(dst, src).then_inc(filled[s], 16)

            def bias(e):
                sp.dma_start(b1row[0:1, :], a["b_e1"][0][bass.ds(e, 1), :]).then_inc(S["b1_filled"], 16)

            expert(0, 0)
            sp.wait_ge(S["freed"], freed_after(MOE0 - 1))
            bias(0)
            with sp.Fori(1, NE) as e:
                sp.wait_ge(S["b1_used"], e)
                bias(e)
                expert(e, e)
            sp.wait_ge(S["nblk_ready"], 1)
            n = sp.value_load(nblk[0:1, 0:1], min_val=0, max_val=P)
            with sp.If(n > 0):
                sp.wait_ge(S["table_ready"], 1)
                with sp.Fori(0, n) as j:
                    e = sp.value_load(tabi[0:1, 0, bass.ds(j, 1)], min_val=0, max_val=NE - 1)
                    sp.wait_ge(S["b1_used"], j + NE)
                    bias(e)
                    expert(e, j + NE)
            sp.wait_ge(S["fin_ready"], 3)
            sp.dma_start(outs["y_prompt"][0].rearrange("(t p) d -> p t d", p=P), tok[:, 0:2, :]).then_inc(S["y_stored"], 16)
            sp.dma_start(outs["y_sample"].rearrange("b t d -> (b t) d"), tok[0:NB, 2, :]).then_inc(S["y_stored"], 16)
            sp.wait_ge(S["y_stored"], 32)
            sp.wait_ge(S["k_stored"], 16)
            sp.wait_ge(S["v_stored"], 16)
            sp.wait_ge(S["rows_stored"], 16 * 6)
            sp.wait_ge(S["caches_shifted"], 32)

        @block.gpsimd
        def _(pool):
            pool.memset(ident[:, :], 0.0).then_inc(S["ident_ready"], 1)
            pool.memset(ones[:, :], 1.0).then_inc(S["consts"], 1)
            pool.wait_ge(S["ident_ready"], 1)
            pool.affine_select(out=ident[:, :], in_=ident[:, :], compare_op=ALU.not_equal, fill=1.0, base=0,
                               pattern=[[-1, P]], channel_multiplier=1).then_inc(S["ident_ready"], 1)
            pool.memset(eps[:, :], EPS).then_inc(S["consts"], 1)
            pool.memset(wgate[:, :, :, :], 0.0).then_inc(S["zeroed"], 1)
            pool.memset(gpad[:, :, 0:30], 0.0).then_inc(S["zeroed"], 1)
            pool.memset(xpad[:, :, 0:3], 0.0).then_inc(S["zeroed"], 1)
            pool.dma_start(ccache, a["cache_cf_conv"][0].rearrange("b w c -> (b w) c").rearrange(
                "(t r) c -> r t c", t=2)).then_inc(S["cc_loaded"], 16)
            for b in range(4):
                pool.dma_start(wcrep[30 * b:30 * b + 30, :], a["w_cf_conv"][0, 0:30, :]).then_inc(S["cc_loaded"], 16)
            pool.dma_start(lcache, a["cache_lru_conv"][0].rearrange("b w c -> (b w) c")).then_inc(S["lc_loaded"], 16)
            for b in range(NB):
                pool.dma_start(wlrep[3 * b:3 * b + 3, :], a["w_lru_conv"][0, 0:3, :]).then_inc(S["lc_loaded"], 16)
            pool.memset(before[:, :], 1.0).then_inc(S["consts"], 1)
            pool.memset(indc[:, :], 1.0).then_inc(S["consts"], 1)
            pool.memset(indl[:, :], 1.0).then_inc(S["consts"], 1)
            pool.memset(pick[:, :, :, :], 0.0).then_inc(S["pick_ready"], 1)
            pool.iota(iota_s[:, :, :], pattern=[[0, 2], [1, CAP]], base=0, channel_multiplier=0,
                      allow_small_or_imprecise_dtypes=True).then_inc(S["consts"], 1)
            pool.iota(iota_e[:, :], pattern=[[1, NE]], base=0, channel_multiplier=0,
                      allow_small_or_imprecise_dtypes=True).then_inc(S["consts"], 1)
            pool.wait_ge(S["consts"], 7)
            pool.affine_select(out=before[:, :], in_=before[:, :], compare_op=ALU.is_gt, fill=0.0, base=0,
                               pattern=[[1, P]], channel_multiplier=-1).then_inc(S["consts"], 1)
            for n, (ind, taps, width) in enumerate(((indc, CW - 1, 4), (indl, LW - 1, NB))):
                pool.affine_select(out=ind[:, :], in_=ind[:, :], compare_op=ALU.is_ge, fill=0.0, base=0,
                                   pattern=[[-taps, width]], channel_multiplier=1).then_inc(S["consts"], 1)
                pool.wait_ge(S["consts"], 9 + 2 * n)
                pool.affine_select(out=ind[:, :], in_=ind[:, :], compare_op=ALU.is_gt, fill=0.0, base=taps,
                                   pattern=[[taps, width]], channel_multiplier=-1).then_inc(S["consts"], 1)

            pool.wait_ge(S["pick_ready"], 1)
            pool.affine_select(out=pick[:, :, :, :], in_=pick[:, :, :, :], compare_op=ALU.not_equal, fill=1.0, base=0,
                               pattern=[[16, 2], [1, H], [36, 4]], channel_multiplier=-1).then_inc(S["pick_ready"], 1)
            for g, name in enumerate(("w_lru_a", "w_lru_x")):
                w = a[name][0].rearrange("(c two) i j -> two i c j", two=2)
                for half in range(2):
                    r = slice(HEAD * half, HEAD * half + HEAD)
                    pool.dma_start(wgate[r, g, :, r], w[half]).then_inc(S["gate_loaded"], 16)
            pool.dma_start(wr[:, :, :], a["w_router"][0].rearrange("(k p) e -> p k e", p=P)).then_inc(S["wr_loaded"], 16)
            pool.dma_start(brow[0:1, :], a["b_router"]).then_inc(S["br_loaded"], 16)
            pool.dma_start(outs["cache_lru"][0, :, 0:LW - 2, :], a["cache_lru_conv"][0, :, 1:LW - 1, :]).then_inc(S["caches_shifted"], 16)
            pool.dma_start(outs["cache_cf"][0, :, 0:CW - 2, :], a["cache_cf_conv"][0, :, 1:CW - 1, :]).then_inc(S["caches_shifted"], 16)
            pool.wait_ge(S["qrow_loaded"], 32)
            pool.wait_ge(S["pick_ready"], 2)
            pool.wait_ge(S["consts"], CONSTS)
            for b in range(NB):
                if b >= 2:
                    pool.wait_ge(S["kc_freed"], b - 1)
                r = 32 * (b % 4)
                pool.partition_broadcast(qb[:, b % 2, :], qrow[r:r + 1, D * (b // 4):D * (b // 4) + D], P).then_inc(S["qb_ready"], 1)
            pool.wait_ge(S["sum_done"], 3)
            pool.memset(lg, 0.0).then_inc(S["lg_zeroed"], 1)
            pool.wait_ge(S["xnt_kept"], 6)
            pool.memset(gT[:, TOK:3 * P], 0.0).then_inc(S["tail_zeroed"], 1)


        @block.scalar
        def _(act):
            act.dma_start(stage_a[0:CW * LC, :], a["w_cf_conv"][0].rearrange("w (t c) -> (w t) c", c=P)).then_inc(S["par_loaded"], 16)
            r = 0
            for name, rows in (("w_lru_conv", 16), ("b_lru_conv", 4), ("b_lru_a", 4), ("b_lru_x", 4), ("lru_lambda", 4),
                               ("b_cf_conv", 4), ("g_cf_ln", 4), ("b_cf_ln", 4), ("g_mix", 8), ("g_xa", 8),
                               ("g_mem", 8), ("g_moe", 8)):
                src = a[name]
                src = src[0].rearrange("w (t c) -> (w t) c", c=P) if rows == 16 else src.rearrange("o (t c) -> (o t) c", c=P)
                act.dma_start(stage_b[r:r + rows, :], src).then_inc(S["par_loaded"], 16)
                r += rows
            assert r == B_ROWS
            act.dma_start(stage_h, a["state_lru_h"][0]).then_inc(S["h0_loaded"], 16)
            for k in range(KD):
                act.wait_ge(S["x_copied"], k + 1)
                act.activation(sq[:, k, :], xT[:, k, :], ACT.Square).then_inc(S["x_squared"], 1)
            def root(n):
                act.wait_ge(S["sum_done"], n + 1)
                act.activation(rstd[:, :], ps[5][:, 0:TOK], ACT.Sqrt, bias=eps[:, 0:1], scale=1.0 / D).then_inc(S["sd_ready"], 1)

            act.wait_ge(S["consts"], 2)
            root(0)
            act.wait_ge(S["mem_loaded"], 16)
            for t in range(2):
                act.activation(xc.rearrange("p c t -> p (c t)")[:, 0:D], mem[:, t, :], ACT.Square,
                               accum_out=mss[:, t:t + 1]).then_inc(S["mem_squared"], 1)
                act.wait_ge(S["mem_squared"], t + 1)
            act.activation(rm, mss, ACT.Sqrt, bias=eps[:, 0:1], scale=1.0 / D).then_inc(S["mem_sd"], 1)
            act.wait_ge(S["par_ready"], 2)
            act.activation(sp_e, spn, ACT.Exp).then_inc(S["sp_exp"], 1)
            act.wait_ge(S["zeroed"], 3)
            for o in range(16):
                if o != 8:
                    wait_tile(act, "in", "in_done", o)
                src, c = ps[o % 4][:, 0:TOK], o % 4
                if o == 8:
                    for j in range(4):
                        act.wait_ge(S["mem_turned"], j + 1)
                        for i in range(2):
                            k = 2 * j + i
                            act.activation(mn[:, k, :], ps[6 + j % 2][:, NMEM * i:NMEM * i + NMEM], ACT.Copy,
                                           scale=par[:, C_GMEM + k:C_GMEM + k + 1]).then_inc(S["mem_ready"], 1)
                    wait_tile(act, "in", "in_done", o)
                if o < 4:
                    act.activation(za[:, c, :], src, ACT.Copy, scale=0.5).then_inc(S["in_kept"], 1)
                elif o < 8:
                    act.activation(th[:, c, :], src, ACT.Tanh, scale=0.5).then_inc(S["in_kept"], 1)
                elif o < 12:
                    act.activation(xpad[:, c, 3:3 + TOK], src, ACT.Copy).then_inc(S["in_kept"], 1)
                else:
                    act.activation(zg[:, c, :], src, ACT.Copy).then_inc(S["in_kept"], 1)

            def keep_kv(j, dst):
                act.wait_ge(S["freed"], freed_after(START["k"] + j if j < 4 else START["v"] + j - 4))
                c = 256 * (j % 4)
                act.activation(dst[:, :, c:c + 256], ps[6 + j % 2][:, :].rearrange("p (t c) -> p t c", t=2),
                               ACT.Copy).then_inc(S["kv_kept"], 1)

            for j in range(4):
                keep_kv(j, kvtok)
            act.wait_ge(S["kv_kept"], 4)
            act.dma_start(outs["mem_k"][0, 0].rearrange("(t p) h d -> p t (h d)", p=P), kvtok).then_inc(S["k_stored"], 16)
            act.wait_ge(S["in_kept"], 16)
            act.activation(uv, zg, ACT.Square).then_inc(S["gelu_sq"], 1)
            act.wait_ge(S["gelu_in"], 2)
            act.activation(uv, uv, ACT.Tanh, scale=GELU_C).then_inc(S["gelu_th"], 1)
            for j in range(4):
                act.wait_ge(S["kt_turned"], j + 1)
                act.activation(kT[:, 2 * j:2 * j + 2, :], ps[6 + j % 2][:, :].rearrange("p (t c) -> p t c", t=2),
                               ACT.Copy).then_inc(S["kt_ready"], 1)
            act.wait_ge(S["sp_ready"], 1)
            for g, (dst, hb) in enumerate(((tr, hba), (ti, hbx))):
                for c in range(LC):
                    act.wait_ge(S["gate_done"], 4 * g + c + 1)
                    act.activation(dst[:, c, :], ps[c][:, 0:TOK], ACT.Tanh, bias=hb[:, c:c + 1],
                                   scale=0.5).then_inc(S["gate_tanh"], 1)
            act.wait_ge(S["gate_tanh"], 4)
            for c in range(LC):
                act.activation(av[:, c, :], tr[:, c, :], ACT.Exp, bias=spn[:, c:c + 1],
                               scale=spn[:, c:c + 1]).then_inc(S["a_ready"], 1)
            act.wait_ge(S["a_ready"], 4)
            for c in range(LC):
                act.activation(tr[:, c, :], tr[:, c, :], ACT.Tanh, bias=spp[:, c:c + 1],
                               scale=spp[:, c:c + 1]).then_inc(S["t_ready"], 1)
            act.wait_ge(S["beta_chain"], 3)
            act.activation(tr, tr, ACT.Sqrt).then_inc(S["t_ready"], 1)
            act.wait_ge(S["gc_cent"], 1)
            act.activation(gc, za, ACT.Square).then_inc(S["gc_sq"], 1)
            act.wait_ge(S["var_done"], 1)
            act.activation(rstd[:, :], ps[5][:, 0:TOK], ACT.Sqrt, bias=eps[:, 0:1], scale=1.0 / LRU).then_inc(S["ln_chain"], 1)
            act.wait_ge(S["yn_ready"], 1)
            act.activation(gc, za, ACT.Tanh, scale=0.5).then_inc(S["y_th"], 1)
            act.wait_ge(S["rows_kept"], 3)
            z3, g3, h3 = rows_out[0:11, 0:512], rows_out[0:38, 512:1024], tok[0:9, 2, 0:512]
            for dst, src in ((outs["lru_conv_prompt"][0, 0], z3[0:3, :]), (outs["cache_lru"][0, :, LW - 2, :], z3[3:11, :]),
                             (outs["cf_conv_prompt"][0, 0], g3[0:30, :]), (outs["cache_cf"][0, :, CW - 2, :], g3[30:38, :]),
                             (outs["lru_h_prompt"][0], h3[0:1, :]), (outs["lru_h_sample"][0], h3[1:9, :])):
                act.dma_start(dst, src).then_inc(S["rows_stored"], 16)
            act.wait_ge(S["rows_stored"], 16 * 6)
            for k in range(KD):
                act.wait_ge(S["res_added"], k + 1)
                act.activation(sq[:, k, :], xT[:, k, :], ACT.Square).then_inc(S["x_squared"], 1)
            root(1)
            for o in range(KD):
                wait_tile(act, "q", "q_done", o)
                act.activation(qT[:, o, :], ps[o % 4][:, 0:TOK], ACT.Copy, scale=HD ** -0.5).then_inc(S["q_kept"], 1)
            for i in range(2):
                act.wait_ge(S["qs_turned"], i + 1)
                act.activation(qs[0:NB, 512 * i:512 * i + 512], ps[6 + i][0:NB, :], ACT.Copy).then_inc(S["qs_kept"], 1)
            act.wait_ge(S["qs_kept"], 2)
            for g in range(2):
                act.dma_start(qrow[0:97:32, D * g:D * g + D], qs[4 * g:4 * g + 4, :]).then_inc(S["qrow_loaded"], 16)
            for h in range(H):
                act.wait_ge(S["mx_ready"], h + 1)
                for t in range(2):
                    act.activation(pm[:, h, t, :], ps[h][:, NMEM * t:NMEM * t + NMEM], ACT.Exp,
                                   bias=mxn[:, 2 * h + t:2 * h + t + 1],
                                   accum_out=rs[:, 2 * h + t:2 * h + t + 1]).then_inc(S["p_exp"], 1)
            act.wait_ge(S["k_stored"], 16)
            for j in range(4):
                keep_kv(4 + j, kvtok)
            act.wait_ge(S["kv_kept"], 8)
            act.dma_start(outs["mem_v"][0, 0].rearrange("(t p) h d -> p t (h d)", p=P), kvtok).then_inc(S["v_stored"], 16)
            for h in range(H):
                act.wait_ge(S["pt_turned"], h + 1)
                act.activation(pT[:, h, :, :], ps[6 + h % 2][:, :].rearrange("p (m t) -> p m t", m=2), ACT.Copy).then_inc(S["pt_kept"], 1)
            for h in range(H):
                act.wait_ge(S["pv_done"], h + 1)
                act.activation(oT[:, 2 * h:2 * h + 2, 0:SEQ], ps[h][:, :].rearrange("p (m t) -> p m t", m=2), ACT.Copy).then_inc(S["pv_kept"], 1)
            act.wait_ge(S["smax_ready"], 1)
            act.activation(psS[0:32, :], ps[6][0:32, 0:256], ACT.Exp, bias=smx[0:32, :], accum_out=ssum[0:32, :]).then_inc(S["s_exp"], 1)
            act.wait_ge(S["sp_turned"], 1)
            act.activation(psT, ps[7][:, 0:64].rearrange("p (m c) -> p m c", m=2), ACT.Copy).then_inc(S["sp_kept"], 1)
            for i in range(2):
                act.wait_ge(S["spv_done"], 1)
                act.activation(osb[:, 0, 512 * i:512 * i + 512], ps[4 + i][:, :], ACT.Copy).then_inc(S["osb_kept"], 1)
            act.wait_ge(S["picked"], 1)
            act.activation(oT[:, :, SEQ:TOK], ps[0][:, 0:64].rearrange("p (c b) -> p c b", b=NB), ACT.Copy).then_inc(S["spv_kept"], 1)
            for k in range(KD):
                act.wait_ge(S["res_added"], KD + k + 1)
                act.activation(sq[:, k, :], xT[:, k, :], ACT.Square).then_inc(S["x_squared"], 1)
            root(2)
            act.wait_ge(S["v0_ready"], 1)
            for t in range(3):
                act.activation(ge[:, t, :], m8[:, t, 0:4], ACT.Exp, bias=nv0[:, t:t + 1],
                               accum_out=gsum[:, t:t + 1]).then_inc(S["ge_ready"], 1)
            for t, (t0, rows) in enumerate(TT):
                for i in range(2):
                    j = 6 + 2 * t + i
                    act.wait_ge(S["tm_turned"], j + 1)
                    act.activation(xnt[0:rows, t, 512 * i:512 * i + 512], ps[j % 4][0:rows, :], ACT.Copy).then_inc(S["xnt_kept"], 1)
            act.dma_start(be2[0:NE, :], a["b_e2"][0]).then_inc(S["be2_loaded"], 16)
            act.dma_start(gfin, a["g_final"].partition_broadcast(P)).then_inc(S["gfin_loaded"], 16)
            act.wait_ge(S["gt0_turned"], 1)
            act.activation(gateT, ps[4][0:NE, 0:TOK], ACT.Copy).then_inc(S["gt0_kept"], 1)

            def keep_gathered(q):
                act.wait_ge(S["gathered"], q + 1)
                for i in range(2):
                    m = act.activation(xeT[:, 4 * i:4 * i + 4, :], ps[4 + i][:, :].rearrange("p (k s) -> p k s", k=4), ACT.Copy)
                m.then_inc(S["xe_ready"], 1)

            def keep_gates(q):
                act.wait_ge(S["gt_turned"], q + 1)
                act.activation(gT[:, 0:TOK], ps[2][:, 0:TOK], ACT.Copy).then_inc(S["gt_ready"], 1)

            def half_swish(b):
                act.wait_ge(S["g_clamped"], b + 1)
                act.activation(tg, g1, ACT.Tanh, scale=ALPHA / 2).then_inc(S["t_done"], 1)

            def keep_h(b):
                act.wait_ge(S["h_turned"], b + 1)
                act.activation(hT, ps[2][:, :], ACT.Copy, scale=0.5).then_inc(S["hT_ready"], 1)

            def keep_y(b, e2):
                act.wait_ge(S["freed"], RING * b + (freed_after(MOE0 - 1) + RING))
                for i in range(2):
                    m = act.activation(ysb[CAP * e2:CAP * e2 + CAP, 512 * i:512 * i + 512],
                                       ps[3][CAP * i:CAP * i + CAP, :], ACT.Copy)
                m.then_inc(S["y_ready"], 1)

            keep_gathered(0)
            with act.Fori(0, PAIRS) as q:
                half_swish(2 * q)
                keep_h(2 * q)
                keep_y(2 * q, 0)
                keep_gates(q)
                half_swish(2 * q + 1)
                keep_gathered(q + 1)
                keep_h(2 * q + 1)
                keep_y(2 * q + 1, 1)
            act.wait_ge(S["nblk_ready"], 1)
            n = act.value_load(nblk[0:1, 0:1], min_val=0, max_val=P)
            with act.If(n > 0):
                act.wait_ge(S["tab_turned"], 1)
                act.activation(tabrow, ps[5][0:1, 0:P], ACT.Copy).then_inc(S["tab_ready"], 1)
                with act.Fori(0, n) as j:
                    keep_gathered(j + (PAIRS + 1))
                    half_swish(j + NE)
                    keep_gates(j + PAIRS)
                    keep_h(j + NE)
                    keep_y(j + NE, 0)
            act.wait_ge(S["fin_sq"], 3)
            act.activation(frs, fss, ACT.Sqrt, bias=eps[:, 0:1], scale=1.0 / D).then_inc(S["fin_sd"], 1)

        @block.vector
        def _(dve):
            for k in range(KD):
                dve.wait_ge(S["x_turned"], k + 1)
                dve.tensor_copy(xT[:, k, :], ps[k % 4][:, 0:TOK]).then_inc(S["x_copied"], 1)
            dve.wait_ge(S["par_turned"], 1)
            dve.tensor_copy(par[:, :], ps[4][:, 0:NPAR]).then_inc(S["par_ready"], 1)
            dve.wait_ge(S["par_ready"], 1)
            lam = par[:, C_LAM:C_LAM + 4]
            dve.tensor_scalar(sp_t, lam, -1.0, None, ALU.mult).then_inc(S["sp_chain"], 1)
            dve.tensor_scalar(hba, par[:, C_BA:C_BA + 4], 0.5, None, ALU.mult).then_inc(S["sp_chain"], 1)
            dve.tensor_scalar(hbx, par[:, C_BX:C_BX + 4], 0.5, None, ALU.mult).then_inc(S["sp_chain"], 1)
            dve.wait_ge(S["sp_chain"], 3)
            dve.tensor_tensor(spn, lam, sp_t, ALU.min).then_inc(S["par_ready"], 1)

            def norm(n, gain):
                dve.wait_ge(S["sd_ready"], n + 1)
                dve.reciprocal(rstd[:, :], rstd[:, :]).then_inc(S["rstd_ready"], 1)
                dve.wait_ge(S["rstd_ready"], n + 1)
                for k in range(KD):
                    dve.scalar_tensor_tensor(out=xn[:, k, :], in0=xT[:, k, :], scalar=par[:, gain + k:gain + k + 1],
                                             in1=rstd[:, :], op0=ALU.mult, op1=ALU.mult).then_inc(S["xn_ready"], 1)

            dve.wait_ge(S["x_copied"], KD)
            norm(0, C_GMIX)
            dve.wait_ge(S["mem_sd"], 1)
            dve.reciprocal(rm, rm).then_inc(S["mem_rec"], 1)
            dve.wait_ge(S["mem_rec"], 1)
            for t in range(2):
                dve.tensor_scalar(mem[:, t, :], mem[:, t, :], rm[:, t:t + 1], None, ALU.mult).then_inc(S["mem_scaled"], 1)
            dve.wait_ge(S["cc_loaded"], 16 * 5)
            dve.wait_ge(S["lc_loaded"], 16 * 9)
            for t in range(2):
                dve.tensor_tensor(ccache[:, t, :], ccache[:, t, :], wcrep, ALU.mult).then_inc(S["prods"], 1)
            dve.tensor_tensor(lcache, lcache, wlrep, ALU.mult).then_inc(S["prods"], 1)
            n_sp = [3]

            def sp_step(ins):
                n_sp[0] += 1
                ins.then_inc(S["sp_chain"], 1)
                dve.wait_ge(S["sp_chain"], n_sp[0])

            dve.wait_ge(S["sp_exp"], 1)
            sp_step(dve.tensor_scalar(sp_q, sp_e, 2.0, None, ALU.add))
            sp_step(dve.reciprocal(sp_q, sp_q))
            sp_step(dve.tensor_tensor(sp_z, sp_e, sp_q, ALU.mult))
            sp_step(dve.tensor_tensor(sp_e, sp_z, sp_z, ALU.mult))
            sp_step(dve.tensor_scalar(sp_q, sp_e, 1.0 / 15, None, ALU.mult))
            for odd in (13, 11, 9, 7, 5, 3):
                sp_step(dve.scalar_tensor_tensor(out=sp_q, in0=sp_q, scalar=1.0 / odd, in1=sp_e, op0=ALU.add, op1=ALU.mult))
            sp_step(dve.scalar_tensor_tensor(out=sp_q, in0=sp_q, scalar=1.0, in1=sp_z, op0=ALU.add, op1=ALU.mult))
            sp_step(dve.tensor_scalar(sp_t, sp_t, 0.0, None, ALU.max))
            sp_step(dve.scalar_tensor_tensor(out=sp_q, in0=sp_q, scalar=2.0, in1=sp_t, op0=ALU.mult, op1=ALU.add))
            dve.tensor_scalar(spn, sp_q, -4.0, None, ALU.mult).then_inc(S["sp_chain"], 1)
            dve.wait_ge(S["sp_chain"], n_sp[0] + 1)
            dve.tensor_scalar(spp, sp_q, 4.0, None, ALU.mult).then_inc(S["sp_ready"], 1)

            dve.wait_ge(S["zeroed"], 3)
            for c in range(LC):
                dve.wait_ge(S["in_kept"], 5 + c)
                dve.scalar_tensor_tensor(out=gpad[:, c, 30:30 + TOK], in0=th[:, c, :], scalar=1.0, in1=za[:, c, :],
                                         op0=ALU.add, op1=ALU.mult).then_inc(S["glu_ready"], 1)
            dve.wait_ge(S["glu_ready"], 4)
            for c in range(LC):
                dve.tensor_scalar(gc[:, c, 0:SEQ], gpad[:, c, 0:SEQ], par[:, C_WCF + c:C_WCF + c + 1],
                                  par[:, C_BCF + c:C_BCF + c + 1], ALU.mult, ALU.add).then_inc(S["cf_tap"], 1)
            with dve.Fori(1, CW) as w:
                for c in range(LC):
                    dve.wait_ge(S["cf_tap"], 4 * w + (c - 3))
                    dve.scalar_tensor_tensor(out=gc[:, c, 0:SEQ], in0=gpad[:, c, bass.ds(w, SEQ)],
                                             scalar=par[:, bass.ds(4 * w + (C_WCF + c), 1)], in1=gc[:, c, 0:SEQ],
                                             op0=ALU.mult, op1=ALU.add).then_inc(S["cf_tap"], 1)
            dve.wait_ge(S["in_kept"], 12)
            for w in range(LW):
                for c in range(LC):
                    src, tap = xpad[:, c, w:w + SEQ], par[:, C_WL + 4 * w + c:C_WL + 4 * w + c + 1]
                    if w == 0:
                        dve.tensor_scalar(xc[:, c, 0:SEQ], src, tap, par[:, C_BLC + c:C_BLC + c + 1],
                                          ALU.mult, ALU.add).then_inc(S["l_tap"], 1)
                        continue
                    dve.wait_ge(S["l_tap"], 4 * w + c - 3)
                    dve.scalar_tensor_tensor(out=xc[:, c, 0:SEQ], in0=src, scalar=tap, in1=xc[:, c, 0:SEQ],
                                             op0=ALU.mult, op1=ALU.add).then_inc(S["l_tap"], 1)
            for c in range(LC):
                dve.tensor_scalar(xc[:, c, SEQ:TOK], xpad[:, c, 3 + SEQ:3 + TOK], par[:, C_WL + 12 + c:C_WL + 13 + c],
                                  par[:, C_BLC + c:C_BLC + c + 1], ALU.mult, ALU.add).then_inc(S["l_smp"], 1)
                dve.tensor_scalar(gc[:, c, SEQ:TOK], gpad[:, c, 30 + SEQ:30 + TOK],
                                  par[:, C_WCF + 120 + c:C_WCF + 121 + c],
                                  par[:, C_BCF + c:C_BCF + c + 1], ALU.mult, ALU.add).then_inc(S["l_smp"], 1)
            dve.wait_ge(S["l_smp"], 8)
            dve.wait_ge(S["freed"], freed_after(0))
            dve.tensor_tensor(xc[:, :, SEQ:TOK], xc[:, :, SEQ:TOK],
                              ps[4][:, 32:64].rearrange("p (c b) -> p c b", b=NB), ALU.add).then_inc(S["l_smp"], 1)
            dve.tensor_tensor(gc[:, :, SEQ:TOK], gc[:, :, SEQ:TOK],
                              ps[4][:, 0:32].rearrange("p (c b) -> p c b", b=NB), ALU.add).then_inc(S["cf_smp"], 1)
            dve.wait_ge(S["gelu_sq"], 1)
            dve.tensor_scalar(uv, uv, GELU_A, 1.0, ALU.mult, ALU.add).then_inc(S["gelu_in"], 1)
            dve.wait_ge(S["gelu_in"], 1)
            dve.tensor_tensor(uv, uv, zg, ALU.mult).then_inc(S["gelu_in"], 1)
            dve.wait_ge(S["gelu_th"], 1)
            dve.scalar_tensor_tensor(out=zg, in0=uv, scalar=1.0, in1=zg, op0=ALU.add, op1=ALU.mult).then_inc(S["gelu_g"], 1)
            dve.wait_ge(S["mu_done"], 1)
            dve.scalar_tensor_tensor(out=za, in0=ps[5][:, 0:TOK].unsqueeze(1).to_broadcast([P, LC, TOK]),
                                     scalar=-1.0 / LRU, in1=gc, op0=ALU.mult, op1=ALU.add).then_inc(S["gc_cent"], 1)
            dve.wait_ge(S["gate_tanh"], 8)
            dve.wait_ge(S["gelu_g"], 1)
            dve.wait_ge(S["a_ready"], 4)
            dve.scalar_tensor_tensor(out=ti, in0=ti, scalar=1.0, in1=xc, op0=ALU.add, op1=ALU.mult).then_inc(S["beta_chain"], 1)
            dve.tensor_tensor(uv, av, av, ALU.mult).then_inc(S["beta_chain"], 1)
            dve.wait_ge(S["beta_chain"], 2)
            dve.wait_ge(S["t_ready"], 4)
            dve.scalar_tensor_tensor(out=tr, in0=uv, scalar=1.0, in1=tr, op0=ALU.add, op1=ALU.mult).then_inc(S["beta_chain"], 1)
            dve.wait_ge(S["t_ready"], 5)
            dve.scalar_tensor_tensor(out=uv, in0=tr, scalar=0.5, in1=ti, op0=ALU.mult, op1=ALU.mult).then_inc(S["u_ready"], 1)
            dve.wait_ge(S["u_ready"], 1)
            for c in range(LC):
                dve.tensor_tensor_scan(hs[:, c, 0:SEQ], av[:, c, 0:SEQ], uv[:, c, 0:SEQ], 0.0,
                                       ALU.mult, ALU.add).then_inc(S["scan_ready"], 1)
            dve.tensor_tensor(hs[:, :, SEQ:TOK], av[:, :, SEQ:TOK],
                              par[:, C_H0:C_H0 + 32].rearrange("p (c b) -> p c b", b=NB), ALU.mult).then_inc(S["scan_ready"], 1)
            dve.wait_ge(S["scan_ready"], 5)
            dve.tensor_tensor(hs[:, :, SEQ:TOK], hs[:, :, SEQ:TOK], uv[:, :, SEQ:TOK], ALU.add).then_inc(S["scan_ready"], 1)
            dve.wait_ge(S["scan_ready"], 6)
            dve.scalar_tensor_tensor(out=zg, in0=zg, scalar=0.5, in1=hs, op0=ALU.mult, op1=ALU.mult).then_inc(S["ylru_ready"], 1)
            dve.wait_ge(S["ln_chain"], 1)
            dve.reciprocal(rstd[:, :], rstd[:, :]).then_inc(S["ln_chain"], 1)
            dve.wait_ge(S["ln_chain"], 2)
            dve.tensor_tensor(za, za, rstd[:, :].unsqueeze(1).to_broadcast([P, LC, TOK]), ALU.mult).then_inc(S["ln_chain"], 1)
            dve.wait_ge(S["ln_chain"], 3)
            for c in range(LC):
                last = dve.tensor_scalar(za[:, c, :], za[:, c, :], par[:, C_GLN + c:C_GLN + c + 1],
                                         par[:, C_BLN + c:C_BLN + c + 1], ALU.mult, ALU.add)
            last.then_inc(S["yn_ready"], 1)
            dve.wait_ge(S["y_th"], 1)
            dve.tensor_scalar(gc, gc, 1.0, 0.5, ALU.add, ALU.mult).then_inc(S["ln_chain"], 1)
            dve.wait_ge(S["ln_chain"], 4)
            dve.tensor_tensor(gc, gc, za, ALU.mult).then_inc(S["ycf_ready"], 1)
            dve.wait_ge(S["rows_turned"], 1)
            dve.tensor_copy(rows_out[0:11, 0:512], ps[6][0:11, :]).then_inc(S["rows_kept"], 1)
            dve.wait_ge(S["rows_turned"], 2)
            dve.tensor_copy(rows_out[0:38, 512:1024], ps[7][0:38, :]).then_inc(S["rows_kept"], 1)
            dve.wait_ge(S["rows_turned"], 3)
            dve.tensor_copy(tok[0:9, 2, 0:512], ps[4][0:9, :]).then_inc(S["rows_kept"], 1)

            def residual(kind, done, base):
                for o in range(KD):
                    wait_tile(dve, kind, done, o)
                    dve.tensor_tensor(xT[:, o, :], xT[:, o, :], ps[o % 4][:, 0:TOK], ALU.add).then_inc(S["res_added"], 1)
                dve.wait_ge(S["res_added"], base + KD)

            residual("out", "out_done", 0)
            norm(1, C_GXA)
            for h in range(H):
                dve.wait_ge(S["score_done"], h + 1)
                dve.tensor_reduce(mxn[:, 2 * h:2 * h + 2], ps[h][:, :].rearrange("p (t m) -> p t m", t=2), AX.X,
                                  ALU.max, negate=True).then_inc(S["mx_ready"], 1)
            n_rec = 0
            for h in range(H):
                dve.wait_ge(S["p_exp"], 2 * h + 2)
                dve.reciprocal(rs[:, 2 * h:2 * h + 2], rs[:, 2 * h:2 * h + 2]).then_inc(S["mx_ready"], 1)
                dve.wait_ge(S["mx_ready"], H + h + 1)
                for t in range(2):
                    last = dve.tensor_scalar(pm[:, h, t, :], pm[:, h, t, :], rs[:, 2 * h + t:2 * h + t + 1], None, ALU.mult)
                last.then_inc(S["p_scaled"], 1)
            for b in range(NB):
                n = START["kc"] + b
                dve.wait_ge(filled[n % RING], 16 * fills_before(n))
                dve.wait_ge(S["qb_ready"], b + 1)
                key = slot(n).rearrange("p (t h d) -> p t h d", t=2, h=H)
                for t in range(2):
                    for h in range(H):
                        q = qb[:, b % 2, HD * h:HD * h + HD]
                        last = dve.tensor_tensor_reduce(key[:, t, h, :], key[:, t, h, :], q, 1.0, 0.0, ALU.mult, ALU.add,
                                                        sT[:, t, 4 * b + h:4 * b + h + 1])
                last.then_inc(S["kc_freed"], 1)
            dve.wait_ge(S["s_turned"], 1)
            dve.tensor_reduce(smx[0:32, :], ps[6][0:32, 0:256], AX.X, ALU.max, negate=True).then_inc(S["smax_ready"], 1)
            dve.wait_ge(S["s_exp"], 1)
            dve.reciprocal(ssum[0:32, :], ssum[0:32, :]).then_inc(S["s_scaled"], 1)
            dve.wait_ge(S["s_scaled"], 1)
            dve.tensor_scalar(psS[0:32, :], psS[0:32, :], ssum[0:32, :], None, ALU.mult).then_inc(S["s_scaled"], 1)
            dve.wait_ge(S["spv_done"], 2)
            for i in range(2):
                dve.tensor_copy(osb[:, 1, 512 * i:512 * i + 512], ps[6 + i][:, :]).then_inc(S["osb_kept"], 1)
            residual("o", "o_done", KD)
            norm(2, C_GMOE)
            dve.wait_ge(S["v_stored"], 16)
            dve.wait_ge(S["rows_stored"], 16 * 6)
            for t, (t0, rows) in enumerate(TT):
                for i in range(2):
                    j = 2 * t + i
                    dve.wait_ge(S["tm_turned"], j + 1)
                    dve.tensor_copy(tok[0:rows, t, 512 * i:512 * i + 512], ps[j % 4][0:rows, :]).then_inc(S["tokr_kept"], 1)
            dve.wait_ge(S["lg_zeroed"], 1)
            dve.wait_ge(S["logit_done"], 1)
            dve.tensor_copy(lg[:, 0:2, :], ps[4][:, 0:2 * NE].rearrange("p (t e) -> p t e", t=2)).then_inc(S["lg_ready"], 1)
            dve.tensor_copy(lg[0:NB, 2, :], ps[4][0:NB, 2 * NE:3 * NE]).then_inc(S["lg_ready"], 1)
            dve.wait_ge(S["lg_ready"], 2)
            for t in range(3):
                dve.max(m8[:, t, :], lg[:, t, :]).then_inc(S["lg_ready"], 1)
            dve.wait_ge(S["lg_ready"], 5)
            dve.tensor_scalar(nv0, m8[:, :, 0], -1.0, None, ALU.mult).then_inc(S["v0_ready"], 1)
            for t in range(3):
                dve.max_index(nm8[:, t, :], m8[:, t, :], lg[:, t, :]).then_inc(S["idx_ready"], 1)
            dve.wait_ge(S["idx_ready"], 3)
            dve.tensor_copy(idf, nm8[:, :, :]).then_inc(S["idx_ready"], 1)
            dve.wait_ge(S["idx_ready"], 4)
            wide = [P, 3, 4, NE]
            dve.tensor_tensor(eq, iota_e[:, :].unsqueeze(1).unsqueeze(1).to_broadcast(wide),
                              idf[:, :, 0:4].unsqueeze(3).to_broadcast(wide), ALU.is_equal).then_inc(S["eq_ready"], 1)
            dve.wait_ge(S["eq_ready"], 1)
            dve.tensor_reduce(mask, eq.rearrange("p t k e -> p t e k"), AX.X, ALU.add).then_inc(S["mask_ready"], 1)
            dve.wait_ge(S["ge_ready"], 3)
            dve.reciprocal(grec, gsum).then_inc(S["gate_chain"], 1)
            dve.wait_ge(S["gate_chain"], 1)
            dve.tensor_tensor(ge, ge, grec.unsqueeze(2).to_broadcast([P, 3, 4]), ALU.mult).then_inc(S["gate_chain"], 1)
            dve.wait_ge(S["gate_chain"], 2)
            dve.tensor_tensor(eq, eq, ge.unsqueeze(3).to_broadcast(wide), ALU.mult).then_inc(S["gate_chain"], 1)
            dve.wait_ge(S["gate_chain"], 3)
            dve.tensor_reduce(gcol, eq.rearrange("p t k e -> p t e k"), AX.X, ALU.add).then_inc(S["gate_chain"], 1)
            dve.wait_ge(S["mask_ready"], 1)
            dve.tensor_scalar(rk, mask, -BIG, BIG, ALU.mult, ALU.add).then_inc(S["rank_chain"], 1)
            dve.wait_ge(S["rank_chain"], 1)
            dve.wait_ge(S["rank_done"], 1)
            dve.tensor_tensor(rkp[:, 0:2, 0:NE], rk[:, 0:2, :], ps[5][:, 0:2 * NE].rearrange("p (t e) -> p t e", t=2),
                              ALU.add).then_inc(S["rank_chain"], 1)
            dve.tensor_tensor(rkp[0:NB, 2, 0:NE], rk[0:NB, 2, :], ps[5][0:NB, 2 * NE:3 * NE], ALU.add).then_inc(S["rank_chain"], 1)
            dve.tensor_copy(count, ps[5][:, 96:128]).then_inc(S["rank_chain"], 1)
            dve.wait_ge(S["rank_chain"], 4)
            dve.wait_ge(S["gate_chain"], 4)

            def one_hot(cols):
                for t, (t0, rows) in enumerate(TT):
                    for i, col in enumerate(cols):
                        last = dve.tensor_scalar(sel[0:rows, t, CAP * i:CAP * i + CAP], iota_s[0:rows, 0, :],
                                                 rkp[0:rows, t, bass.ds(col, 1)], None, ALU.is_equal)
                last.then_inc(S["sel_ready"], 1)

            one_hot((0, 1))
            for q in range(1, PASSES):
                dve.tensor_scalar(rkp[:, 0:2, NE * q:NE * q + NE], rkp[:, 0:2, 0:NE], -float(CAP * q), None, ALU.add)
                dve.tensor_scalar(rkp[0:NB, 2, NE * q:NE * q + NE], rkp[0:NB, 2, 0:NE], -float(CAP * q), None,
                                  ALU.add).then_inc(S["rank_chain"], 1)
            dve.tensor_copy(gcp.rearrange("p t (q e) -> p t q e", e=NE),
                            gcol.unsqueeze(2).to_broadcast([P, 3, PASSES, NE])).then_inc(S["gate_chain"], 1)
            n_bc = [0]

            def step(ins):
                n_bc[0] += 1
                ins.then_inc(S["block_chain"], 1)
                dve.wait_ge(S["block_chain"], n_bc[0])

            for q in range(1, PASSES):
                last = dve.tensor_scalar(flag[:, NE * (q - 1):NE * q], count, float(CAP * q), None, ALU.is_gt)
            step(last)
            step(dve.tensor_tensor_scan(scan, ones[:, :], flag, 0.0, ALU.mult, ALU.add))
            dve.tensor_copy(nblk[0:1, 0:1], scan[0:1, P - 1:P]).then_inc(S["nblk_ready"], 1)
            step(dve.tensor_reduce(tbc, before[:, :], AX.X, ALU.add))
            step(dve.tensor_scalar(tbc, tbc, -1.0, float(P), ALU.mult, ALU.add))
            step(dve.tensor_scalar(tb, scan, tbc, None, ALU.is_equal))
            step(dve.tensor_tensor(tb, tb, flag, ALU.mult))
            step(dve.tensor_tensor_scan(iota_b, ones[:, :], ones[:, :], -1.0, ALU.mult, ALU.add))
            step(dve.tensor_tensor(tb, tb, iota_b, ALU.mult))
            dve.tensor_reduce(tbc, tb, AX.X, ALU.add).then_inc(S["tab_ready"], 1)
            dve.memset(fss, 0.0).then_inc(S["fin_rec"], 1)
            dve.wait_ge(S["rank_chain"], 4 + PASSES - 1)
            dve.wait_ge(S["gate_chain"], 5)
            dve.wait_ge(S["tokr_kept"], 6)

            def add_round(first, t):
                rows = TT[t][1]
                dve.wait_ge(S["comb_done"], first + (t + 1))
                for i in range(2):
                    dst = tok[0:rows, t, 512 * i:512 * i + 512]
                    last = dve.tensor_tensor(dst, dst, ps[6 + i][0:rows, :], ALU.add)
                last.then_inc(S["acc_done"], 1)

            def gated(cols):
                for t, (t0, rows) in enumerate(TT):
                    for i, col in enumerate(cols):
                        last = dve.tensor_scalar(selg[0:rows, t, CAP * i:CAP * i + CAP], iota_s[0:rows, 0, :],
                                                 rkp[0:rows, t, bass.ds(col, 1)], gcp[0:rows, t, bass.ds(col, 1)],
                                                 ALU.is_equal, ALU.mult)
                last.then_inc(S["selg_ready"], 1)

            def swiglu(b):
                dve.wait_ge(S["freed"], RING * b + (freed_after(MOE0 - 1) + W_SLOTS))
                dve.tensor_scalar(g1, ps[0][:, :], LIMIT, None, ALU.min).then_inc(S["g_clamped"], 1)
                dve.tensor_scalar(u1, ps[1][:, :], -LIMIT, LIMIT, ALU.max, ALU.min).then_inc(S["u_clamped"], 1)
                dve.wait_ge(S["t_done"], b + 1)
                dve.scalar_tensor_tensor(out=tg, in0=tg, scalar=1.0, in1=g1, op0=ALU.add, op1=ALU.mult).then_inc(S["tu_done"], 1)
                dve.wait_ge(S["tu_done"], b + 1)
                dve.wait_ge(S["u_clamped"], b + 1)
                dve.scalar_tensor_tensor(out=hh, in0=u1, scalar=1.0, in1=tg, op0=ALU.add, op1=ALU.mult).then_inc(S["h_ready"], 1)

            with dve.Fori(0, PAIRS) as q:
                add_round(3 * q, 0)
                swiglu(2 * q)
                add_round(3 * q, 1)
                add_round(3 * q, 2)
                dve.wait_ge(S["gathered"], q + 1)
                one_hot((2 * q + 2, 2 * q + 3))
                gated((2 * q, 2 * q + 1))
                swiglu(2 * q + 1)
            for t in range(3):
                add_round(3 * PAIRS, t)
            n = dve.value_load(nblk[0:1, 0:1], min_val=0, max_val=P)
            with dve.If(n > 0):
                dve.wait_ge(S["tab_ready"], 2)
                dve.tensor_copy(tabi[0:1, 1, :], tabrow).then_inc(S["block_chain"], 1)
                dve.wait_ge(S["block_chain"], n_bc[0] + 1)
                dve.tensor_scalar(tabi[0:1, 0, :], tabi[0:1, 1, :], NE - 1, None, ALU.bitwise_and).then_inc(S["block_chain"], 1)
                dve.tensor_scalar(tabrow, tabrow, float(NE), None, ALU.add).then_inc(S["block_chain"], 1)
                dve.wait_ge(S["block_chain"], n_bc[0] + 3)
                dve.tensor_copy(tabi[0:1, 1, :], tabrow).then_inc(S["table_ready"], 1)
                dve.wait_ge(S["table_ready"], 1)
                dve.wait_ge(S["gathered"], PAIRS + 1)
                dve.memset(sel[:, :, CAP:2 * CAP], 0.0)
                dve.memset(selg[:, :, CAP:2 * CAP], 0.0)
                with dve.Fori(0, n) as j:
                    col = dve.value_load(tabi[0:1, 1, bass.ds(j, 1)], min_val=NE, max_val=NCOL - 1)
                    dve.wait_ge(S["gathered"], j + (PAIRS + 1))
                    one_hot((col,))
                    gated((col,))
                    swiglu(j + NE)
                    for t in range(3):
                        add_round(3 * j + 3 * (PAIRS + 1), t)
            dve.wait_ge(S["acc_done"], 3 * n + 3 * (PAIRS + 1))
            dve.wait_ge(S["fin_rec"], 1)
            for t, (t0, rows) in enumerate(TT):
                r = slice(0, rows)
                dve.tensor_tensor_reduce(xnt[r, t, :], tok[r, t, :], tok[r, t, :], 1.0, 0.0, ALU.mult, ALU.add,
                                         fss[r, t:t + 1]).then_inc(S["fin_sq"], 1)
            dve.wait_ge(S["fin_sd"], 1)
            dve.reciprocal(frs, frs).then_inc(S["fin_rec"], 1)
            dve.wait_ge(S["fin_rec"], 2)
            dve.wait_ge(S["gfin_loaded"], 16)
            for t, (t0, rows) in enumerate(TT):
                r = slice(0, rows)
                dve.scalar_tensor_tensor(out=tok[r, t, :], in0=tok[r, t, :], scalar=frs[r, t:t + 1], in1=gfin[r, :],
                                         op0=ALU.mult, op1=ALU.mult).then_inc(S["fin_ready"], 1)

        @block.tensor
        def _(pe):
            pe.wait_ge(S["ident_ready"], 2)
            pe.wait_ge(S["x_loaded"], 32)
            for k in range(KD):
                if k >= 4:
                    pe.wait_ge(S["x_copied"], k - 3)
                for t, (t0, rows) in enumerate(TT):
                    m = pe.transpose(ps[k % 4][:, t0:t0 + rows], x0[0:rows, t, k * P:(k + 1) * P], ident[0:rows, 0:rows])
                m.then_inc(S["x_turned"], 1)
            def norm_sum(n):
                for k in range(KD):
                    pe.wait_ge(S["x_squared"], KD * n + k + 1)
                    m = pe.matmul(ps[5][:, 0:TOK], ones[:, :], sq[:, k, :], start=(k == 0), stop=(k == KD - 1))
                m.then_inc(S["sum_done"], 1)

            pe.wait_ge(S["consts"], 2)
            norm_sum(0)
            pe.wait_ge(S["par_loaded"], n_par)
            pe.wait_ge(S["h0_loaded"], 16)
            pe.transpose(ps[4][:, 0:C_B], stage_a[0:C_B, :], ident[0:C_B, 0:C_B])
            pe.transpose(ps[4][:, C_B:C_H0], stage_b[0:B_ROWS, :], ident[0:B_ROWS, 0:B_ROWS])
            for c in range(LC):
                m = pe.transpose(ps[4][:, C_H0 + NB * c:C_H0 + NB * c + NB], stage_h[:, c * P:(c + 1) * P], ident[0:NB, 0:NB])
            m.then_inc(S["par_turned"], 1)

            def small_inputs():
                pe.wait_ge(S["mem_scaled"], 2)
                for j in range(4):
                    if j >= 2:
                        pe.wait_ge(S["mem_ready"], 2 * (j - 1))
                    for i in range(2):
                        for t in range(2):
                            m = pe.transpose(ps[6 + j % 2][:, NMEM * i + P * t:NMEM * i + P * t + P],
                                             mem[:, t, (2 * j + i) * P:(2 * j + i + 1) * P], ident[:, :])
                    m.then_inc(S["mem_turned"], 1)
                pe.wait_ge(S["prods"], 3)
                pe.wait_ge(S["par_ready"], 1)
                pe.wait_ge(S["consts"], CONSTS)
                for c in range(LC):
                    for t in range(2):
                        pe.matmul(ps[4][:, NB * c + 4 * t:NB * c + 4 * t + 4], ccache[:, t, c * P:(c + 1) * P], indc[:, :],
                                  start=True, stop=True)
                    m = pe.matmul(ps[4][:, 32 + NB * c:40 + NB * c], lcache[:, c * P:(c + 1) * P], indl[:, :],
                                  start=True, stop=True)
                m.then_inc(S["freed"], HEADROOM)

            def project(kind, done, src, bank_free, first_wait):
                count = dict(FRONT)[kind]
                for i in range(count):
                    n = START[kind] + i
                    if kind == "in" and i == HEADROOM:
                        small_inputs()
                    pe.wait_ge(filled[n % RING], 16 * fills_before(n))
                    for half in range(2):
                        o = 2 * i + half
                        bank_free(o)
                        for k in range(KD):
                            if i == 0 and half == 0:
                                first_wait(k)
                            m = pe.matmul(ps[o % 4][:, 0:TOK], wslot(n)[:, k, half * P:(half + 1) * P], src(k),
                                          start=(k == 0), stop=(k == KD - 1))
                        m.then_inc(S["freed" if half else done], 1)

            def in_free(o):
                if o >= 4:
                    pe.wait_ge(S["in_kept"], o - 3)

            project("in", "in_done", lambda k: xn[:, k, :], in_free, lambda k: pe.wait_ge(S["xn_ready"], k + 1))

            def kv(kind, j0):
                for i in range(4):
                    n, j = START[kind] + i, j0 + i
                    pe.wait_ge(filled[n % RING], 16 * fills_before(n))
                    if j in (2, 3, 6, 7):
                        pe.wait_ge(S["kv_kept"], j - 1)
                    for t in range(2):
                        for k in range(KD):
                            m = pe.matmul(ps[6 + j % 2][:, 256 * t:256 * t + 256], mn[:, k, P * t:P * t + P],
                                          wslot(n)[:, k, :], start=(k == 0), stop=(k == KD - 1))
                    m.then_inc(S["freed"], 1)

            pe.wait_ge(S["mem_ready"], KD)
            kv("k", 0)
            pe.wait_ge(S["kv_kept"], 4)
            for j in range(4):
                if j >= 2:
                    pe.wait_ge(S["kt_ready"], j - 1)
                for i in range(2):
                    for t in range(2):
                        m = pe.transpose(ps[6 + j % 2][:, NMEM * i + P * t:NMEM * i + P * t + P],
                                         kvtok[:, t, (2 * j + i) * P:(2 * j + i + 1) * P], ident[:, :])
                m.then_inc(S["kt_turned"], 1)
            pe.wait_ge(S["gate_loaded"], 64)
            pe.wait_ge(S["l_tap"], 16)
            pe.wait_ge(S["l_smp"], 9)
            pe.wait_ge(S["in_kept"], 16)
            for g in range(2):
                for c in range(LC):
                    if g:
                        pe.wait_ge(S["gate_tanh"], c + 1)
                    pe.matmul(ps[c][:, 0:TOK], wgate[:, g, c, :], xc[:, c, :], start=True, stop=True).then_inc(S["gate_done"], 1)
            pe.wait_ge(S["cf_smp"], 1)
            pe.wait_ge(S["cf_tap"], 4 * CW)
            for c in range(LC):
                m = pe.matmul(ps[5][:, 0:TOK], ones[:, :], gc[:, c, :], start=(c == 0), stop=(c == LC - 1))
            m.then_inc(S["mu_done"], 1)
            pe.wait_ge(S["gc_sq"], 1)
            for c in range(LC):
                m = pe.matmul(ps[5][:, 0:TOK], ones[:, :], gc[:, c, :], start=(c == 0), stop=(c == LC - 1))
            m.then_inc(S["var_done"], 1)
            pe.wait_ge(S["kt_ready"], 4)
            for c in range(LC):
                m = pe.transpose(ps[6][0:11, c * P:(c + 1) * P], xpad[:, c, 3 + SEQ - 3:3 + TOK], ident[:, :])
            m.then_inc(S["rows_turned"], 1)
            for c in range(LC):
                m = pe.transpose(ps[7][0:38, c * P:(c + 1) * P], gpad[:, c, 30 + SEQ - 30:30 + TOK], ident[:, :])
            m.then_inc(S["rows_turned"], 1)
            pe.wait_ge(S["scan_ready"], 6)
            for c in range(LC):
                m = pe.transpose(ps[4][0:9, c * P:(c + 1) * P], hs[:, c, SEQ - 1:TOK], ident[:, :])
            m.then_inc(S["rows_turned"], 1)

            def out_free(o):
                if o >= 4:
                    pe.wait_ge(S["res_added"], o - 3)

            pe.wait_ge(S["ylru_ready"], 1)
            pe.wait_ge(S["gate_tanh"], 8)

            def out_wait(k):
                if k == 4:
                    pe.wait_ge(S["ycf_ready"], 1)

            project("out", "out_done", lambda k: zg[:, k, :] if k < 4 else gc[:, k - 4, :], out_free, out_wait)
            norm_sum(1)

            def q_free(o):
                if o < 4:
                    pe.wait_ge(S["res_added"], o + 5)
                else:
                    pe.wait_ge(S["q_kept"], o - 3)

            project("q", "q_done", lambda k: xn[:, k, :], q_free, lambda k: pe.wait_ge(S["xn_ready"], KD + k + 1))
            pe.wait_ge(S["q_kept"], KD)
            pe.wait_ge(S["rows_kept"], 3)
            for i in range(2):
                for c in range(4):
                    m = pe.transpose(ps[6 + i][0:NB, c * P:(c + 1) * P], qT[:, 4 * i + c, SEQ:TOK], ident[:, :])
                m.then_inc(S["qs_turned"], 1)
            for h in range(H):
                for t in range(2):
                    for i in range(2):
                        m = pe.matmul(ps[h][:, NMEM * t:NMEM * t + NMEM], qT[:, 2 * h + i, P * t:P * t + P],
                                      kT[:, 2 * h + i, :], start=(i == 0), stop=(i == 1))
                m.then_inc(S["score_done"], 1)
            pe.wait_ge(S["qs_kept"], 2)
            kv("v", 4)
            for h in range(H):
                pe.wait_ge(S["p_scaled"], h + 1)
                if h < 2:
                    pe.wait_ge(S["kv_kept"], 7 + h)
                else:
                    pe.wait_ge(S["pt_kept"], h - 1)
                for mt in range(2):
                    for t in range(2):
                        m = pe.transpose(ps[6 + h % 2][:, SEQ * mt + P * t:SEQ * mt + P * t + P],
                                         pm[:, h, t, P * mt:P * mt + P], ident[:, :])
                m.then_inc(S["pt_turned"], 1)
            for h in range(H):
                pe.wait_ge(S["pt_kept"], h + 1)
                for i in range(2):
                    for mt in range(2):
                        m = pe.matmul(ps[h][:, SEQ * i:SEQ * i + SEQ], kvtok[:, mt, HD * h + P * i:HD * h + P * i + P],
                                      pT[:, h, mt, :], start=(mt == 0), stop=(mt == 1))
                m.then_inc(S["pv_done"], 1)
            pe.wait_ge(S["kc_freed"], NB)
            for t in range(2):
                m = pe.transpose(ps[6][0:32, P * t:P * t + P], sT[:, t, :], ident[:, :])
            m.then_inc(S["s_turned"], 1)
            pe.wait_ge(S["s_scaled"], 2)
            for t in range(2):
                m = pe.transpose(ps[7][:, 32 * t:32 * t + 32], psS[0:32, P * t:P * t + P], ident[0:32, 0:32])
            m.then_inc(S["sp_turned"], 1)
            pe.wait_ge(S["sp_kept"], 1)
            for g in range(2):
                for b in range(4):
                    n = START["vc"] + 4 * g + b
                    pe.wait_ge(filled[n % RING], 16 * fills_before(n))
                for i in range(2):
                    for t in range(2):
                        for b in range(4):
                            val = slot(START["vc"] + 4 * g + b)
                            m = pe.matmul(ps[4 + 2 * g + i][32 * b:32 * b + 32, :], psT[:, t, :],
                                          val[:, D * t + 512 * i:D * t + 512 * i + 512], start=(t == 0), stop=(t == 1))
                m.then_inc(S["spv_done"], 1)
            pe.wait_ge(S["spv_done"], 2)
            pe.sem_inc(S["freed"], 8)
            pe.wait_ge(S["osb_kept"], 4)
            pe.wait_ge(S["pick_ready"], 2)
            pe.wait_ge(S["pv_kept"], 1)
            for c in range(KD):
                for g in range(2):
                    m = pe.matmul(ps[0][:, NB * c + 4 * g:NB * c + 4 * g + 4], osb[:, g, c * P:(c + 1) * P],
                                  pick[:, g, c // 2, :], start=True, stop=True)
            m.then_inc(S["picked"], 1)
            pe.wait_ge(S["spv_kept"], 1)
            pe.wait_ge(S["pv_kept"], H)

            def o_free(o):
                if o >= 4:
                    pe.wait_ge(S["res_added"], KD + o - 3)

            project("o", "o_done", lambda k: oT[:, k, :], o_free, lambda k: None)
            norm_sum(2)
            def turn_tokens(j):
                t, i = (j % 6) // 2, j % 2
                t0, rows = TT[t]
                if j >= 4:
                    pe.wait_ge(S["tokr_kept"], min(j - 3, 6))
                if j >= 10:
                    pe.wait_ge(S["xnt_kept"], j - 9)
                src = xT if j < 6 else xn
                for c in range(4):
                    m = pe.transpose(ps[j % 4][0:rows, c * P:(c + 1) * P], src[:, 4 * i + c, t0:t0 + rows], ident[:, :])
                m.then_inc(S["tm_turned"], 1)

            pe.wait_ge(S["res_added"], 2 * KD)
            for j in range(6):
                turn_tokens(j)
            pe.wait_ge(S["wr_loaded"], 16)
            pe.wait_ge(S["br_loaded"], 16)
            for t, (t0, rows) in enumerate(TT):
                dst = ps[4][0:rows, NE * t:NE * t + NE]
                pe.matmul(dst, ones[0:1, 0:rows], brow[0:1, :], start=True, stop=False)
                for k in range(KD):
                    if t == 0:
                        pe.wait_ge(S["xn_ready"], 2 * KD + k + 1)
                    m = pe.matmul(dst, xn[:, k, t0:t0 + rows], wr[:, k, :], start=False, stop=(k == KD - 1))
            m.then_inc(S["logit_done"], 1)
            for j in range(6, 10):
                turn_tokens(j)
            pe.wait_ge(S["mask_ready"], 1)
            for t, (t0, rows) in enumerate(TT):
                for i in range(t + 1):
                    n_k = TT[i][1]
                    lhs = before if i == t else ones
                    m = pe.matmul(ps[5][0:rows, NE * t:NE * t + NE], lhs[0:n_k, 0:rows], mask[0:n_k, i, :],
                                  start=(i == 0), stop=(i == t))
            for i, (t0, n_k) in enumerate(TT):
                m = pe.matmul(ps[5][:, 96:128], ones[0:n_k, :], mask[0:n_k, i, :], start=(i == 0), stop=(i == 2))
            m.then_inc(S["rank_done"], 1)
            for j in range(10, 12):
                turn_tokens(j)
            pe.wait_ge(S["gate_chain"], 4)
            for t, (t0, rows) in enumerate(TT):
                m = pe.transpose(ps[4][0:NE, t0:t0 + rows], gcol[0:rows, t, :], ident[0:rows, 0:rows])
            m.then_inc(S["gt0_turned"], 1)

            def rounds(q, t):
                t0, rows = TT[t]
                if q is None:
                    if t:
                        pe.wait_ge(S["acc_done"], t)
                else:
                    pe.wait_ge(S["acc_done"], 3 * q + (3 + t))
                for i in range(2):
                    cols = slice(512 * i, 512 * i + 512)
                    if q is None:
                        m = pe.matmul(ps[6 + i][0:rows, :], gateT[:, t0:t0 + rows], be2[0:NE, cols], start=True, stop=True)
                    else:
                        m = pe.matmul(ps[6 + i][:, :], gT[:, t0:t0 + P], ysb[:, cols], start=True, stop=True)
                m.then_inc(S["comb_done"], 1)

            def gather(q):
                pe.wait_ge(S["sel_ready"], q + 1)
                for k in range(KD):
                    for t, (t0, rows) in enumerate(TT):
                        m = pe.matmul(ps[4 + k // 4][:, P * (k % 4):P * (k % 4) + P], xnt[0:rows, t, k * P:(k + 1) * P],
                                      sel[0:rows, t, :], start=(t == 0), stop=(t == 2))
                m.then_inc(S["gathered"], 1)

            def turn_gates(q):
                pe.wait_ge(S["selg_ready"], q + 1)
                for t, (t0, rows) in enumerate(TT):
                    m = pe.transpose(ps[2][:, t0:t0 + rows], selg[0:rows, t, :], ident[0:rows, 0:rows])
                m.then_inc(S["gt_turned"], 1)

            def up(b, e2, between):
                pe.wait_ge(S["b1_filled"], 16 * b + 16)
                for gu in range(2):
                    for i in range(2):
                        m = pe.matmul(ps[gu][CAP * i:CAP * i + CAP, :], ones[0:1, 0:CAP],
                                      b1row[0:1, D * gu + 512 * i:D * gu + 512 * i + 512], start=True, stop=False)
                m.then_inc(S["b1_used"], 1)
                for k in range(W_SLOTS):
                    pe.wait_ge(filled[k], 16 * b + 16 * fills_before(MOE0 + k))
                    for gu in range(2):
                        for i in range(2):
                            m = pe.matmul(ps[gu][CAP * i:CAP * i + CAP, :], xeT[:, k, CAP * e2:CAP * e2 + CAP],
                                          ring[:, k, D * gu + 512 * i:D * gu + 512 * i + 512],
                                          start=False, stop=(k == W_SLOTS - 1))
                    m.then_inc(S["freed"], 1)
                    between(k)

            def turn_h(b):
                pe.wait_ge(S["h_ready"], b + 1)
                for j in range(4):
                    m = pe.transpose(ps[2][:, j * P:(j + 1) * P], hh[:, j * P:(j + 1) * P], ident[:, :])
                m.then_inc(S["h_turned"], 1)

            def down(b):
                pe.wait_ge(S["hT_ready"], b + 1)
                for k in range(KD):
                    s = W_SLOTS + k // 2
                    if k % 2 == 0:
                        pe.wait_ge(filled[s], 16 * b + 16 * fills_before(MOE0 + s))
                    for i in range(2):
                        m = pe.matmul(ps[3][CAP * i:CAP * i + CAP, :], hTv[:, k % 4, CAP * (k // 4):CAP * (k // 4) + CAP],
                                      ring[:, s, D * (k % 2) + 512 * i:D * (k % 2) + 512 * i + 512],
                                      start=(k == 0), stop=(k == KD - 1))
                    if k % 2:
                        m.then_inc(S["freed"], 1)

            def pair(q, first):
                prev = None if first else q - 1

                def between(k):
                    if k == 2:
                        if first:
                            pe.wait_ge(S["be2_loaded"], 16)
                        else:
                            pe.wait_ge(S["y_ready"], 2 * q)
                            pe.wait_ge(S["gt_ready"], q)
                        rounds(prev, 0)

                pe.wait_ge(S["xe_ready"], q + 1)
                up(2 * q, 0, between)
                rounds(prev, 1)
                turn_h(2 * q)
                rounds(prev, 2)
                down(2 * q)
                up(2 * q + 1, 1, lambda k: None)
                turn_gates(q)
                gather(q + 1)
                pe.wait_ge(S["gt_ready"], q + 1)
                turn_h(2 * q + 1)
                pe.wait_ge(S["y_ready"], 2 * q + 1)
                down(2 * q + 1)

            pe.wait_ge(S["xnt_kept"], 6)
            pe.wait_ge(S["gt0_kept"], 1)
            gather(0)
            pe.wait_ge(S["tail_zeroed"], 1)
            pair(0, True)
            with pe.Fori(1, PAIRS) as q:
                pair(q, False)
            pe.wait_ge(S["y_ready"], NE)
            for t in range(3):
                rounds(PAIRS - 1, t)
            pe.wait_ge(S["nblk_ready"], 1)
            n = pe.value_load(nblk[0:1, 0:1], min_val=0, max_val=P)
            with pe.If(n > 0):
                pe.wait_ge(S["tab_ready"], 1)
                pe.wait_ge(S["xe_ready"], PAIRS + 1)
                pe.transpose(ps[5][0:1, 0:P], tbc, ident[:, :]).then_inc(S["tab_turned"], 1)
                pe.wait_ge(S["tab_ready"], 2)
                with pe.Fori(0, n) as j:
                    pe.wait_ge(S["xe_ready"], j + (PAIRS + 1))
                    gather(j + (PAIRS + 1))
                    pe.wait_ge(S["xe_ready"], j + (PAIRS + 2))
                    up(j + NE, 0, lambda k: None)
                    turn_gates(j + PAIRS)
                    pe.wait_ge(S["gt_ready"], j + (PAIRS + 1))
                    turn_h(j + NE)
                    down(j + NE)
                    pe.wait_ge(S["y_ready"], j + (NE + 1))
                    for t in range(3):
                        rounds(j + PAIRS, t)


INPUTS = ["x_prompt", "x_sample", "state_lru_h", "cache_lru_conv", "cache_cf_conv", "cache_mem_k", "cache_mem_v",
          "mem_prompt", "g_mix", "w_in", "w_lru_conv", "b_lru_conv", "w_lru_a", "b_lru_a", "w_lru_x", "b_lru_x",
          "lru_lambda", "w_cf_conv", "b_cf_conv", "g_cf_ln", "b_cf_ln", "w_out", "g_xa", "g_mem", "w_q", "w_k", "w_v",
          "w_o", "g_moe", "w_router", "b_router", "w_e1", "b_e1", "w_e2", "b_e2", "g_final"]
OUTPUTS = [("y_prompt", (1, SEQ, D)), ("y_sample", (NB, 1, D)), ("lru_h_prompt", (1, 1, LRU)),
           ("lru_conv_prompt", (1, 1, LW - 1, LRU)), ("cf_conv_prompt", (1, 1, CW - 1, LRU)),
           ("mem_k", (1, 1, NMEM, H, HD)), ("mem_v", (1, 1, NMEM, H, HD)), ("lru_h_sample", (1, NB, LRU)),
           ("cache_lru", (1, NB, LW - 1, LRU)), ("cache_cf", (1, NB, CW - 1, LRU))]


def kernel(**inputs):
    import concourse.bacc as bacc
    from concourse.bass_utils import run_bass_kernel_spmd

    nc = bacc.Bacc("TRN2", target_bir_lowering=False, num_devices=1)
    arrays, a, outs = {}, {}, {}
    for name in INPUTS:
        x = np.ascontiguousarray(inputs[name])
        arrays["in_" + name] = x
        a[name] = nc.dram_tensor("in_" + name, x.shape, mybir.dt.from_np(x.dtype), kind="ExternalInput").ap()
    for name, shape in OUTPUTS:
        outs[name] = nc.dram_tensor("out_" + name, shape, F32, kind="ExternalOutput").ap()
    build(nc, a, outs)
    r = run_bass_kernel_spmd(nc, [arrays], core_ids=[0])
    return tuple(r.results[0]["out_" + name] for name, _ in OUTPUTS)
```

```python
import numpy as np
from contextlib import ExitStack

import concourse.bass as bass
import concourse.mybir as mybir

F32 = mybir.dt.float32
I32 = mybir.dt.int32
U32 = mybir.dt.uint32
ALU = mybir.AluOpType
ACT = mybir.ActivationFunctionType
AX = mybir.AxisListType

P = 128
D = 1024
KD = D // P
SEQ = 256
NB = 8
TOK = SEQ + NB
TT = [(0, P), (P, P), (2 * P, NB)]
LRU = 512
LC = LRU // P
HEAD = 64
CW = 31
LW = 4
NMEM = 256
H = 4
HD = D // H
NE = 32
CAP = 64
PASSES = -(-TOK // CAP)
NCOL = PASSES * NE
EPS = 1e-6
LIMIT = 7.0
ALPHA = 1.702
GELU_C = 0.7978845608028654
GELU_A = 0.044715
BIG = 4096.0

SLOT = 2048
RING = 12
W_SLOTS = 8
HEADROOM = 4
IN_FIRST = 6
TURN_BANK = (2, 3, 6, 7)
LAST_BANKS = (6, 0, 4)
PAIRS = NE // 2

FRONT = [("in", 8), ("k", 4), ("va", 2), ("out", 4), ("q", 4), ("vb", 2), ("kc", 8), ("vc", 8), ("o", 4)]
START = {}
_n = HEADROOM
for _kind, _count in FRONT:
    START[_kind] = _n
    _n += _count
MOE0 = _n
KV_ENTRY = [START["k"] + _i for _i in range(4)] + [START[_k] + _i for _k in ("va", "vb") for _i in range(2)]
KV_BANK = [6, 7, 6, 7, 6, 5, 6, 7]
assert MOE0 % RING == 0
HEAD_SLOTS = W_SLOTS // 2
KC_SLOTS = 8

IN_ORDER = [4, 5, 6, 7, 0, 1, 2, 3]

C_WCF = 0
C_B = CW * LC
C_WL, C_BLC, C_BA, C_BX, C_LAM, C_BCF, C_GLN, C_BLN = (C_B + 4 * i for i in (0, 4, 5, 6, 7, 8, 9, 10))
C_GMIX, C_GXA, C_GMEM, C_GMOE = (C_B + 44 + 8 * i for i in range(4))
B_ROWS = 76
C_H0 = C_B + B_ROWS
NPAR = C_H0 + LC * NB


def freed_after(n):
    if n < HEADROOM:
        return IN_FIRST + HEADROOM
    if n < HEADROOM + IN_FIRST:
        return n - HEADROOM + 1
    if n < START["kc"]:
        return n + 1
    return n + 1 - KC_SLOTS


def fills_before(n):
    return n // RING + 1 - (1 if n % RING < HEADROOM else 0)


def build(nc, a, outs):
    ctx = ExitStack()
    with ctx:
        def sb(name, shape, dt=F32):
            return ctx.enter_context(nc.sbuf_tensor(name, shape, dt))

        def sem(name):
            return ctx.enter_context(nc.semaphore(name))

        ring = sb("ring", [P, RING, SLOT])
        MIXER_W = 4 * (30 + TOK) + 4 * (3 + TOK) + 9 * LC * TOK
        EXPERT_W = 3 * D + KD * 2 * CAP + 9 * P + 5 * 512 + 3 * D + D
        MIXW = max(MIXER_W, EXPERT_W)
        mix = sb("mix", [P, MIXW])
        xT = sb("xT", [P, KD, TOK])
        xn = sb("xn", [P, KD, TOK])
        rstd = sb("rstd", [P, TOK])
        sq = sb("sq", [P, KD, TOK])
        tok = sb("tok", [P, 3, D])
        mn = sb("mn", [P, KD, NMEM])
        kT = sb("kT", [P, KD, NMEM])
        wgate = sb("wgate", [P, 2, LC, P])
        par = sb("par", [P, NPAR])
        ident = sb("ident", [P, P])
        ones = sb("ones", [P, P])
        before = sb("before", [P, P])
        wr = sb("wr", [P, KD, NE])
        brout = sb("brout", [P, NE])
        iota_s = sb("iota_s", [P, 2, CAP])
        iota_e = sb("iota_e", [P, NE])
        indc = sb("indc", [120, 4])
        indl = sb("indl", [24, NB])
        eps = sb("eps", [P, 1])
        small = sb("small", [P, 64])

        pos = [0]

        def part(width, shape=None, **kw):
            v = mix[:, pos[0]:pos[0] + width]
            pos[0] += width
            return v.rearrange(shape, **kw) if shape else v

        gpad = part(4 * (30 + TOK), "p (c t) -> p c t", c=LC)
        xpad = part(4 * (3 + TOK), "p (c t) -> p c t", c=LC)
        zg, za, th, gc, xc, tr, ti, av, uv = (part(LC * TOK, "p (c t) -> p c t", c=LC) for _ in range(9))
        hs = th
        assert pos[0] == MIXER_W
        stage_a = av.rearrange("p c t -> p (c t)")[:, 0:P]
        stage_b = tr.rearrange("p c t -> p (c t)")[:, 0:P]
        stage_h = uv.rearrange("p c t -> p (c t)")[0:NB, 0:LRU]
        rows_out = sq[:, 4:8, :].rearrange("p c t -> p (c t)")
        pos[0] = 0
        qT = part(KD * TOK, "p (c t) -> p c t", c=KD)
        oT = part(KD * TOK, "p (c t) -> p c t", c=KD)
        pm_at = pos[0]
        pm = part(H * 2 * NMEM, "p (h t m) -> p h t m", h=H, t=2)
        osb = mix[:, pm_at:pm_at + 2 * D].rearrange("p (g c) -> p g c", g=2)
        pT = part(H * 2 * SEQ, "p (h m t) -> p h m t", h=H, m=2)
        qrow = part(2 * D)
        sT = part(2 * NB * H, "p (m c) -> p m c", m=2)
        psS = part(2 * P)
        psT = part(2 * NB * H, "p (m c) -> p m c", m=2)
        pos[0] = 0
        xnt = part(3 * D, "p (t d) -> p t d", t=3)
        xeT = part(KD * 2 * CAP, "p (k s) -> p k s", k=KD)
        sel = part(3 * P, "p (t s) -> p t s", t=3)
        selg = part(3 * P, "p (t s) -> p t s", t=3)
        gT = part(3 * P)
        g1, u1, tg, hh, hT = (part(512) for _ in range(5))
        hTv = hT.rearrange("p (j s) -> p j s", j=4)
        ysb = part(D)
        b1row = part(2 * D)
        head_u = part(D)
        assert pos[0] == EXPERT_W
        sqf = sq[:, :, :].rearrange("p c t -> p (c t)")
        xnf = xn[:, :, :].rearrange("p c t -> p (c t)")
        be2, gfin = xnf[:, 0:D], xnf[:, D:2 * D]
        qb = xnf[:, 0:2 * D].rearrange("p (i c) -> p i c", i=2)
        qs = tok[:, 2, :]
        at = [0]

        def table(*shape):
            n = int(np.prod(shape))
            v = sqf[:, at[0]:at[0] + n]
            at[0] += n
            return v if len(shape) == 1 else v.rearrange("p (a c) -> p a c", a=shape[0])

        rkp, gcp = table(3, NCOL), table(3, NCOL)
        gcol, mask, lg, rk = (table(3, NE) for _ in range(4))
        iota_b = table(P)
        eq_at = at[0]
        eq = table(3 * 4 * NE).rearrange("p (t k e) -> p t k e", t=3, k=4)
        flag, scan, tb = (sqf[:, eq_at + P * i:eq_at + P * i + P] for i in range(3))
        tabrow = table(P)[0:1, :]
        count = table(NE)
        assert at[0] <= KD * TOK
        gateT = rstd[0:NE, :]
        head = [v[:, 0:SLOT].rearrange("p (g c) -> p g c", g=2) for v in
                (mn[:, :, :].rearrange("p k m -> p (k m)"), kT[:, :, :].rearrange("p k m -> p (k m)"),
                 xT[:, :, :].rearrange("p k t -> p (k t)"))]
        head = [(v[:, 0, :], v[:, 1, :]) for v in head]
        head.insert(2, (wgate[:, :, :, :].rearrange("p g c i -> p (g c i)"), head_u))
        tabi = sb("tabi", [1, 2, P], I32)
        nblk = sb("nblk", [1, 1], I32)

        kvtok = tok[:, 0:2, :]
        x0 = ring[:, 0:2, :].rearrange("p s c -> p (s c)")[:, 0:3 * D].rearrange("p (t d) -> p t d", t=3)
        wlrep = ring[0:24, 1, D:D + LRU]
        lcache = ring[0:24, 1, D + LRU:D + 2 * LRU]
        mem = ring[:, 2, :].rearrange("p (t d) -> p t d", t=2)
        ccache = ring[0:120, 3, 0:2 * LRU].rearrange("p (t c) -> p t c", t=2)
        wcrep = ring[0:120, 3, 2 * LRU:3 * LRU]

        small_at = [0]

        def tiny(n):
            v = small[:, small_at[0]:small_at[0] + n]
            small_at[0] += n
            return v

        rm = tiny(2)
        mss = tiny(2)
        spn, spp, sp_e, sp_z, sp_q, sp_t = (tiny(4) for _ in range(6))
        hba, hbx = tiny(4), tiny(4)
        mxn, rs, fss, frs = tiny(8), tiny(8), tiny(3), tiny(3)
        tss, trs = tiny(3), tiny(3)

        pick = sb("pick", [P, 2, H, 4])
        extra = sb("extra", [P, 96])
        m8 = extra[:, 0:24].rearrange("p (t k) -> p t k", t=3)
        ge = extra[:, 24:36].rearrange("p (t k) -> p t k", t=3)
        idf = extra[:, 36:60].rearrange("p (t k) -> p t k", t=3)
        smx, ssum = extra[:, 60:61], extra[:, 61:62]
        tbc = extra[:, 62:63]
        unused = extra[:, 72:73]
        gsum, nv0, grec = extra[:, 63:66], extra[:, 66:69], extra[:, 69:72]
        nm8 = sb("idx8", [P, 3, 8], U32)
        ps = [ctx.enter_context(nc.psum_tensor(f"ps{i}", [P, 512], F32)) for i in range(8)]

        filled = [sem(f"filled{i}") for i in range(RING)]
        names = """x_loaded par_loaded h0_loaded mem_loaded cc_loaded lc_loaded gate_loaded router_loaded
        head_filled consts zeroed ident_ready pick_ready freed kc_freed
        x_turned x_copied x_squared sum_done sd_ready rstd_ready xn_ready par_turned par_ready
        mem_squared mem_sd mem_rec mem_scaled mem_turned mem_ready prods
        in_done in_kept glu_ready cf_tap cf_smp l_tap l_smp sp_chain sp_exp sp_ready
        kv_kept kt_turned kt_ready kv_stored
        gate_done gate_tanh a_ready t_ready beta_chain u_ready scan_ready gelu_sq gelu_in gelu_th gelu_g ylru_ready
        rows_turned rows_kept rows_stored caches_shifted
        mu_done gc_cent gc_sq var_done ln_chain yn_ready y_th ycf_ready
        out_done res_added q_done q_kept score_done mx_ready p_exp p_scaled pt_turned pt_kept pv_done pv_kept
        qs_turned qs_kept qrow_loaded qb_ready s_turned smax_ready s_exp s_scaled sp_turned sp_kept spv_done osb_kept picked spv_kept
        o_done tok_squared tok_rooted tm_turned tokr_kept xnt_kept logit_done lg_zeroed lg_ready idx_ready eq_ready gate_chain rank_chain block_chain nblk_ready v0_ready ge_ready mask_ready rank_done
        gt0_turned gt0_kept be2_loaded tab_turned tab_ready table_ready
        tail_zeroed sel_ready selg_ready gathered xe_ready gt_turned gt_ready g_clamped u_clamped t_done tu_done h_ready
        h_turned hT_ready y_ready comb_done acc_done b1_filled b1_used gfin_loaded
        fin_sq fin_sd fin_rec fin_ready y_stored""".split()
        S = {n: sem(n) for n in names}

        def slot(n):
            return ring[:, n % RING, :]

        def wait_tile(eng, kind, done, o):
            if o % 2:
                eng.wait_ge(S["freed"], freed_after(START[kind] + o // 2))
            else:
                eng.wait_ge(S[done], o // 2 + 1)

        def wslot(n):
            return slot(n).rearrange("p (k c) -> p k c", k=KD)

        PAR_ROWS, at_row = [], 0
        for name, rows in (("w_lru_conv", 16), ("b_lru_conv", 4), ("b_lru_a", 4), ("b_lru_x", 4), ("lru_lambda", 4),
                           ("b_cf_conv", 4), ("g_cf_ln", 4), ("b_cf_ln", 4), ("g_mix", 8), ("g_xa", 8),
                           ("g_mem", 8), ("g_moe", 8)):
            src = a[name]
            src = src[0].rearrange("w (t c) -> (w t) c", c=P) if rows == 16 else src.rearrange("o (t c) -> (o t) c", c=P)
            PAR_ROWS.append((at_row, rows, src))
            at_row += rows
        assert at_row == B_ROWS
        CONSTS = 12
        n_par = 16 * 13
        block = ctx.enter_context(nc.Block())

        @block.sync
        def _(sp):
            sp.dma_start(x0[:, 0:2, :], a["x_prompt"][0].rearrange("(t p) d -> p t d", p=P)).then_inc(S["x_loaded"], 16)
            sp.dma_start(x0[0:NB, 2, :], a["x_sample"].rearrange("b t d -> (b t) d")).then_inc(S["x_loaded"], 16)
            for r0, rows, src in PAR_ROWS[1::2]:
                sp.dma_start(stage_b[r0:r0 + rows, :], src).then_inc(S["par_loaded"], 16)
            sp.wait_ge(S["par_loaded"], n_par)
            sp.wait_ge(S["h0_loaded"], 16)

            def source(kind, i):
                if kind == "kc" or kind == "vc":
                    c = a["cache_mem_k" if kind == "kc" else "cache_mem_v"]
                    return c[0, i].rearrange("(t p) h d -> p t (h d)", p=P)
                w = a["w_" + kind[0] if kind in ("va", "vb") else "w_" + kind][0]
                c = IN_ORDER[i] if kind == "in" else i + 2 if kind == "vb" else i
                return w[:, 256 * c:256 * c + 256].rearrange("(k p) c -> p k c", p=P)

            for kind, count in FRONT:
                for i in range(count):
                    n = START[kind] + i
                    if kind == "in" and i == 1:
                        sp.dma_start(mem, a["mem_prompt"][0].rearrange("(t p) d -> p t d", p=P)).then_inc(S["mem_loaded"], 16)
                    if n >= RING:
                        m = n - RING
                        if START["kc"] <= m < START["vc"]:
                            sp.wait_ge(S["kc_freed"], m - START["kc"] + 1)
                        else:
                            sp.wait_ge(S["freed"], freed_after(m))
                    dst = slot(n).rearrange("p (t c) -> p t c", t=2) if kind in ("kc", "vc") else wslot(n)
                    sp.dma_start(dst, source(kind, i)).then_inc(filled[n % RING], 16)

            def fill(e, s, free):
                sp.wait_ge(S["freed"], free)
                if s < W_SLOTS:
                    src = a["w_e1"][0][bass.ds(e, 1), s * P:(s + 1) * P, :].rearrange("o p c -> p (o c)")
                    dst = ring[:, s, :]
                else:
                    j = s - W_SLOTS
                    src = a["w_e2"][0][bass.ds(e, 1), j * 2 * P:(j + 1) * 2 * P, :].rearrange(
                        "o (t p) c -> p (o t) c", p=P)
                    dst = ring[:, s, :].rearrange("p (t c) -> p t c", t=2)
                sp.dma_start(dst, src).then_inc(filled[s], 16)

            def expert(e, b, first=0):
                for s in range(first, RING):
                    fill(e, s, RING * b + freed_after(MOE0 + s - RING))

            def bias(e):
                sp.dma_start(b1row[0:1, :], a["b_e1"][0][bass.ds(e, 1), :]).then_inc(S["b1_filled"], 16)

            def fill_head(k):
                for gu in range(2):
                    sp.dma_start(head[k][gu], a["w_e1"][0, 0, k * P:(k + 1) * P, D * gu:D * gu + D]).then_inc(S["head_filled"], 16)

            sp.wait_ge(S["freed"], freed_after(KV_ENTRY[7]))
            fill_head(0)
            sp.wait_ge(S["score_done"], H)
            fill_head(1)
            fill_head(2)
            for s in range(HEAD_SLOTS, W_SLOTS):
                fill(0, s, freed_after(MOE0 + s - RING))
            bias(0)
            for s in range(HEAD_SLOTS):
                fill(1, s, freed_after(MOE0 + s - RING))
            for s in range(W_SLOTS, RING):
                fill(0, s, freed_after(MOE0 + s - RING))
            sp.wait_ge(S["tm_turned"], 6)
            fill_head(3)
            sp.wait_ge(S["b1_used"], 1)
            bias(1)
            for s in range(HEAD_SLOTS, W_SLOTS):
                fill(1, s, freed_after(MOE0 + 2 * (s - HEAD_SLOTS)))
            expert(1, 1, W_SLOTS)
            with sp.Fori(2, NE) as e:
                sp.wait_ge(S["b1_used"], e)
                bias(e)
                expert(e, e)
            sp.wait_ge(S["nblk_ready"], 1)
            n = sp.value_load(nblk[0:1, 0:1], min_val=0, max_val=P)
            with sp.If(n > 0):
                sp.wait_ge(S["table_ready"], 1)
                with sp.Fori(0, n) as j:
                    e = sp.value_load(tabi[0:1, 0, bass.ds(j, 1)], min_val=0, max_val=NE - 1)
                    sp.wait_ge(S["b1_used"], j + NE)
                    bias(e)
                    expert(e, j + NE)
            for t in range(2):
                sp.wait_ge(S["fin_ready"], t + 1)
                sp.dma_start(outs["y_prompt"][0, t * P:(t + 1) * P, :], tok[:, t, :]).then_inc(S["y_stored"], 16)
            sp.wait_ge(S["fin_ready"], 3)
            sp.dma_start(outs["y_sample"].rearrange("b t d -> (b t) d"), tok[0:NB, 2, :]).then_inc(S["y_stored"], 16)
            sp.wait_ge(S["y_stored"], 48)
            sp.wait_ge(S["kv_stored"], 32)
            sp.wait_ge(S["rows_stored"], 16 * 6)
            sp.wait_ge(S["caches_shifted"], 32)

        @block.gpsimd
        def _(pool):
            pool.memset(ident[:, :], 0.0).then_inc(S["ident_ready"], 1)
            pool.memset(ones[:, :], 1.0).then_inc(S["consts"], 1)
            pool.wait_ge(S["ident_ready"], 1)
            pool.affine_select(out=ident[:, :], in_=ident[:, :], compare_op=ALU.not_equal, fill=1.0, base=0,
                               pattern=[[-1, P]], channel_multiplier=1).then_inc(S["ident_ready"], 1)
            pool.memset(eps[:, :], EPS).then_inc(S["consts"], 1)
            pool.memset(tss, 0.0).then_inc(S["zeroed"], 1)
            pool.memset(wgate[:, :, :, :], 0.0).then_inc(S["zeroed"], 1)
            pool.memset(gpad[:, :, 0:30], 0.0).then_inc(S["zeroed"], 1)
            pool.memset(xpad[:, :, 0:3], 0.0).then_inc(S["zeroed"], 1)
            pool.wait_ge(S["par_loaded"], n_par)
            pool.dma_start(ccache, a["cache_cf_conv"][0].rearrange("b w c -> (b w) c").rearrange(
                "(t r) c -> r t c", t=2)).then_inc(S["cc_loaded"], 16)
            for b in range(4):
                pool.dma_start(wcrep[30 * b:30 * b + 30, :], a["w_cf_conv"][0, 0:30, :]).then_inc(S["cc_loaded"], 16)
            pool.dma_start(lcache, a["cache_lru_conv"][0].rearrange("b w c -> (b w) c")).then_inc(S["lc_loaded"], 16)
            for b in range(NB):
                pool.dma_start(wlrep[3 * b:3 * b + 3, :], a["w_lru_conv"][0, 0:3, :]).then_inc(S["lc_loaded"], 16)
            pool.memset(before[:, :], 1.0).then_inc(S["consts"], 1)
            pool.memset(indc[:, :], 1.0).then_inc(S["consts"], 1)
            pool.memset(indl[:, :], 1.0).then_inc(S["consts"], 1)
            pool.memset(pick[:, :, :, :], 0.0).then_inc(S["pick_ready"], 1)
            pool.iota(iota_s[:, :, :], pattern=[[0, 2], [1, CAP]], base=0, channel_multiplier=0,
                      allow_small_or_imprecise_dtypes=True).then_inc(S["consts"], 1)
            pool.iota(iota_e[:, :], pattern=[[1, NE]], base=0, channel_multiplier=0,
                      allow_small_or_imprecise_dtypes=True).then_inc(S["consts"], 1)
            pool.wait_ge(S["consts"], 7)
            pool.affine_select(out=before[:, :], in_=before[:, :], compare_op=ALU.is_gt, fill=0.0, base=0,
                               pattern=[[1, P]], channel_multiplier=-1).then_inc(S["consts"], 1)
            for n, (ind, taps, width) in enumerate(((indc, CW - 1, 4), (indl, LW - 1, NB))):
                pool.affine_select(out=ind[:, :], in_=ind[:, :], compare_op=ALU.is_ge, fill=0.0, base=0,
                                   pattern=[[-taps, width]], channel_multiplier=1).then_inc(S["consts"], 1)
                pool.wait_ge(S["consts"], 9 + 2 * n)
                pool.affine_select(out=ind[:, :], in_=ind[:, :], compare_op=ALU.is_gt, fill=0.0, base=taps,
                                   pattern=[[taps, width]], channel_multiplier=-1).then_inc(S["consts"], 1)

            pool.wait_ge(S["pick_ready"], 1)
            pool.affine_select(out=pick[:, :, :, :], in_=pick[:, :, :, :], compare_op=ALU.not_equal, fill=1.0, base=0,
                               pattern=[[16, 2], [1, H], [36, 4]], channel_multiplier=-1).then_inc(S["pick_ready"], 1)
            for g, name in enumerate(("w_lru_a", "w_lru_x")):
                w = a[name][0].rearrange("(c two) i j -> two i c j", two=2)
                for half in range(2):
                    r = slice(HEAD * half, HEAD * half + HEAD)
                    pool.dma_start(wgate[r, g, :, r], w[half]).then_inc(S["gate_loaded"], 16)
            pool.dma_start(wr[:, :, :], a["w_router"][0].rearrange("(k p) e -> p k e", p=P)).then_inc(S["router_loaded"], 16)
            pool.dma_start(brout[:, :], a["b_router"].partition_broadcast(P)).then_inc(S["router_loaded"], 16)
            pool.dma_start(outs["cache_lru"][0, :, 0:LW - 2, :], a["cache_lru_conv"][0, :, 1:LW - 1, :]).then_inc(S["caches_shifted"], 16)
            pool.dma_start(outs["cache_cf"][0, :, 0:CW - 2, :], a["cache_cf_conv"][0, :, 1:CW - 1, :]).then_inc(S["caches_shifted"], 16)
            pool.wait_ge(S["qrow_loaded"], 32)
            pool.wait_ge(S["pick_ready"], 2)
            pool.wait_ge(S["consts"], CONSTS)
            for b in range(NB):
                if b >= 2:
                    pool.wait_ge(S["kc_freed"], b - 1)
                r = 32 * (b % 4)
                pool.partition_broadcast(qb[:, b % 2, :], qrow[r:r + 1, D * (b // 4):D * (b // 4) + D], P).then_inc(S["qb_ready"], 1)
            pool.wait_ge(S["sum_done"], 2)
            pool.memset(lg, 0.0).then_inc(S["lg_zeroed"], 1)
            pool.wait_ge(S["xnt_kept"], 6)
            pool.memset(gT[:, TOK:3 * P], 0.0).then_inc(S["tail_zeroed"], 1)


        @block.scalar
        def _(act):
            act.dma_start(stage_a[0:CW * LC, :], a["w_cf_conv"][0].rearrange("w (t c) -> (w t) c", c=P)).then_inc(S["par_loaded"], 16)
            for r0, rows, src in PAR_ROWS[0::2]:
                act.dma_start(stage_b[r0:r0 + rows, :], src).then_inc(S["par_loaded"], 16)
            act.dma_start(stage_h, a["state_lru_h"][0]).then_inc(S["h0_loaded"], 16)
            for k in range(KD):
                act.wait_ge(S["x_copied"], k + 1)
                act.activation(sq[:, k, :], xT[:, k, :], ACT.Square).then_inc(S["x_squared"], 1)
            def root(n):
                act.wait_ge(S["sum_done"], n + 1)
                act.activation(rstd[:, :], ps[5][:, 0:TOK], ACT.Sqrt, bias=eps[:, 0:1], scale=1.0 / D).then_inc(S["sd_ready"], 1)

            act.wait_ge(S["consts"], 2)
            root(0)
            act.wait_ge(S["mem_loaded"], 16)
            for t in range(2):
                act.activation(xc.rearrange("p c t -> p (c t)")[:, 0:D], mem[:, t, :], ACT.Square,
                               accum_out=mss[:, t:t + 1]).then_inc(S["mem_squared"], 1)
                act.wait_ge(S["mem_squared"], t + 1)
            act.activation(rm, mss, ACT.Sqrt, bias=eps[:, 0:1], scale=1.0 / D).then_inc(S["mem_sd"], 1)
            act.wait_ge(S["par_ready"], 2)
            act.activation(sp_e, spn, ACT.Exp).then_inc(S["sp_exp"], 1)
            act.wait_ge(S["zeroed"], 4)
            for o in range(16):
                if o != 2 * IN_FIRST:
                    wait_tile(act, "in", "in_done", o)
                src, c = ps[o % 4][:, 0:TOK], o % 4
                if o == 2 * IN_FIRST:
                    for j in range(4):
                        act.wait_ge(S["mem_turned"], j + 1)
                        for i in range(2):
                            k = 2 * j + i
                            act.activation(mn[:, k, :], ps[6 + j % 2][:, NMEM * i:NMEM * i + NMEM], ACT.Copy,
                                           scale=par[:, C_GMEM + k:C_GMEM + k + 1]).then_inc(S["mem_ready"], 1)
                    wait_tile(act, "in", "in_done", o)
                if o < 4:
                    act.activation(za[:, c, :], src, ACT.Copy, scale=0.5).then_inc(S["in_kept"], 1)
                elif o < 8:
                    act.activation(th[:, c, :], src, ACT.Tanh, scale=0.5).then_inc(S["in_kept"], 1)
                elif o < 12:
                    act.activation(xpad[:, c, 3:3 + TOK], src, ACT.Copy).then_inc(S["in_kept"], 1)
                else:
                    act.activation(zg[:, c, :], src, ACT.Copy).then_inc(S["in_kept"], 1)

            def keep_kv(j, dst):
                act.wait_ge(S["freed"], freed_after(KV_ENTRY[j]))
                c = 256 * (j % 4)
                act.activation(dst[:, :, c:c + 256], ps[KV_BANK[j]][:, :].rearrange("p (t c) -> p t c", t=2),
                               ACT.Copy).then_inc(S["kv_kept"], 1)

            for j in range(4):
                keep_kv(j, kvtok)
            act.wait_ge(S["kv_kept"], 4)
            act.dma_start(outs["mem_k"][0, 0].rearrange("(t p) h d -> p t (h d)", p=P), kvtok).then_inc(S["kv_stored"], 16)
            act.wait_ge(S["in_kept"], 16)
            act.activation(uv, zg, ACT.Square).then_inc(S["gelu_sq"], 1)
            for j in range(4):
                act.wait_ge(S["kt_turned"], j + 1)
                act.activation(kT[:, 2 * j:2 * j + 2, :], ps[6 + j % 2][:, :].rearrange("p (t c) -> p t c", t=2),
                               ACT.Copy).then_inc(S["kt_ready"], 1)
            act.wait_ge(S["gelu_in"], 2)
            act.activation(uv, uv, ACT.Tanh, scale=GELU_C).then_inc(S["gelu_th"], 1)
            act.wait_ge(S["sp_ready"], 1)
            for g, (dst, hb) in enumerate(((tr, hba), (ti, hbx))):
                for c in range(LC):
                    act.wait_ge(S["gate_done"], 4 * g + c + 1)
                    act.activation(dst[:, c, :], ps[c][:, 0:TOK], ACT.Tanh, bias=hb[:, c:c + 1],
                                   scale=0.5).then_inc(S["gate_tanh"], 1)
            act.wait_ge(S["gate_tanh"], 4)
            for c in range(LC):
                act.activation(av[:, c, :], tr[:, c, :], ACT.Exp, bias=spn[:, c:c + 1],
                               scale=spn[:, c:c + 1]).then_inc(S["a_ready"], 1)
            act.wait_ge(S["a_ready"], 4)
            for c in range(LC):
                act.activation(tr[:, c, :], tr[:, c, :], ACT.Tanh, bias=spp[:, c:c + 1],
                               scale=spp[:, c:c + 1]).then_inc(S["t_ready"], 1)
            act.wait_ge(S["beta_chain"], 3)
            act.activation(tr, tr, ACT.Sqrt).then_inc(S["t_ready"], 1)
            act.wait_ge(S["gc_cent"], 1)
            act.activation(gc, za, ACT.Square).then_inc(S["gc_sq"], 1)
            act.wait_ge(S["kv_stored"], 16)
            keep_kv(4, kvtok)
            act.wait_ge(S["var_done"], 1)
            act.activation(rstd[:, :], ps[5][:, 0:TOK], ACT.Sqrt, bias=eps[:, 0:1], scale=1.0 / LRU).then_inc(S["ln_chain"], 1)
            act.wait_ge(S["yn_ready"], 1)
            act.activation(gc, za, ACT.Tanh, scale=0.5).then_inc(S["y_th"], 1)
            keep_kv(5, kvtok)
            act.wait_ge(S["rows_kept"], 3)
            z3, g3, h3 = rows_out[0:11, 0:512], rows_out[0:38, 512:1024], tok[0:9, 2, 0:512]
            for dst, src in ((outs["lru_conv_prompt"][0, 0], z3[0:3, :]), (outs["cache_lru"][0, :, LW - 2, :], z3[3:11, :]),
                             (outs["cf_conv_prompt"][0, 0], g3[0:30, :]), (outs["cache_cf"][0, :, CW - 2, :], g3[30:38, :]),
                             (outs["lru_h_prompt"][0], h3[0:1, :]), (outs["lru_h_sample"][0], h3[1:9, :])):
                act.dma_start(dst, src).then_inc(S["rows_stored"], 16)
            act.wait_ge(S["rows_stored"], 16 * 6)
            for k in range(KD):
                act.wait_ge(S["res_added"], k + 1)
                act.activation(sq[:, k, :], xT[:, k, :], ACT.Square).then_inc(S["x_squared"], 1)
            root(1)
            for o in range(KD):
                wait_tile(act, "q", "q_done", o)
                act.activation(qT[:, o, :], ps[o % 4][:, 0:TOK], ACT.Copy, scale=HD ** -0.5).then_inc(S["q_kept"], 1)
            for i in range(2):
                act.wait_ge(S["qs_turned"], i + 1)
                act.activation(qs[0:NB, 512 * i:512 * i + 512], ps[(4, 7)[i]][0:NB, :], ACT.Copy).then_inc(S["qs_kept"], 1)
            act.wait_ge(S["qs_kept"], 2)
            for g in range(2):
                act.dma_start(qrow[0:97:32, D * g:D * g + D], qs[4 * g:4 * g + 4, :]).then_inc(S["qrow_loaded"], 16)
            for h in range(H):
                act.wait_ge(S["mx_ready"], h + 1)
                for t in range(2):
                    act.activation(pm[:, h, t, :], ps[h][:, NMEM * t:NMEM * t + NMEM], ACT.Exp,
                                   bias=mxn[:, 2 * h + t:2 * h + t + 1],
                                   accum_out=rs[:, 2 * h + t:2 * h + t + 1]).then_inc(S["p_exp"], 1)
            for h in range(H):
                act.wait_ge(S["mx_ready"], H + h + 1)
                for t in range(2):
                    m = act.activation(pm[:, h, t, :], pm[:, h, t, :], ACT.Copy, scale=rs[:, 2 * h + t:2 * h + t + 1])
                m.then_inc(S["p_scaled"], 1)
            for j in range(6, 8):
                keep_kv(j, kvtok)
            act.wait_ge(S["kv_kept"], 8)
            act.dma_start(outs["mem_v"][0, 0].rearrange("(t p) h d -> p t (h d)", p=P), kvtok).then_inc(S["kv_stored"], 16)
            for h in range(H):
                act.wait_ge(S["pt_turned"], h + 1)
                act.activation(pT[:, h, :, :], ps[6 + h % 2][:, :].rearrange("p (m t) -> p m t", m=2), ACT.Copy).then_inc(S["pt_kept"], 1)
            def keep_head(h):
                act.wait_ge(S["pv_done"], h + 1)
                act.activation(oT[:, 2 * h:2 * h + 2, 0:SEQ], ps[h][:, :].rearrange("p (m t) -> p m t", m=2),
                               ACT.Copy).then_inc(S["pv_kept"], 1)

            keep_head(0)
            keep_head(1)
            act.wait_ge(S["smax_ready"], 1)
            act.activation(psS[0:32, :], ps[6][0:32, 0:256], ACT.Exp, bias=smx[0:32, :], accum_out=ssum[0:32, :]).then_inc(S["s_exp"], 1)
            keep_head(2)
            act.wait_ge(S["sp_turned"], 1)
            act.activation(psT, ps[7][:, 0:64].rearrange("p (m c) -> p m c", m=2), ACT.Copy).then_inc(S["sp_kept"], 1)
            for i in range(2):
                act.wait_ge(S["spv_done"], 1)
                act.activation(osb[:, 0, 512 * i:512 * i + 512], ps[4 + i][:, :], ACT.Copy).then_inc(S["osb_kept"], 1)
            keep_head(3)
            act.wait_ge(S["picked"], 1)
            act.activation(oT[:, :, SEQ:TOK], ps[0][:, 0:64].rearrange("p (c b) -> p c b", b=NB), ACT.Copy).then_inc(S["spv_kept"], 1)
            act.activation(unused, eps[:, 0:1], ACT.Sqrt)
            for t, (t0, rows) in enumerate(TT):
                act.wait_ge(S["tokr_kept"], 2 * t + 2)
                act.activation(xnt[0:rows, t, :], tok[0:rows, t, :], ACT.Square,
                               accum_out=tss[0:rows, t:t + 1]).then_inc(S["tok_squared"], 1)
            act.wait_ge(S["tok_squared"], 3)
            act.activation(trs, tss, ACT.Sqrt, bias=eps[:, 0:1], scale=1.0 / D).then_inc(S["tok_rooted"], 1)
            act.wait_ge(S["v0_ready"], 1)
            for t in range(3):
                act.activation(ge[:, t, :], m8[:, t, 0:4], ACT.Exp, bias=nv0[:, t:t + 1],
                               accum_out=gsum[:, t:t + 1]).then_inc(S["ge_ready"], 1)
            act.wait_ge(S["tok_rooted"], 2)
            for t, (t0, rows) in enumerate(TT):
                for i in range(2):
                    j = 6 + 2 * t + i
                    act.wait_ge(S["tm_turned"], j + 1)
                    act.activation(xnt[0:rows, t, 512 * i:512 * i + 512], ps[TURN_BANK[j % 4]][0:rows, :], ACT.Copy,
                                   scale=trs[0:rows, t:t + 1]).then_inc(S["xnt_kept"], 1)
            act.dma_start(be2[0:NE, :], a["b_e2"][0]).then_inc(S["be2_loaded"], 16)
            act.dma_start(gfin, a["g_final"].partition_broadcast(P)).then_inc(S["gfin_loaded"], 16)
            act.wait_ge(S["gt0_turned"], 1)
            act.activation(gateT, ps[4][0:NE, 0:TOK], ACT.Copy).then_inc(S["gt0_kept"], 1)

            def keep_gathered(q):
                act.wait_ge(S["gathered"], q + 1)
                for i in range(2):
                    m = act.activation(xeT[:, 4 * i:4 * i + 4, :], ps[4 + i][:, :].rearrange("p (k s) -> p k s", k=4), ACT.Copy)
                m.then_inc(S["xe_ready"], 1)

            def keep_gates(q):
                act.wait_ge(S["gt_turned"], q + 1)
                act.activation(gT[:, 0:TOK], ps[2][:, 0:TOK], ACT.Copy).then_inc(S["gt_ready"], 1)

            def half_swish(b):
                act.wait_ge(S["g_clamped"], b + 1)
                act.activation(tg, g1, ACT.Tanh, scale=ALPHA / 2).then_inc(S["t_done"], 1)

            def keep_h(b):
                act.wait_ge(S["h_turned"], b + 1)
                act.activation(hT, ps[2][:, :], ACT.Copy, scale=0.5).then_inc(S["hT_ready"], 1)

            def keep_y(b, e2):
                act.wait_ge(S["freed"], RING * b + (freed_after(MOE0 - 1) + RING))
                for i in range(2):
                    m = act.activation(ysb[CAP * e2:CAP * e2 + CAP, 512 * i:512 * i + 512],
                                       ps[3][CAP * i:CAP * i + CAP, :], ACT.Copy)
                m.then_inc(S["y_ready"], 1)

            keep_gathered(0)
            with act.Fori(0, PAIRS) as q:
                half_swish(2 * q)
                keep_h(2 * q)
                keep_y(2 * q, 0)
                keep_gates(q)
                half_swish(2 * q + 1)
                keep_h(2 * q + 1)
                keep_gathered(q + 1)
                keep_y(2 * q + 1, 1)
            act.wait_ge(S["nblk_ready"], 1)
            n = act.value_load(nblk[0:1, 0:1], min_val=0, max_val=P)
            with act.If(n > 0):
                act.wait_ge(S["tab_turned"], 1)
                act.activation(tabrow, ps[5][0:1, 0:P], ACT.Copy).then_inc(S["tab_ready"], 1)
                with act.Fori(0, n) as j:
                    keep_gathered(j + (PAIRS + 1))
                    half_swish(j + NE)
                    keep_gates(j + PAIRS)
                    keep_h(j + NE)
                    keep_y(j + NE, 0)
            act.wait_ge(S["fin_rec"], 1)
            for t, (t0, rows) in enumerate(TT):
                act.wait_ge(S["acc_done"], 3 * n + (3 * (PAIRS + 1) - 2 + t))
                act.activation(xnt[0:rows, t, :], tok[0:rows, t, :], ACT.Square,
                               accum_out=fss[0:rows, t:t + 1]).then_inc(S["fin_sq"], 1)
                act.wait_ge(S["fin_sq"], t + 1)
                act.activation(frs[:, t:t + 1], fss[:, t:t + 1], ACT.Sqrt, bias=eps[:, 0:1], scale=1.0 / D).then_inc(S["fin_sd"], 1)

        @block.vector
        def _(dve):
            for k in range(KD):
                dve.wait_ge(S["x_turned"], k + 1)
                dve.tensor_copy(xT[:, k, :], ps[k % 4][:, 0:TOK]).then_inc(S["x_copied"], 1)
            dve.wait_ge(S["sd_ready"], 1)
            dve.reciprocal(rstd[:, :], rstd[:, :]).then_inc(S["rstd_ready"], 1)
            dve.wait_ge(S["par_turned"], 1)
            dve.tensor_copy(par[:, :], ps[4][:, 0:NPAR]).then_inc(S["par_ready"], 1)
            dve.wait_ge(S["par_ready"], 1)
            lam = par[:, C_LAM:C_LAM + 4]
            dve.tensor_scalar(sp_t, lam, -1.0, None, ALU.mult).then_inc(S["sp_chain"], 1)
            dve.tensor_scalar(hba, par[:, C_BA:C_BA + 4], 0.5, None, ALU.mult).then_inc(S["sp_chain"], 1)
            dve.tensor_scalar(hbx, par[:, C_BX:C_BX + 4], 0.5, None, ALU.mult).then_inc(S["sp_chain"], 1)
            dve.wait_ge(S["sp_chain"], 3)
            dve.tensor_tensor(spn, lam, sp_t, ALU.min).then_inc(S["par_ready"], 1)

            def norm(n, gain):
                if n:
                    dve.wait_ge(S["sd_ready"], n + 1)
                    dve.reciprocal(rstd[:, :], rstd[:, :]).then_inc(S["rstd_ready"], 1)
                dve.wait_ge(S["rstd_ready"], n + 1)
                for k in range(KD):
                    dve.scalar_tensor_tensor(out=xn[:, k, :], in0=xT[:, k, :], scalar=par[:, gain + k:gain + k + 1],
                                             in1=rstd[:, :], op0=ALU.mult, op1=ALU.mult).then_inc(S["xn_ready"], 1)

            dve.wait_ge(S["x_copied"], KD)
            norm(0, C_GMIX)
            dve.wait_ge(S["mem_sd"], 1)
            dve.reciprocal(rm, rm).then_inc(S["mem_rec"], 1)
            dve.wait_ge(S["mem_rec"], 1)
            for t in range(2):
                dve.tensor_scalar(mem[:, t, :], mem[:, t, :], rm[:, t:t + 1], None, ALU.mult).then_inc(S["mem_scaled"], 1)
            dve.wait_ge(S["cc_loaded"], 16 * 5)
            dve.wait_ge(S["lc_loaded"], 16 * 9)
            for t in range(2):
                dve.tensor_tensor(ccache[:, t, :], ccache[:, t, :], wcrep, ALU.mult).then_inc(S["prods"], 1)
            dve.tensor_tensor(lcache, lcache, wlrep, ALU.mult).then_inc(S["prods"], 1)
            n_sp = [3]

            def sp_step(ins):
                n_sp[0] += 1
                ins.then_inc(S["sp_chain"], 1)
                dve.wait_ge(S["sp_chain"], n_sp[0])

            dve.wait_ge(S["sp_exp"], 1)
            sp_step(dve.tensor_scalar(sp_q, sp_e, 2.0, None, ALU.add))
            sp_step(dve.reciprocal(sp_q, sp_q))
            sp_step(dve.tensor_tensor(sp_z, sp_e, sp_q, ALU.mult))
            sp_step(dve.tensor_tensor(sp_e, sp_z, sp_z, ALU.mult))
            sp_step(dve.tensor_scalar(sp_q, sp_e, 1.0 / 15, None, ALU.mult))
            for odd in (13, 11, 9, 7, 5, 3):
                sp_step(dve.scalar_tensor_tensor(out=sp_q, in0=sp_q, scalar=1.0 / odd, in1=sp_e, op0=ALU.add, op1=ALU.mult))
            sp_step(dve.scalar_tensor_tensor(out=sp_q, in0=sp_q, scalar=1.0, in1=sp_z, op0=ALU.add, op1=ALU.mult))
            sp_step(dve.tensor_scalar(sp_t, sp_t, 0.0, None, ALU.max))
            sp_step(dve.scalar_tensor_tensor(out=sp_q, in0=sp_q, scalar=2.0, in1=sp_t, op0=ALU.mult, op1=ALU.add))
            dve.tensor_scalar(spn, sp_q, -4.0, None, ALU.mult).then_inc(S["sp_chain"], 1)
            dve.wait_ge(S["sp_chain"], n_sp[0] + 1)
            dve.tensor_scalar(spp, sp_q, 4.0, None, ALU.mult).then_inc(S["sp_ready"], 1)

            dve.wait_ge(S["zeroed"], 4)
            for c in range(LC):
                dve.wait_ge(S["in_kept"], 5 + c)
                dve.scalar_tensor_tensor(out=gpad[:, c, 30:30 + TOK], in0=th[:, c, :], scalar=1.0, in1=za[:, c, :],
                                         op0=ALU.add, op1=ALU.mult).then_inc(S["glu_ready"], 1)
            dve.wait_ge(S["glu_ready"], 4)
            for c in range(LC):
                dve.tensor_scalar(gc[:, c, 0:SEQ], gpad[:, c, 0:SEQ], par[:, C_WCF + c:C_WCF + c + 1],
                                  par[:, C_BCF + c:C_BCF + c + 1], ALU.mult, ALU.add).then_inc(S["cf_tap"], 1)
            with dve.Fori(1, CW) as w:
                for c in range(LC):
                    dve.wait_ge(S["cf_tap"], 4 * w + (c - 3))
                    dve.scalar_tensor_tensor(out=gc[:, c, 0:SEQ], in0=gpad[:, c, bass.ds(w, SEQ)],
                                             scalar=par[:, bass.ds(4 * w + (C_WCF + c), 1)], in1=gc[:, c, 0:SEQ],
                                             op0=ALU.mult, op1=ALU.add).then_inc(S["cf_tap"], 1)
            dve.wait_ge(S["in_kept"], 12)
            for w in range(LW):
                for c in range(LC):
                    src, tap = xpad[:, c, w:w + SEQ], par[:, C_WL + 4 * w + c:C_WL + 4 * w + c + 1]
                    if w == 0:
                        dve.tensor_scalar(xc[:, c, 0:SEQ], src, tap, par[:, C_BLC + c:C_BLC + c + 1],
                                          ALU.mult, ALU.add).then_inc(S["l_tap"], 1)
                        continue
                    dve.wait_ge(S["l_tap"], 4 * w + c - 3)
                    dve.scalar_tensor_tensor(out=xc[:, c, 0:SEQ], in0=src, scalar=tap, in1=xc[:, c, 0:SEQ],
                                             op0=ALU.mult, op1=ALU.add).then_inc(S["l_tap"], 1)
            for c in range(LC):
                dve.tensor_scalar(xc[:, c, SEQ:TOK], xpad[:, c, 3 + SEQ:3 + TOK], par[:, C_WL + 12 + c:C_WL + 13 + c],
                                  par[:, C_BLC + c:C_BLC + c + 1], ALU.mult, ALU.add).then_inc(S["l_smp"], 1)
                dve.tensor_scalar(gc[:, c, SEQ:TOK], gpad[:, c, 30 + SEQ:30 + TOK],
                                  par[:, C_WCF + 120 + c:C_WCF + 121 + c],
                                  par[:, C_BCF + c:C_BCF + c + 1], ALU.mult, ALU.add).then_inc(S["l_smp"], 1)
            dve.wait_ge(S["l_smp"], 8)
            dve.wait_ge(S["freed"], freed_after(0))
            dve.tensor_tensor(xc[:, :, SEQ:TOK], xc[:, :, SEQ:TOK],
                              ps[4][:, 32:64].rearrange("p (c b) -> p c b", b=NB), ALU.add).then_inc(S["l_smp"], 1)
            dve.tensor_tensor(gc[:, :, SEQ:TOK], gc[:, :, SEQ:TOK],
                              ps[4][:, 0:32].rearrange("p (c b) -> p c b", b=NB), ALU.add).then_inc(S["cf_smp"], 1)
            dve.wait_ge(S["gelu_sq"], 1)
            dve.tensor_scalar(uv, uv, GELU_A, 1.0, ALU.mult, ALU.add).then_inc(S["gelu_in"], 1)
            dve.wait_ge(S["gelu_in"], 1)
            dve.tensor_tensor(uv, uv, zg, ALU.mult).then_inc(S["gelu_in"], 1)
            dve.wait_ge(S["gelu_th"], 1)
            dve.scalar_tensor_tensor(out=zg, in0=uv, scalar=1.0, in1=zg, op0=ALU.add, op1=ALU.mult).then_inc(S["gelu_g"], 1)
            dve.wait_ge(S["mu_done"], 1)
            dve.scalar_tensor_tensor(out=za, in0=ps[5][:, 0:TOK].unsqueeze(1).to_broadcast([P, LC, TOK]),
                                     scalar=-1.0 / LRU, in1=gc, op0=ALU.mult, op1=ALU.add).then_inc(S["gc_cent"], 1)
            dve.wait_ge(S["gate_tanh"], 8)
            dve.wait_ge(S["gelu_g"], 1)
            dve.wait_ge(S["a_ready"], 4)
            dve.scalar_tensor_tensor(out=ti, in0=ti, scalar=1.0, in1=xc, op0=ALU.add, op1=ALU.mult).then_inc(S["beta_chain"], 1)
            dve.tensor_tensor(uv, av, av, ALU.mult).then_inc(S["beta_chain"], 1)
            dve.wait_ge(S["beta_chain"], 2)
            dve.wait_ge(S["t_ready"], 4)
            dve.scalar_tensor_tensor(out=tr, in0=uv, scalar=1.0, in1=tr, op0=ALU.add, op1=ALU.mult).then_inc(S["beta_chain"], 1)
            dve.wait_ge(S["t_ready"], 5)
            dve.scalar_tensor_tensor(out=uv, in0=tr, scalar=0.5, in1=ti, op0=ALU.mult, op1=ALU.mult).then_inc(S["u_ready"], 1)
            dve.wait_ge(S["u_ready"], 1)
            for c in range(LC):
                dve.tensor_tensor_scan(hs[:, c, 0:SEQ], av[:, c, 0:SEQ], uv[:, c, 0:SEQ], 0.0,
                                       ALU.mult, ALU.add).then_inc(S["scan_ready"], 1)
            dve.tensor_tensor(hs[:, :, SEQ:TOK], av[:, :, SEQ:TOK],
                              par[:, C_H0:C_H0 + 32].rearrange("p (c b) -> p c b", b=NB), ALU.mult).then_inc(S["scan_ready"], 1)
            dve.wait_ge(S["scan_ready"], 5)
            dve.tensor_tensor(hs[:, :, SEQ:TOK], hs[:, :, SEQ:TOK], uv[:, :, SEQ:TOK], ALU.add).then_inc(S["scan_ready"], 1)
            dve.wait_ge(S["scan_ready"], 6)
            dve.scalar_tensor_tensor(out=zg, in0=zg, scalar=0.5, in1=hs, op0=ALU.mult, op1=ALU.mult).then_inc(S["ylru_ready"], 1)
            dve.wait_ge(S["ln_chain"], 1)
            dve.reciprocal(rstd[:, :], rstd[:, :]).then_inc(S["ln_chain"], 1)
            dve.wait_ge(S["ln_chain"], 2)
            dve.tensor_tensor(za, za, rstd[:, :].unsqueeze(1).to_broadcast([P, LC, TOK]), ALU.mult).then_inc(S["ln_chain"], 1)
            dve.wait_ge(S["ln_chain"], 3)
            for c in range(LC):
                last = dve.tensor_scalar(za[:, c, :], za[:, c, :], par[:, C_GLN + c:C_GLN + c + 1],
                                         par[:, C_BLN + c:C_BLN + c + 1], ALU.mult, ALU.add)
            last.then_inc(S["yn_ready"], 1)
            dve.wait_ge(S["y_th"], 1)
            dve.tensor_scalar(gc, gc, 1.0, 0.5, ALU.add, ALU.mult).then_inc(S["ln_chain"], 1)
            dve.wait_ge(S["ln_chain"], 4)
            dve.tensor_tensor(gc, gc, za, ALU.mult).then_inc(S["ycf_ready"], 1)
            dve.wait_ge(S["rows_turned"], 1)
            dve.tensor_copy(rows_out[0:11, 0:512], ps[6][0:11, :]).then_inc(S["rows_kept"], 1)
            dve.wait_ge(S["rows_turned"], 2)
            dve.tensor_copy(rows_out[0:38, 512:1024], ps[7][0:38, :]).then_inc(S["rows_kept"], 1)
            dve.wait_ge(S["rows_turned"], 3)
            dve.tensor_copy(tok[0:9, 2, 0:512], ps[4][0:9, :]).then_inc(S["rows_kept"], 1)

            def residual(kind, done, base, gain=None):
                for o in range(KD):
                    wait_tile(dve, kind, done, o)
                    dve.tensor_tensor(xT[:, o, :], xT[:, o, :], ps[o % 4][:, 0:TOK], ALU.add).then_inc(S["res_added"], 1)
                    if gain is not None:
                        dve.wait_ge(S["res_added"], base + o + 1)
                        dve.tensor_scalar(xn[:, o, :], xT[:, o, :], par[:, gain + o:gain + o + 1], None,
                                          ALU.mult).then_inc(S["xn_ready"], 1)
                dve.wait_ge(S["res_added"], base + KD)

            residual("out", "out_done", 0)
            norm(1, C_GXA)
            def largest(h):
                dve.wait_ge(S["score_done"], h + 1)
                dve.tensor_reduce(mxn[:, 2 * h:2 * h + 2], ps[h][:, :].rearrange("p (t m) -> p t m", t=2), AX.X,
                                  ALU.max, negate=True).then_inc(S["mx_ready"], 1)

            def over_sum(h):
                dve.wait_ge(S["p_exp"], 2 * h + 2)
                dve.reciprocal(rs[:, 2 * h:2 * h + 2], rs[:, 2 * h:2 * h + 2]).then_inc(S["mx_ready"], 1)

            def dots(b):
                n = START["kc"] + b
                dve.wait_ge(filled[n % RING], 16 * fills_before(n))
                dve.wait_ge(S["qb_ready"], b + 1)
                key = slot(n).rearrange("p (t h d) -> p t h d", t=2, h=H)
                for t in range(2):
                    for h in range(H):
                        q = qb[:, b % 2, HD * h:HD * h + HD]
                        last = dve.tensor_tensor_reduce(key[:, t, h, :], key[:, t, h, :], q, 1.0, 0.0, ALU.mult, ALU.add,
                                                        sT[:, t, 4 * b + h:4 * b + h + 1])
                last.then_inc(S["kc_freed"], 1)

            largest(0)
            largest(1)
            dots(0)
            largest(2)
            largest(3)
            dots(1)
            for h in range(H):
                over_sum(h)
            for b in range(2, NB):
                dots(b)
            dve.wait_ge(S["s_turned"], 1)
            dve.tensor_reduce(smx[0:32, :], ps[6][0:32, 0:256], AX.X, ALU.max, negate=True).then_inc(S["smax_ready"], 1)
            dve.wait_ge(S["s_exp"], 1)
            dve.reciprocal(ssum[0:32, :], ssum[0:32, :]).then_inc(S["s_scaled"], 1)
            dve.wait_ge(S["s_scaled"], 1)
            dve.tensor_scalar(psS[0:32, :], psS[0:32, :], ssum[0:32, :], None, ALU.mult).then_inc(S["s_scaled"], 1)
            dve.wait_ge(S["spv_done"], 2)
            for i in range(2):
                dve.tensor_copy(osb[:, 1, 512 * i:512 * i + 512], ps[6 + i][:, :]).then_inc(S["osb_kept"], 1)
            residual("o", "o_done", KD, C_GMOE)
            dve.wait_ge(S["kv_stored"], 32)
            dve.wait_ge(S["rows_stored"], 16 * 6)
            for t, (t0, rows) in enumerate(TT):
                for i in range(2):
                    j = 2 * t + i
                    dve.wait_ge(S["tm_turned"], j + 1)
                    dve.tensor_copy(tok[0:rows, t, 512 * i:512 * i + 512], ps[TURN_BANK[j % 4]][0:rows, :]).then_inc(S["tokr_kept"], 1)
            dve.wait_ge(S["lg_zeroed"], 1)
            dve.wait_ge(S["tok_rooted"], 1)
            dve.reciprocal(trs, trs).then_inc(S["tok_rooted"], 1)
            dve.wait_ge(S["tok_rooted"], 2)
            dve.wait_ge(S["logit_done"], 1)
            dve.wait_ge(S["router_loaded"], 32)
            for t, (t0, rows) in enumerate(TT):
                dve.scalar_tensor_tensor(out=lg[0:rows, t, :], in0=ps[4][0:rows, NE * t:NE * t + NE], scalar=trs[0:rows, t:t + 1],
                                         in1=brout[0:rows, :], op0=ALU.mult, op1=ALU.add).then_inc(S["lg_ready"], 1)
            dve.wait_ge(S["lg_ready"], 3)
            for t in range(3):
                dve.max(m8[:, t, :], lg[:, t, :]).then_inc(S["lg_ready"], 1)
            dve.wait_ge(S["lg_ready"], 6)
            dve.tensor_scalar(nv0, m8[:, :, 0], -1.0, None, ALU.mult).then_inc(S["v0_ready"], 1)
            for t in range(3):
                dve.max_index(nm8[:, t, :], m8[:, t, :], lg[:, t, :]).then_inc(S["idx_ready"], 1)
            dve.wait_ge(S["idx_ready"], 3)
            dve.tensor_copy(idf, nm8[:, :, :]).then_inc(S["idx_ready"], 1)
            dve.wait_ge(S["idx_ready"], 4)
            wide = [P, 3, 4, NE]
            dve.tensor_tensor(eq, iota_e[:, :].unsqueeze(1).unsqueeze(1).to_broadcast(wide),
                              idf[:, :, 0:4].unsqueeze(3).to_broadcast(wide), ALU.is_equal).then_inc(S["eq_ready"], 1)
            dve.wait_ge(S["eq_ready"], 1)
            dve.tensor_reduce(mask, eq.rearrange("p t k e -> p t e k"), AX.X, ALU.add).then_inc(S["mask_ready"], 1)
            dve.wait_ge(S["ge_ready"], 3)
            dve.reciprocal(grec, gsum).then_inc(S["gate_chain"], 1)
            dve.wait_ge(S["gate_chain"], 1)
            dve.tensor_tensor(ge, ge, grec.unsqueeze(2).to_broadcast([P, 3, 4]), ALU.mult).then_inc(S["gate_chain"], 1)
            dve.wait_ge(S["gate_chain"], 2)
            dve.tensor_tensor(eq, eq, ge.unsqueeze(3).to_broadcast(wide), ALU.mult).then_inc(S["gate_chain"], 1)
            dve.wait_ge(S["gate_chain"], 3)
            dve.tensor_reduce(gcol, eq.rearrange("p t k e -> p t e k"), AX.X, ALU.add).then_inc(S["gate_chain"], 1)
            dve.wait_ge(S["mask_ready"], 1)
            dve.tensor_scalar(rk, mask, -BIG, BIG, ALU.mult, ALU.add).then_inc(S["rank_chain"], 1)
            dve.wait_ge(S["rank_chain"], 1)
            dve.wait_ge(S["rank_done"], 1)
            dve.tensor_tensor(rkp[:, 0:2, 0:NE], rk[:, 0:2, :], ps[5][:, 0:2 * NE].rearrange("p (t e) -> p t e", t=2),
                              ALU.add).then_inc(S["rank_chain"], 1)
            dve.tensor_tensor(rkp[0:NB, 2, 0:NE], rk[0:NB, 2, :], ps[5][0:NB, 2 * NE:3 * NE], ALU.add).then_inc(S["rank_chain"], 1)
            dve.tensor_copy(count, ps[5][:, 96:128]).then_inc(S["rank_chain"], 1)
            dve.wait_ge(S["rank_chain"], 4)
            dve.wait_ge(S["gate_chain"], 4)

            def one_hot(cols):
                for t, (t0, rows) in enumerate(TT):
                    for i, col in enumerate(cols):
                        last = dve.tensor_scalar(sel[0:rows, t, CAP * i:CAP * i + CAP], iota_s[0:rows, 0, :],
                                                 rkp[0:rows, t, bass.ds(col, 1)], None, ALU.is_equal)
                last.then_inc(S["sel_ready"], 1)

            one_hot((0, 1))
            for q in range(1, PASSES):
                dve.tensor_scalar(rkp[:, 0:2, NE * q:NE * q + NE], rkp[:, 0:2, 0:NE], -float(CAP * q), None, ALU.add)
                dve.tensor_scalar(rkp[0:NB, 2, NE * q:NE * q + NE], rkp[0:NB, 2, 0:NE], -float(CAP * q), None,
                                  ALU.add).then_inc(S["rank_chain"], 1)
            dve.tensor_copy(gcp.rearrange("p t (q e) -> p t q e", e=NE),
                            gcol.unsqueeze(2).to_broadcast([P, 3, PASSES, NE])).then_inc(S["gate_chain"], 1)
            n_bc = [0]

            def step(ins):
                n_bc[0] += 1
                ins.then_inc(S["block_chain"], 1)
                dve.wait_ge(S["block_chain"], n_bc[0])

            for q in range(1, PASSES):
                last = dve.tensor_scalar(flag[:, NE * (q - 1):NE * q], count, float(CAP * q), None, ALU.is_gt)
            step(last)
            step(dve.tensor_tensor_scan(scan, ones[:, :], flag, 0.0, ALU.mult, ALU.add))
            dve.tensor_copy(nblk[0:1, 0:1], scan[0:1, P - 1:P]).then_inc(S["nblk_ready"], 1)
            step(dve.tensor_reduce(tbc, before[:, :], AX.X, ALU.add))
            step(dve.tensor_scalar(tbc, tbc, -1.0, float(P), ALU.mult, ALU.add))
            step(dve.tensor_scalar(tb, scan, tbc, None, ALU.is_equal))
            step(dve.tensor_tensor(tb, tb, flag, ALU.mult))
            step(dve.tensor_tensor_scan(iota_b, ones[:, :], ones[:, :], -1.0, ALU.mult, ALU.add))
            step(dve.tensor_tensor(tb, tb, iota_b, ALU.mult))
            dve.tensor_reduce(tbc, tb, AX.X, ALU.add).then_inc(S["tab_ready"], 1)
            dve.memset(fss, 0.0).then_inc(S["fin_rec"], 1)
            dve.wait_ge(S["rank_chain"], 4 + PASSES - 1)
            dve.wait_ge(S["gate_chain"], 5)
            dve.wait_ge(S["tokr_kept"], 6)

            def add_round(first, t, bank=6):
                rows = TT[t][1]
                dve.wait_ge(S["comb_done"], first + (t + 1))
                for i in range(2):
                    dst = tok[0:rows, t, 512 * i:512 * i + 512]
                    last = dve.tensor_tensor(dst, dst, ps[bank + i][0:rows, :], ALU.add)
                last.then_inc(S["acc_done"], 1)

            def gated(cols):
                for t, (t0, rows) in enumerate(TT):
                    for i, col in enumerate(cols):
                        last = dve.tensor_scalar(selg[0:rows, t, CAP * i:CAP * i + CAP], iota_s[0:rows, 0, :],
                                                 rkp[0:rows, t, bass.ds(col, 1)], gcp[0:rows, t, bass.ds(col, 1)],
                                                 ALU.is_equal, ALU.mult)
                last.then_inc(S["selg_ready"], 1)

            def swiglu(b):
                dve.wait_ge(S["freed"], RING * b + (freed_after(MOE0 - 1) + W_SLOTS))
                dve.tensor_scalar(g1, ps[0][:, :], LIMIT, None, ALU.min).then_inc(S["g_clamped"], 1)
                dve.tensor_scalar(u1, ps[1][:, :], -LIMIT, LIMIT, ALU.max, ALU.min).then_inc(S["u_clamped"], 1)
                dve.wait_ge(S["t_done"], b + 1)
                dve.scalar_tensor_tensor(out=tg, in0=tg, scalar=1.0, in1=g1, op0=ALU.add, op1=ALU.mult).then_inc(S["tu_done"], 1)
                dve.wait_ge(S["tu_done"], b + 1)
                dve.wait_ge(S["u_clamped"], b + 1)
                dve.scalar_tensor_tensor(out=hh, in0=u1, scalar=1.0, in1=tg, op0=ALU.add, op1=ALU.mult).then_inc(S["h_ready"], 1)

            def next_pair(q):
                dve.wait_ge(S["gathered"], q + 1)
                one_hot((2 * q + 2, 2 * q + 3))
                gated((2 * q, 2 * q + 1))

            swiglu(0)
            next_pair(0)
            swiglu(1)
            for t in range(3):
                add_round(0, t)
            with dve.Fori(1, PAIRS) as q:
                add_round(3 * q, 0)
                swiglu(2 * q)
                add_round(3 * q, 1)
                add_round(3 * q, 2)
                next_pair(q)
                swiglu(2 * q + 1)
            for t in range(3):
                add_round(3 * PAIRS, t, LAST_BANKS[t])
            n = dve.value_load(nblk[0:1, 0:1], min_val=0, max_val=P)
            with dve.If(n > 0):
                dve.wait_ge(S["tab_ready"], 2)
                dve.tensor_copy(tabi[0:1, 1, :], tabrow).then_inc(S["block_chain"], 1)
                dve.wait_ge(S["block_chain"], n_bc[0] + 1)
                dve.tensor_scalar(tabi[0:1, 0, :], tabi[0:1, 1, :], NE - 1, None, ALU.bitwise_and).then_inc(S["block_chain"], 1)
                dve.tensor_scalar(tabrow, tabrow, float(NE), None, ALU.add).then_inc(S["block_chain"], 1)
                dve.wait_ge(S["block_chain"], n_bc[0] + 3)
                dve.tensor_copy(tabi[0:1, 1, :], tabrow).then_inc(S["table_ready"], 1)
                dve.wait_ge(S["table_ready"], 1)
                dve.wait_ge(S["gathered"], PAIRS + 1)
                dve.memset(sel[:, :, CAP:2 * CAP], 0.0)
                dve.memset(selg[:, :, CAP:2 * CAP], 0.0)
                with dve.Fori(0, n) as j:
                    col = dve.value_load(tabi[0:1, 1, bass.ds(j, 1)], min_val=NE, max_val=NCOL - 1)
                    dve.wait_ge(S["gathered"], j + (PAIRS + 1))
                    one_hot((col,))
                    gated((col,))
                    swiglu(j + NE)
                    for t in range(3):
                        add_round(3 * j + 3 * (PAIRS + 1), t)
            dve.wait_ge(S["gfin_loaded"], 16)
            for t, (t0, rows) in enumerate(TT):
                r = slice(0, rows)
                dve.wait_ge(S["fin_sd"], t + 1)
                dve.reciprocal(frs[:, t:t + 1], frs[:, t:t + 1]).then_inc(S["fin_rec"], 1)
                dve.wait_ge(S["fin_rec"], t + 2)
                dve.scalar_tensor_tensor(out=tok[r, t, :], in0=tok[r, t, :], scalar=frs[r, t:t + 1], in1=gfin[r, :],
                                         op0=ALU.mult, op1=ALU.mult).then_inc(S["fin_ready"], 1)

        @block.tensor
        def _(pe):
            pe.wait_ge(S["ident_ready"], 2)
            pe.wait_ge(S["x_loaded"], 32)
            for k in range(KD):
                if k >= 4:
                    pe.wait_ge(S["x_copied"], k - 3)
                for t, (t0, rows) in enumerate(TT):
                    m = pe.transpose(ps[k % 4][:, t0:t0 + rows], x0[0:rows, t, k * P:(k + 1) * P], ident[0:rows, 0:rows])
                m.then_inc(S["x_turned"], 1)
            def norm_sum(n):
                for k in range(KD):
                    pe.wait_ge(S["x_squared"], KD * n + k + 1)
                    m = pe.matmul(ps[5][:, 0:TOK], ones[:, :], sq[:, k, :], start=(k == 0), stop=(k == KD - 1))
                m.then_inc(S["sum_done"], 1)

            pe.wait_ge(S["consts"], 2)
            norm_sum(0)
            pe.wait_ge(S["par_loaded"], n_par)
            pe.wait_ge(S["h0_loaded"], 16)
            pe.transpose(ps[4][:, 0:C_B], stage_a[0:C_B, :], ident[0:C_B, 0:C_B])
            pe.transpose(ps[4][:, C_B:C_H0], stage_b[0:B_ROWS, :], ident[0:B_ROWS, 0:B_ROWS])
            for c in range(LC):
                m = pe.transpose(ps[4][:, C_H0 + NB * c:C_H0 + NB * c + NB], stage_h[:, c * P:(c + 1) * P], ident[0:NB, 0:NB])
            m.then_inc(S["par_turned"], 1)

            def small_inputs():
                pe.wait_ge(S["mem_scaled"], 2)
                for j in range(4):
                    if j >= 2:
                        pe.wait_ge(S["mem_ready"], 2 * (j - 1))
                    for i in range(2):
                        for t in range(2):
                            m = pe.transpose(ps[6 + j % 2][:, NMEM * i + P * t:NMEM * i + P * t + P],
                                             mem[:, t, (2 * j + i) * P:(2 * j + i + 1) * P], ident[:, :])
                    m.then_inc(S["mem_turned"], 1)
                pe.wait_ge(S["prods"], 3)
                pe.wait_ge(S["par_ready"], 1)
                pe.wait_ge(S["consts"], CONSTS)
                for c in range(LC):
                    for t in range(2):
                        pe.matmul(ps[4][:, NB * c + 4 * t:NB * c + 4 * t + 4], ccache[:, t, c * P:(c + 1) * P], indc[:, :],
                                  start=True, stop=True)
                    m = pe.matmul(ps[4][:, 32 + NB * c:40 + NB * c], lcache[:, c * P:(c + 1) * P], indl[:, :],
                                  start=True, stop=True)
                m.then_inc(S["freed"], HEADROOM)

            def project(kind, done, src, bank_free, first_wait):
                count = dict(FRONT)[kind]
                for i in range(count):
                    n = START[kind] + i
                    if kind == "in" and i == IN_FIRST:
                        small_inputs()
                    pe.wait_ge(filled[n % RING], 16 * fills_before(n))
                    for half in range(2):
                        o = 2 * i + half
                        bank_free(o)
                        for k in range(KD):
                            if i == 0 and half == 0:
                                first_wait(k)
                            m = pe.matmul(ps[o % 4][:, 0:TOK], wslot(n)[:, k, half * P:(half + 1) * P], src(k),
                                          start=(k == 0), stop=(k == KD - 1))
                        m.then_inc(S["freed" if half else done], 1)

            def in_free(o):
                if o >= 4:
                    pe.wait_ge(S["in_kept"], o - 3)

            project("in", "in_done", lambda k: xn[:, k, :], in_free, lambda k: pe.wait_ge(S["xn_ready"], k + 1))

            def kv(j, tiles=(0, 1)):
                n = KV_ENTRY[j]
                pe.wait_ge(filled[n % RING], 16 * fills_before(n))
                for t in tiles:
                    for k in range(KD):
                        m = pe.matmul(ps[KV_BANK[j]][:, 256 * t:256 * t + 256], mn[:, k, P * t:P * t + P],
                                      wslot(n)[:, k, :], start=(k == 0), stop=(k == KD - 1))
                if tiles[-1] == 1:
                    m.then_inc(S["freed"], 1)

            pe.wait_ge(S["mem_ready"], KD)
            for j in range(4):
                if j >= 2:
                    pe.wait_ge(S["kv_kept"], j - 1)
                kv(j)
            pe.wait_ge(S["kv_kept"], 4)
            for j in range(4):
                if j >= 2:
                    pe.wait_ge(S["kt_ready"], j - 1)
                for i in range(2):
                    for t in range(2):
                        m = pe.transpose(ps[6 + j % 2][:, NMEM * i + P * t:NMEM * i + P * t + P],
                                         kvtok[:, t, (2 * j + i) * P:(2 * j + i + 1) * P], ident[:, :])
                m.then_inc(S["kt_turned"], 1)
            pe.wait_ge(S["gate_loaded"], 64)
            pe.wait_ge(S["l_tap"], 16)
            pe.wait_ge(S["l_smp"], 9)
            pe.wait_ge(S["in_kept"], 16)
            for g in range(2):
                for c in range(LC):
                    if g:
                        pe.wait_ge(S["gate_tanh"], c + 1)
                    pe.matmul(ps[c][:, 0:TOK], wgate[:, g, c, :], xc[:, c, :], start=True, stop=True).then_inc(S["gate_done"], 1)
            pe.wait_ge(S["cf_smp"], 1)
            pe.wait_ge(S["cf_tap"], 4 * CW)
            for c in range(LC):
                m = pe.matmul(ps[5][:, 0:TOK], ones[:, :], gc[:, c, :], start=(c == 0), stop=(c == LC - 1))
            m.then_inc(S["mu_done"], 1)
            pe.wait_ge(S["kt_ready"], 4)
            kv(4)
            pe.wait_ge(S["gc_sq"], 1)
            for c in range(LC):
                m = pe.matmul(ps[5][:, 0:TOK], ones[:, :], gc[:, c, :], start=(c == 0), stop=(c == LC - 1))
            m.then_inc(S["var_done"], 1)
            pe.wait_ge(S["kv_kept"], 5)
            for c in range(LC):
                m = pe.transpose(ps[6][0:11, c * P:(c + 1) * P], xpad[:, c, 3 + SEQ - 3:3 + TOK], ident[:, :])
            m.then_inc(S["rows_turned"], 1)
            for c in range(LC):
                m = pe.transpose(ps[7][0:38, c * P:(c + 1) * P], gpad[:, c, 30 + SEQ - 30:30 + TOK], ident[:, :])
            m.then_inc(S["rows_turned"], 1)
            pe.wait_ge(S["scan_ready"], 6)
            for c in range(LC):
                m = pe.transpose(ps[4][0:9, c * P:(c + 1) * P], hs[:, c, SEQ - 1:TOK], ident[:, :])
            m.then_inc(S["rows_turned"], 1)

            pe.wait_ge(S["ln_chain"], 1)
            kv(5)

            def out_free(o):
                if o >= 4:
                    pe.wait_ge(S["res_added"], o - 3)

            pe.wait_ge(S["ylru_ready"], 1)
            pe.wait_ge(S["gate_tanh"], 8)

            def out_wait(k):
                if k == 4:
                    pe.wait_ge(S["ycf_ready"], 1)

            project("out", "out_done", lambda k: zg[:, k, :] if k < 4 else gc[:, k - 4, :], out_free, out_wait)
            pe.wait_ge(S["kv_kept"], 6)
            norm_sum(1)
            pe.wait_ge(S["rows_kept"], 1)
            kv(6, (0,))

            def q_free(o):
                if o < 4:
                    pe.wait_ge(S["res_added"], o + 5)
                else:
                    pe.wait_ge(S["q_kept"], o - 3)

            project("q", "q_done", lambda k: xn[:, k, :], q_free, lambda k: pe.wait_ge(S["xn_ready"], KD + k + 1))
            pe.wait_ge(S["q_kept"], KD)
            pe.wait_ge(S["rows_kept"], 3)
            for i in range(2):
                for c in range(4):
                    m = pe.transpose(ps[(4, 7)[i]][0:NB, c * P:(c + 1) * P], qT[:, 4 * i + c, SEQ:TOK], ident[:, :])
                m.then_inc(S["qs_turned"], 1)
            for h in range(H):
                for t in range(2):
                    for i in range(2):
                        m = pe.matmul(ps[h][:, NMEM * t:NMEM * t + NMEM], qT[:, 2 * h + i, P * t:P * t + P],
                                      kT[:, 2 * h + i, :], start=(i == 0), stop=(i == 1))
                m.then_inc(S["score_done"], 1)
            pe.wait_ge(S["qs_kept"], 2)
            kv(6, (1,))
            kv(7)
            for h in range(H):
                pe.wait_ge(S["p_scaled"], h + 1)
                if h < 2:
                    pe.wait_ge(S["kv_kept"], 7 + h)
                else:
                    pe.wait_ge(S["pt_kept"], h - 1)
                for mt in range(2):
                    for t in range(2):
                        m = pe.transpose(ps[6 + h % 2][:, SEQ * mt + P * t:SEQ * mt + P * t + P],
                                         pm[:, h, t, P * mt:P * mt + P], ident[:, :])
                m.then_inc(S["pt_turned"], 1)
            def values(h):
                pe.wait_ge(S["pt_kept"], h + 1)
                for i in range(2):
                    for mt in range(2):
                        m = pe.matmul(ps[h][:, SEQ * i:SEQ * i + SEQ], kvtok[:, mt, HD * h + P * i:HD * h + P * i + P],
                                      pT[:, h, mt, :], start=(mt == 0), stop=(mt == 1))
                m.then_inc(S["pv_done"], 1)

            values(0)
            values(1)
            pe.wait_ge(S["kc_freed"], NB)
            pe.wait_ge(S["pt_kept"], H)
            for t in range(2):
                m = pe.transpose(ps[6][0:32, P * t:P * t + P], sT[:, t, :], ident[:, :])
            m.then_inc(S["s_turned"], 1)
            values(2)
            pe.wait_ge(S["s_scaled"], 2)
            for t in range(2):
                m = pe.transpose(ps[7][:, 32 * t:32 * t + 32], psS[0:32, P * t:P * t + P], ident[0:32, 0:32])
            m.then_inc(S["sp_turned"], 1)
            pe.wait_ge(S["sp_kept"], 1)
            for g in range(2):
                for b in range(4):
                    n = START["vc"] + 4 * g + b
                    pe.wait_ge(filled[n % RING], 16 * fills_before(n))
                for i in range(2):
                    for t in range(2):
                        for b in range(4):
                            val = slot(START["vc"] + 4 * g + b)
                            m = pe.matmul(ps[4 + 2 * g + i][32 * b:32 * b + 32, :], psT[:, t, :],
                                          val[:, D * t + 512 * i:D * t + 512 * i + 512], start=(t == 0), stop=(t == 1))
                m.then_inc(S["spv_done"], 1)
            pe.wait_ge(S["spv_done"], 2)
            pe.sem_inc(S["freed"], 8)
            values(3)
            pe.wait_ge(S["osb_kept"], 4)
            pe.wait_ge(S["pick_ready"], 2)
            pe.wait_ge(S["pv_kept"], 1)
            for c in range(KD):
                for g in range(2):
                    m = pe.matmul(ps[0][:, NB * c + 4 * g:NB * c + 4 * g + 4], osb[:, g, c * P:(c + 1) * P],
                                  pick[:, g, c // 2, :], start=True, stop=True)
            m.then_inc(S["picked"], 1)
            pe.wait_ge(S["spv_kept"], 1)
            pe.wait_ge(S["pv_kept"], H)

            def o_free(o):
                if o >= 4:
                    pe.wait_ge(S["res_added"], KD + o - 3)

            project("o", "o_done", lambda k: oT[:, k, :], o_free, lambda k: None)
            def turn_tokens(j):
                t, i = (j % 6) // 2, j % 2
                t0, rows = TT[t]
                if j >= 4:
                    pe.wait_ge(S["tokr_kept"], min(j - 3, 6))
                if j >= 10:
                    pe.wait_ge(S["xnt_kept"], j - 9)
                src = xT if j < 6 else xn
                for c in range(4):
                    m = pe.transpose(ps[TURN_BANK[j % 4]][0:rows, c * P:(c + 1) * P], src[:, 4 * i + c, t0:t0 + rows], ident[:, :])
                m.then_inc(S["tm_turned"], 1)

            def up_bias(b):
                pe.wait_ge(S["b1_filled"], 16 * b + 16)
                for gu in range(2):
                    for i in range(2):
                        m = pe.matmul(ps[gu][CAP * i:CAP * i + CAP, :], ones[0:1, 0:CAP],
                                      b1row[0:1, D * gu + 512 * i:D * gu + 512 * i + 512], start=True, stop=False)
                m.then_inc(S["b1_used"], 1)

            pe.wait_ge(S["res_added"], 2 * KD)
            for j in range(6):
                turn_tokens(j)
            pe.wait_ge(S["router_loaded"], 32)
            for t, (t0, rows) in enumerate(TT):
                dst = ps[4][0:rows, NE * t:NE * t + NE]
                for k in range(KD):
                    if t == 0:
                        pe.wait_ge(S["xn_ready"], 2 * KD + k + 1)
                    m = pe.matmul(dst, xn[:, k, t0:t0 + rows], wr[:, k, :], start=(k == 0), stop=(k == KD - 1))
            m.then_inc(S["logit_done"], 1)
            for j in range(6, 10):
                turn_tokens(j)
            up_bias(0)
            pe.wait_ge(S["mask_ready"], 1)
            for t, (t0, rows) in enumerate(TT):
                for i in range(t + 1):
                    n_k = TT[i][1]
                    lhs = before if i == t else ones
                    m = pe.matmul(ps[5][0:rows, NE * t:NE * t + NE], lhs[0:n_k, 0:rows], mask[0:n_k, i, :],
                                  start=(i == 0), stop=(i == t))
            for i, (t0, n_k) in enumerate(TT):
                m = pe.matmul(ps[5][:, 96:128], ones[0:n_k, :], mask[0:n_k, i, :], start=(i == 0), stop=(i == 2))
            m.then_inc(S["rank_done"], 1)
            for j in range(10, 12):
                turn_tokens(j)
            pe.wait_ge(S["gate_chain"], 4)
            for t, (t0, rows) in enumerate(TT):
                m = pe.transpose(ps[4][0:NE, t0:t0 + rows], gcol[0:rows, t, :], ident[0:rows, 0:rows])
            m.then_inc(S["gt0_turned"], 1)

            def rounds(q, t, bank=6):
                t0, rows = TT[t]
                if q is None and t:
                    pe.wait_ge(S["acc_done"], t)
                if q is not None and bank == 6:
                    pe.wait_ge(S["acc_done"], 3 * q + (3 + t))
                for i in range(2):
                    cols = slice(512 * i, 512 * i + 512)
                    if q is None:
                        m = pe.matmul(ps[bank + i][0:rows, :], gateT[:, t0:t0 + rows], be2[0:NE, cols], start=True, stop=True)
                    else:
                        m = pe.matmul(ps[bank + i][:, :], gT[:, t0:t0 + P], ysb[:, cols], start=True, stop=True)
                m.then_inc(S["comb_done"], 1)

            def gather(q, halves=(0, 1)):
                pe.wait_ge(S["sel_ready"], q + 1)
                for i in halves:
                    for k in range(4 * i, 4 * i + 4):
                        for t, (t0, rows) in enumerate(TT):
                            m = pe.matmul(ps[4 + i][:, P * (k % 4):P * (k % 4) + P], xnt[0:rows, t, k * P:(k + 1) * P],
                                          sel[0:rows, t, :], start=(t == 0), stop=(t == 2))
                if halves[-1] == 1:
                    m.then_inc(S["gathered"], 1)

            def turn_gates(q):
                pe.wait_ge(S["selg_ready"], q + 1)
                for t, (t0, rows) in enumerate(TT):
                    m = pe.transpose(ps[2][:, t0:t0 + rows], selg[0:rows, t, :], ident[0:rows, 0:rows])
                m.then_inc(S["gt_turned"], 1)

            def up(b, e2, between, outside=False):
                if not outside:
                    up_bias(b)
                order = list(range(W_SLOTS))
                if outside:
                    order = [k for i in range(HEAD_SLOTS) for k in (HEAD_SLOTS + i, i)]
                for n_done, k in enumerate(order):
                    g_u = (ring[:, k, 0:D], ring[:, k, D:2 * D])
                    if outside and k < HEAD_SLOTS:
                        pe.wait_ge(S["head_filled"], 2 * 16 * HEAD_SLOTS)
                        g_u = head[k]
                    elif k < HEAD_SLOTS:
                        pe.wait_ge(filled[k], 16 * b + 16 * (fills_before(MOE0 + k) - 1))
                    else:
                        pe.wait_ge(filled[k], 16 * b + 16 * fills_before(MOE0 + k))
                    for gu in range(2):
                        for i in range(2):
                            m = pe.matmul(ps[gu][CAP * i:CAP * i + CAP, :], xeT[:, k, CAP * e2:CAP * e2 + CAP],
                                          g_u[gu][:, 512 * i:512 * i + 512],
                                          start=False, stop=(n_done == W_SLOTS - 1))
                    m.then_inc(S["freed"], 1)
                    between(k)

            def turn_h(b):
                pe.wait_ge(S["h_ready"], b + 1)
                for j in range(4):
                    m = pe.transpose(ps[2][:, j * P:(j + 1) * P], hh[:, j * P:(j + 1) * P], ident[:, :])
                m.then_inc(S["h_turned"], 1)

            def down(b):
                pe.wait_ge(S["hT_ready"], b + 1)
                for k in range(KD):
                    s = W_SLOTS + k // 2
                    if k % 2 == 0:
                        pe.wait_ge(filled[s], 16 * b + 16 * fills_before(MOE0 + s))
                    for i in range(2):
                        m = pe.matmul(ps[3][CAP * i:CAP * i + CAP, :], hTv[:, k % 4, CAP * (k // 4):CAP * (k // 4) + CAP],
                                      ring[:, s, D * (k % 2) + 512 * i:D * (k % 2) + 512 * i + 512],
                                      start=(k == 0), stop=(k == KD - 1))
                    if k % 2:
                        m.then_inc(S["freed"], 1)

            def pair(q, first):
                def between(k):
                    if k == 2:
                        pe.wait_ge(S["y_ready"], 2 * q)
                        pe.wait_ge(S["gt_ready"], q)
                        rounds(q - 1, 0)

                def gather_next(k):
                    if k == 3:
                        turn_gates(q)
                        gather(q + 1, (0,))

                pe.wait_ge(S["xe_ready"], q + 1)
                if first:
                    up(2 * q, 0, lambda k: None, True)
                    turn_h(2 * q)
                else:
                    up(2 * q, 0, between)
                    rounds(q - 1, 1)
                    turn_h(2 * q)
                    rounds(q - 1, 2)
                down(2 * q)
                up(2 * q + 1, 1, gather_next)
                gather(q + 1, (1,))
                if first:
                    pe.wait_ge(S["be2_loaded"], 16)
                    rounds(None, 0)
                pe.wait_ge(S["gt_ready"], q + 1)
                turn_h(2 * q + 1)
                if first:
                    rounds(None, 1)
                pe.wait_ge(S["y_ready"], 2 * q + 1)
                down(2 * q + 1)
                if first:
                    rounds(None, 2)

            pe.wait_ge(S["xnt_kept"], 6)
            pe.wait_ge(S["gt0_kept"], 1)
            gather(0)
            pe.wait_ge(S["tail_zeroed"], 1)
            pair(0, True)
            with pe.Fori(1, PAIRS) as q:
                pair(q, False)
            pe.wait_ge(S["y_ready"], NE)
            pe.wait_ge(S["xe_ready"], PAIRS + 1)
            for t in range(3):
                rounds(PAIRS - 1, t, LAST_BANKS[t])
            pe.wait_ge(S["nblk_ready"], 1)
            n = pe.value_load(nblk[0:1, 0:1], min_val=0, max_val=P)
            with pe.If(n > 0):
                pe.wait_ge(S["acc_done"], 3 * (PAIRS + 1))
                pe.wait_ge(S["tab_ready"], 1)
                pe.wait_ge(S["xe_ready"], PAIRS + 1)
                pe.transpose(ps[5][0:1, 0:P], tbc, ident[:, :]).then_inc(S["tab_turned"], 1)
                pe.wait_ge(S["tab_ready"], 2)
                with pe.Fori(0, n) as j:
                    pe.wait_ge(S["xe_ready"], j + (PAIRS + 1))
                    gather(j + (PAIRS + 1))
                    pe.wait_ge(S["xe_ready"], j + (PAIRS + 2))
                    up(j + NE, 0, lambda k: None)
                    turn_gates(j + PAIRS)
                    pe.wait_ge(S["gt_ready"], j + (PAIRS + 1))
                    turn_h(j + NE)
                    down(j + NE)
                    pe.wait_ge(S["y_ready"], j + (NE + 1))
                    for t in range(3):
                        rounds(j + PAIRS, t)


INPUTS = ["x_prompt", "x_sample", "state_lru_h", "cache_lru_conv", "cache_cf_conv", "cache_mem_k", "cache_mem_v",
          "mem_prompt", "g_mix", "w_in", "w_lru_conv", "b_lru_conv", "w_lru_a", "b_lru_a", "w_lru_x", "b_lru_x",
          "lru_lambda", "w_cf_conv", "b_cf_conv", "g_cf_ln", "b_cf_ln", "w_out", "g_xa", "g_mem", "w_q", "w_k", "w_v",
          "w_o", "g_moe", "w_router", "b_router", "w_e1", "b_e1", "w_e2", "b_e2", "g_final"]
OUTPUTS = [("y_prompt", (1, SEQ, D)), ("y_sample", (NB, 1, D)), ("lru_h_prompt", (1, 1, LRU)),
           ("lru_conv_prompt", (1, 1, LW - 1, LRU)), ("cf_conv_prompt", (1, 1, CW - 1, LRU)),
           ("mem_k", (1, 1, NMEM, H, HD)), ("mem_v", (1, 1, NMEM, H, HD)), ("lru_h_sample", (1, NB, LRU)),
           ("cache_lru", (1, NB, LW - 1, LRU)), ("cache_cf", (1, NB, CW - 1, LRU))]


def kernel(**inputs):
    import concourse.bacc as bacc
    from concourse.bass_utils import run_bass_kernel_spmd

    nc = bacc.Bacc("TRN2", target_bir_lowering=False, num_devices=1)
    arrays, a, outs = {}, {}, {}
    for name in INPUTS:
        x = np.ascontiguousarray(inputs[name])
        arrays["in_" + name] = x
        a[name] = nc.dram_tensor("in_" + name, x.shape, mybir.dt.from_np(x.dtype), kind="ExternalInput").ap()
    for name, shape in OUTPUTS:
        outs[name] = nc.dram_tensor("out_" + name, shape, F32, kind="ExternalOutput").ap()
    build(nc, a, outs)
    r = run_bass_kernel_spmd(nc, [arrays], core_ids=[0])
    return tuple(r.results[0]["out_" + name] for name, _ in OUTPUTS)
```
